# Optimizing a Trainium2 kernel written in Bass

```python
import math
import jax, jax.numpy as jnp
from jax import lax
import numpy as np
import jax
import jax.numpy as jnp

D_MODEL = 1024
BATCH = 1
SEQ = 256
DEPTH = 2

N_A_LAYERS = DEPTH // 2
N_B_LAYERS = DEPTH - N_A_LAYERS
D_FF = 2816
RWKV_HEAD = 64
RWKV_HEADS = D_MODEL // RWKV_HEAD
LORA_DECAY = 64
LORA_AAA = 64
LORA_GATE = 160
RWKV_LN_EPS = 64e-5
N_SHIFT_MIX = 6
DIFF_HEAD = 64
DIFF_HEADS = D_MODEL // (2 * DIFF_HEAD)
DIFF_V_HEAD = 2 * DIFF_HEAD
Q_BLOCK = 128
NORM_EPS = 1e-6
SUBLN_EPS = 1e-5


def rms_norm(x, g, eps=NORM_EPS):
    xf = x.astype(jnp.float32)
    y = xf * lax.rsqrt(jnp.mean(xf * xf, axis=-1, keepdims=True) + eps)
    return (y * g.astype(jnp.float32)).astype(x.dtype)

def swiglu(h, w_in, w_out):
    gate, up = jnp.split(h @ w_in, 2, axis=-1)
    return (jax.nn.silu(gate) * up) @ w_out

def lambda_init(layer_idx):
    return 0.8 - 0.6 * math.exp(-0.3 * layer_idx)

def alibi_slopes(n_heads):
    return 2.0 ** (-8.0 * jnp.arange(1, n_heads + 1, dtype=jnp.float32) / n_heads)

def wkv7_scan(r, decay, k, v, a, b):
    B, T, H, N = r.shape

    def step(S, inp):
        r_t, w_t, k_t, v_t, a_t, b_t = inp
        sa = jnp.einsum('bhij,bhj->bhi', S, a_t)
        S = S * w_t[:, :, None, :] + sa[..., None] * b_t[:, :, None, :] + v_t[..., None] * k_t[:, :, None, :]
        return S, jnp.einsum('bhij,bhj->bhi', S, r_t)

    xs = [jnp.moveaxis(t.astype(jnp.float32), 1, 0) for t in (r, decay, k, v, a, b)]
    S0 = jnp.zeros((B, H, N, N), jnp.float32)
    _, y = lax.scan(step, S0, xs)
    return jnp.moveaxis(y, 0, 1)

def rwkv7_time_mix(h, mu, w_rkv, w0, w1, w2, a0, a1, a2, g1, g2, k_k, k_a, r_k, ln_g, ln_b, w_o):
    B, T, C = h.shape
    H, N = RWKV_HEADS, RWKV_HEAD
    h_prev = jnp.pad(h, ((0, 0), (1, 0), (0, 0)))[:, :-1]
    dx = h_prev - h
    r, k, v = jnp.einsum('sbtc,scd->sbtd', h[None] + dx[None] * mu[:3, None, None, :], w_rkv)
    xw = h + dx * mu[3]
    xa = h + dx * mu[4]
    xg = h + dx * mu[5]
    w_log = -jax.nn.softplus(-(w0 + jnp.tanh(xw @ w1) @ w2)) - 0.5
    decay = jnp.exp(-jnp.exp(w_log.astype(jnp.float32)))
    a = jax.nn.sigmoid(a0 + (xa @ a1) @ a2)
    g = jax.nn.sigmoid(xg @ g1) @ g2
    kk = (k * k_k).reshape(B, T, H, N).astype(jnp.float32)
    kk = kk * lax.rsqrt(jnp.maximum(jnp.sum(kk * kk, axis=-1, keepdims=True), 1e-24))
    k = k * (1 + (a - 1) * k_a)
    heads = lambda t: t.reshape(B, T, H, N)
    a_h = heads(a).astype(jnp.float32)
    y = wkv7_scan(heads(r), heads(decay), heads(k), heads(v), -kk, kk * a_h)
    mean = jnp.mean(y, axis=-1, keepdims=True)
    var = jnp.mean(jnp.square(y - mean), axis=-1, keepdims=True)
    y = ((y - mean) * lax.rsqrt(var + RWKV_LN_EPS)).reshape(B, T, C) * ln_g + ln_b
    bonus = jnp.sum(heads(r).astype(jnp.float32) * heads(k).astype(jnp.float32) * r_k, axis=-1, keepdims=True)
    y = y + (bonus * heads(v).astype(jnp.float32)).reshape(B, T, C)
    return (y.astype(h.dtype) * g) @ w_o

def shared_kv(x, kv_norm, w_kv, k_norm):
    B, T, _ = x.shape
    kv = rms_norm(x, kv_norm) @ w_kv
    k = rms_norm(kv[..., :D_MODEL].reshape(B, T, DIFF_HEADS, 2, DIFF_HEAD), k_norm).transpose(0, 2, 3, 1, 4)
    v = kv[..., D_MODEL:].reshape(B, T, DIFF_HEADS, DIFF_V_HEAD).transpose(0, 2, 1, 3)
    return k, v

def diff_attention(h, k_sh, v_sh, w_q, q_norm, lam, subln, w_o, lam_init):
    B, T, _ = h.shape
    H, d = DIFF_HEADS, DIFF_HEAD
    n_blk = T // Q_BLOCK
    q = rms_norm((h @ w_q).reshape(B, T, H, 2, d), q_norm)
    q = q.reshape(B, n_blk, Q_BLOCK, H, 2, d).transpose(1, 0, 3, 4, 2, 5)
    lamf = lam.astype(jnp.float32)
    lam_full = jnp.exp(jnp.sum(lamf[0] * lamf[1])) - jnp.exp(jnp.sum(lamf[2] * lamf[3])) + lam_init
    slopes = alibi_slopes(H)
    k_pos = jnp.arange(T, dtype=jnp.int32)
    scale = d ** -0.5

    def block(args):
        qb, start = args
        s = jnp.einsum('bhcqd,bhckd->bhcqk', qb, k_sh).astype(jnp.float32) * scale
        dist = (start + jnp.arange(Q_BLOCK, dtype=jnp.int32))[:, None] - k_pos[None, :]
        bias = -slopes[:, None, None] * dist.astype(jnp.float32)
        s = jnp.where(dist >= 0, s + bias[None, :, None], -jnp.inf)
        p = jax.nn.softmax(s, axis=-1)
        attn = p[:, :, 0] - lam_full * p[:, :, 1]
        return jnp.einsum('bhqk,bhkd->bhqd', attn.astype(v_sh.dtype), v_sh)

    starts = jnp.arange(n_blk, dtype=jnp.int32) * Q_BLOCK
    o = lax.map(block, (q, starts))
    o = rms_norm(o, subln, SUBLN_EPS) * (1.0 - lam_init)
    o = o.transpose(1, 0, 3, 2, 4).reshape(B, T, H * DIFF_V_HEAD)
    return o @ w_o

def first_inputs(seed: int = 0) -> dict:
    key = jax.random.key(seed)
    ks = jax.random.split(key, 29)
    C, F = D_MODEL, D_FF
    nA, nB = N_A_LAYERS, N_B_LAYERS
    nrm = lambda k, shape, s: jax.random.normal(k, shape, jnp.float32) * s
    gain = lambda k, shape: 1.0 + nrm(k, shape, 0.02)
    return {
        "x": nrm(ks[0], (BATCH, SEQ, C), 1.0),
        "ffn_norm": gain(ks[1], (DEPTH, 2, C)),
        "ffn_w_in": nrm(ks[2], (DEPTH, 2, C, 2 * F), C ** -0.5),
        "ffn_w_out": nrm(ks[3], (DEPTH, 2, F, C), F ** -0.5),
        "mix_norm": gain(ks[4], (DEPTH, C)),
        "rwkv_mu": jax.random.uniform(ks[5], (nA, N_SHIFT_MIX, C), jnp.float32),
        "rwkv_w_rkv": nrm(ks[6], (nA, 3, C, C), C ** -0.5),
        "rwkv_w0": jax.random.uniform(ks[7], (nA, C), jnp.float32, -6.0, -1.0),
        "rwkv_w1": nrm(ks[8], (nA, C, LORA_DECAY), C ** -0.5),
        "rwkv_w2": nrm(ks[9], (nA, LORA_DECAY, C), 0.5 * LORA_DECAY ** -0.5),
        "rwkv_a0": nrm(ks[10], (nA, C), 0.1),
        "rwkv_a1": nrm(ks[11], (nA, C, LORA_AAA), C ** -0.5),
        "rwkv_a2": nrm(ks[12], (nA, LORA_AAA, C), 0.5 * LORA_AAA ** -0.5),
        "rwkv_g1": nrm(ks[13], (nA, C, LORA_GATE), C ** -0.5),
        "rwkv_g2": nrm(ks[14], (nA, LORA_GATE, C), LORA_GATE ** -0.5),
        "rwkv_k_k": 0.85 + nrm(ks[15], (nA, C), 0.02),
        "rwkv_k_a": gain(ks[16], (nA, C)),
        "rwkv_r_k": nrm(ks[17], (nA, RWKV_HEADS, RWKV_HEAD), 0.1),
        "rwkv_ln_g": gain(ks[18], (nA, C)),
        "rwkv_ln_b": nrm(ks[19], (nA, C), 0.02),
        "rwkv_w_o": nrm(ks[20], (nA, C, C), 0.5 * C ** -0.5),
        "kv_norm": gain(ks[21], (C,)),
        "w_kv": nrm(ks[22], (C, 2 * C), C ** -0.5),
        "k_norm": gain(ks[23], (DIFF_HEAD,)),
        "diff_w_q": nrm(ks[24], (nB, C, C), C ** -0.5),
        "diff_q_norm": gain(ks[25], (nB, DIFF_HEAD)),
        "diff_lambda": nrm(ks[26], (nB, 4, DIFF_HEAD), 0.1),
        "diff_subln": gain(ks[27], (nB, DIFF_V_HEAD)),
        "diff_w_o": nrm(ks[28], (nB, C, C), 0.5 * C ** -0.5),
    }

def first_block(x, ffn_norm, ffn_w_in, ffn_w_out, mix_norm, rwkv_mu, rwkv_w_rkv, rwkv_w0, rwkv_w1, rwkv_w2,
              rwkv_a0, rwkv_a1, rwkv_a2, rwkv_g1, rwkv_g2, rwkv_k_k, rwkv_k_a, rwkv_r_k, rwkv_ln_g, rwkv_ln_b,
              rwkv_w_o, kv_norm, w_kv, k_norm, diff_w_q, diff_q_norm, diff_lambda, diff_subln, diff_w_o):
    k_sh = None
    v_sh = None
    for l in range(DEPTH):
        x = x + 0.5 * swiglu(rms_norm(x, ffn_norm[l, 0]), ffn_w_in[l, 0], ffn_w_out[l, 0])
        h = rms_norm(x, mix_norm[l])
        if l < N_A_LAYERS:
            i = l
            x = x + rwkv7_time_mix(h, rwkv_mu[i], rwkv_w_rkv[i], rwkv_w0[i], rwkv_w1[i], rwkv_w2[i],
                                   rwkv_a0[i], rwkv_a1[i], rwkv_a2[i], rwkv_g1[i], rwkv_g2[i],
                                   rwkv_k_k[i], rwkv_k_a[i], rwkv_r_k[i], rwkv_ln_g[i], rwkv_ln_b[i], rwkv_w_o[i])
        else:
            j = l - N_A_LAYERS
            x = x + diff_attention(h, k_sh, v_sh, diff_w_q[j], diff_q_norm[j], diff_lambda[j],
                                   diff_subln[j], diff_w_o[j], lambda_init(l))
        x = x + 0.5 * swiglu(rms_norm(x, ffn_norm[l, 1]), ffn_w_in[l, 1], ffn_w_out[l, 1])
        if l == N_A_LAYERS - 1:
            k_sh, v_sh = shared_kv(x, kv_norm, w_kv, k_norm)
    return x


DEPTH_2 = 1

CHUNK = 64
HEAD_DIM = 64
RMS_EPS = 1e-6
NEG_INF = -1e30

SWA_Q_HEADS = 8
SWA_KV_HEADS = 2
SWA_GROUP = SWA_Q_HEADS // SWA_KV_HEADS
SWA_WINDOW = 128
SWA_WINDOW_CHUNKS = SWA_WINDOW // CHUNK
SWA_KEYS = (SWA_WINDOW_CHUNKS + 1) * CHUNK
SWA_WIDTH = SWA_Q_HEADS * HEAD_DIM
SWA_KV_WIDTH = SWA_KV_HEADS * HEAD_DIM

SB_HEADS = 8
SB_WIDTH = SB_HEADS * HEAD_DIM
SB_BLOCK = 128

N_BRANCHES = 2
SPLIT_POINTS = (
    SWA_WIDTH,
    SWA_WIDTH + SWA_KV_WIDTH,
    SWA_WIDTH + 2 * SWA_KV_WIDTH,
    SWA_WIDTH + 2 * SWA_KV_WIDTH + SB_WIDTH,
    SWA_WIDTH + 2 * SWA_KV_WIDTH + 2 * SB_WIDTH,
    SWA_WIDTH + 2 * SWA_KV_WIDTH + 3 * SB_WIDTH,
)
IN_WIDTH = SWA_WIDTH + 2 * SWA_KV_WIDTH + 3 * SB_WIDTH + N_BRANCHES * D_MODEL

PEER_HEADS = 8
PEER_N_KEYS = 128
PEER_N_EXPERTS = PEER_N_KEYS * PEER_N_KEYS
PEER_QUERY_DIM = 256
PEER_HALF = PEER_QUERY_DIM // 2
PEER_TOPK = 16
PEER_BLOCK = 128


def rms_norm_2(x, gain):
    xf = x.astype(jnp.float32)
    y = xf * lax.rsqrt(jnp.mean(xf * xf, axis=-1, keepdims=True) + RMS_EPS)
    return (y * gain.astype(jnp.float32)).astype(x.dtype)

def alibi_slopes_2(n_heads):
    return jnp.exp2(-8.0 * jnp.arange(1, n_heads + 1, dtype=jnp.float32) / n_heads)

def sliding_window_sink_attention(q, k, v, q_gain, k_gain, sinks):
    b, s = q.shape[0], q.shape[1]
    nc = s // CHUNK
    pad = SWA_WINDOW_CHUNKS * CHUNK
    q = rms_norm_2(q, q_gain)
    k = rms_norm_2(k, k_gain)
    kp = jnp.pad(k, ((0, 0), (pad, 0), (0, 0), (0, 0))).reshape(
        b, nc + SWA_WINDOW_CHUNKS, CHUNK, SWA_KV_HEADS, HEAD_DIM)
    vp = jnp.pad(v, ((0, 0), (pad, 0), (0, 0), (0, 0))).reshape(
        b, nc + SWA_WINDOW_CHUNKS, CHUNK, SWA_KV_HEADS, HEAD_DIM)
    kw = jnp.concatenate([kp[:, i:i + nc] for i in range(SWA_WINDOW_CHUNKS + 1)], axis=2)
    vw = jnp.concatenate([vp[:, i:i + nc] for i in range(SWA_WINDOW_CHUNKS + 1)], axis=2)
    qc = q.reshape(b, nc, CHUNK, SWA_KV_HEADS, SWA_GROUP, HEAD_DIM)
    logits = jnp.einsum('bcqhgd,bckhd->bhgcqk', qc, kw).astype(jnp.float32) * (HEAD_DIM ** -0.5)
    dist = jnp.abs(jnp.arange(CHUNK)[:, None] + pad - jnp.arange(SWA_KEYS)[None, :]).astype(jnp.float32)
    slopes = alibi_slopes_2(SWA_Q_HEADS).reshape(SWA_KV_HEADS, SWA_GROUP)
    logits = logits - slopes[None, :, :, None, None, None] * dist
    key_pos = jnp.arange(nc)[:, None] * CHUNK - pad + jnp.arange(SWA_KEYS)[None, :]
    logits = jnp.where((key_pos >= 0)[:, None, :], logits, NEG_INF)
    sink = jnp.broadcast_to(
        sinks.astype(jnp.float32).reshape(1, SWA_KV_HEADS, SWA_GROUP, 1, 1, 1),
        logits.shape[:-1] + (1,))
    probs = jax.nn.softmax(jnp.concatenate([logits, sink], axis=-1), axis=-1)[..., :-1]
    out = jnp.einsum('bhgcqk,bckhd->bcqhgd', probs.astype(v.dtype), vw)
    return out.reshape(b, s, SWA_WIDTH)

def stick_breaking_attention(q, k, v):
    b, s, h, dh = q.shape
    nb = s // SB_BLOCK
    qb = q.reshape(b, nb, SB_BLOCK, h, dh).transpose(1, 0, 2, 3, 4)
    key_pos = jnp.arange(s)

    def block(args):
        q_blk, blk_idx = args
        z = jnp.einsum('bqhd,bkhd->bhqk', q_blk, k).astype(jnp.float32) * (dh ** -0.5)
        q_pos = blk_idx * SB_BLOCK + jnp.arange(SB_BLOCK)
        before = key_pos[None, :] < q_pos[:, None]
        log_beta = jax.nn.log_sigmoid(z)
        log_keep = jnp.where(before, jax.nn.log_sigmoid(-z), 0.0)
        suffix = lax.cumsum(log_keep, axis=3, reverse=True) - log_keep
        weights = jnp.where(before, jnp.exp(log_beta + suffix), 0.0)
        return jnp.einsum('bhqk,bkhd->bqhd', weights.astype(v.dtype), v)

    out = lax.map(block, (qb, jnp.arange(nb)))
    return out.transpose(1, 0, 2, 3, 4).reshape(b, s, h * dh)

def peer_ffn(x, w_q, sub_keys, u, v):
    b, s, d = x.shape
    tokens = x.reshape(-1, PEER_BLOCK, d)

    def block(xb):
        q = (xb @ w_q).reshape(PEER_BLOCK, PEER_HEADS, 2, PEER_HALF)
        scores = jnp.einsum('thpd,hpkd->thpk', q, sub_keys).astype(jnp.float32)
        top_s, top_i = lax.top_k(scores, PEER_TOPK)
        cand_s = (top_s[:, :, 0, :, None] + top_s[:, :, 1, None, :]).reshape(
            PEER_BLOCK, PEER_HEADS, PEER_TOPK * PEER_TOPK)
        cand_i = (top_i[:, :, 0, :, None] * PEER_N_KEYS + top_i[:, :, 1, None, :]).reshape(
            PEER_BLOCK, PEER_HEADS, PEER_TOPK * PEER_TOPK)
        best_s, best_pos = lax.top_k(cand_s, PEER_TOPK)
        expert = jnp.take_along_axis(cand_i, best_pos, axis=-1)
        gate = jax.nn.softmax(best_s, axis=-1)
        act = jax.nn.gelu(jnp.einsum('thkd,td->thk', u[expert], xb).astype(jnp.float32),
                          approximate=False)
        return jnp.einsum('thk,thkd->td', (gate * act).astype(v.dtype), v[expert])

    return lax.map(block, tokens).reshape(b, s, d)

def second_inputs(seed: int = 0) -> dict:
    key = jax.random.key(seed)
    ks = jax.random.split(key, 16)

    def normal(k, shape, scale):
        return jax.random.normal(k, shape, jnp.float32) * scale

    return {
        'x': normal(ks[0], (BATCH, SEQ, D_MODEL), 1.0),
        'mix_norm_gain': 1.0 + normal(ks[1], (DEPTH_2, D_MODEL), 0.02),
        'w_in': normal(ks[2], (DEPTH_2, D_MODEL, IN_WIDTH), D_MODEL ** -0.5),
        'gate_bias': normal(ks[3], (DEPTH_2, N_BRANCHES * D_MODEL), 0.1),
        'swa_q_gain': 1.0 + normal(ks[4], (DEPTH_2, HEAD_DIM), 0.02),
        'swa_k_gain': 1.0 + normal(ks[5], (DEPTH_2, HEAD_DIM), 0.02),
        'swa_sinks': normal(ks[6], (DEPTH_2, SWA_Q_HEADS), 0.5),
        'w_up_swa': normal(ks[7], (DEPTH_2, SWA_WIDTH, D_MODEL), SWA_WIDTH ** -0.5),
        'w_up_sb': normal(ks[8], (DEPTH_2, SB_WIDTH, D_MODEL), SB_WIDTH ** -0.5),
        'w_out': normal(ks[9], (DEPTH_2, D_MODEL, D_MODEL), D_MODEL ** -0.5),
        'ffn_norm_gain': 1.0 + normal(ks[10], (DEPTH_2, D_MODEL), 0.02),
        'peer_w_q': normal(ks[11], (DEPTH_2, D_MODEL, PEER_HEADS * PEER_QUERY_DIM), D_MODEL ** -0.5),
        'peer_sub_keys': normal(ks[12], (DEPTH_2, PEER_HEADS, 2, PEER_N_KEYS, PEER_HALF), PEER_HALF ** -0.5),
        'peer_u': normal(ks[13], (DEPTH_2, PEER_N_EXPERTS, D_MODEL), D_MODEL ** -0.5),
        'peer_v': normal(ks[14], (DEPTH_2, PEER_N_EXPERTS, D_MODEL), PEER_HEADS ** -0.5),
    }

def second_block(x, mix_norm_gain, w_in, gate_bias, swa_q_gain, swa_k_gain, swa_sinks,
              w_up_swa, w_up_sb, w_out, ffn_norm_gain, peer_w_q, peer_sub_keys, peer_u, peer_v):
    b, s, d = x.shape
    for layer in range(DEPTH_2):
        h = rms_norm_2(x, mix_norm_gain[layer])
        proj = h @ w_in[layer]
        q_a, k_a, v_a, q_b, k_b, v_b, gate_logits = jnp.split(proj, SPLIT_POINTS, axis=-1)
        y_a = sliding_window_sink_attention(
            q_a.reshape(b, s, SWA_Q_HEADS, HEAD_DIM),
            k_a.reshape(b, s, SWA_KV_HEADS, HEAD_DIM),
            v_a.reshape(b, s, SWA_KV_HEADS, HEAD_DIM),
            swa_q_gain[layer], swa_k_gain[layer], swa_sinks[layer])
        y_b = stick_breaking_attention(
            q_b.reshape(b, s, SB_HEADS, HEAD_DIM),
            k_b.reshape(b, s, SB_HEADS, HEAD_DIM),
            v_b.reshape(b, s, SB_HEADS, HEAD_DIM))
        gates = jax.nn.sigmoid(gate_logits + gate_bias[layer]).reshape(b, s, N_BRANCHES, d)
        merged = gates[:, :, 0] * (y_a @ w_up_swa[layer]) + gates[:, :, 1] * (y_b @ w_up_sb[layer])
        x = x + merged @ w_out[layer]
        h = rms_norm_2(x, ffn_norm_gain[layer])
        x = x + peer_ffn(h, peer_w_q[layer], peer_sub_keys[layer], peer_u[layer], peer_v[layer])
    return x


def setup_inputs(seed=0):
    out = dict(first_inputs(seed))
    for name, value in second_inputs(seed + 1).items():
        if name != "x":
            out[name + "_2"] = value
    return out


def reference(
    x, ffn_norm, ffn_w_in, ffn_w_out, mix_norm, rwkv_mu, rwkv_w_rkv, rwkv_w0, rwkv_w1, rwkv_w2,
    rwkv_a0, rwkv_a1, rwkv_a2, rwkv_g1, rwkv_g2, rwkv_k_k, rwkv_k_a, rwkv_r_k, rwkv_ln_g,
    rwkv_ln_b, rwkv_w_o, kv_norm, w_kv, k_norm, diff_w_q, diff_q_norm, diff_lambda, diff_subln,
    diff_w_o, mix_norm_gain_2, w_in_2, gate_bias_2, swa_q_gain_2, swa_k_gain_2, swa_sinks_2,
    w_up_swa_2, w_up_sb_2, w_out_2, ffn_norm_gain_2, peer_w_q_2, peer_sub_keys_2, peer_u_2,
    peer_v_2,
):
    x = first_block(
        x, ffn_norm, ffn_w_in, ffn_w_out, mix_norm, rwkv_mu, rwkv_w_rkv, rwkv_w0, rwkv_w1,
        rwkv_w2, rwkv_a0, rwkv_a1, rwkv_a2, rwkv_g1, rwkv_g2, rwkv_k_k, rwkv_k_a, rwkv_r_k,
        rwkv_ln_g, rwkv_ln_b, rwkv_w_o, kv_norm, w_kv, k_norm, diff_w_q, diff_q_norm,
        diff_lambda, diff_subln, diff_w_o,
    )
    return second_block(
        x, mix_norm_gain_2, w_in_2, gate_bias_2, swa_q_gain_2, swa_k_gain_2, swa_sinks_2,
        w_up_swa_2, w_up_sb_2, w_out_2, ffn_norm_gain_2, peer_w_q_2, peer_sub_keys_2, peer_u_2,
        peer_v_2,
    )


_drawn_inputs = setup_inputs


def setup_inputs(seed=0):
    import zlib

    import numpy as np

    out = dict(_drawn_inputs(seed))
    spreads = {}
    factors = {'mix_norm': 2.719,
     'rwkv_w1': 4.083,
     'rwkv_w2': 4.118,
     'rwkv_a0': 2.799,
     'rwkv_k_k': 5.094,
     'rwkv_k_a': 4.238,
     'rwkv_ln_g': 4.64,
     'rwkv_ln_b': 3.757,
     'kv_norm': 3.61,
     'k_norm': 4.727,
     'diff_q_norm': 4.956,
     'diff_subln': 5.141,
     'mix_norm_gain_2': 3.862,
     'gate_bias_2': 2.985,
     'swa_q_gain_2': 8.0,
     'swa_k_gain_2': 8.0,
     'swa_sinks_2': 6.143,
     'ffn_norm_gain_2': 15.98}
    for name, (base, spread) in spreads.items():
        noise = np.random.default_rng([zlib.crc32(name.encode()), seed]).standard_normal(out[name].shape)
        drawn = base * np.exp(spread * noise) if base else spread * noise
        out[name] = jnp.asarray(drawn.astype(out[name].dtype))
    for name, factor in factors.items():
        out[name] = (out[name] * factor).astype(out[name].dtype)
    return out
```

```python
import math

import numpy as np

import concourse.bass as bass
import concourse.mybir as mybir
from concourse.alu_op_type import AluOpType as ALU

F32 = mybir.dt.float32
U32 = mybir.dt.uint32
ACT = mybir.ActivationFunctionType
AX = mybir.AxisListType

P = 128
T = 256
TB = T // P
D = 1024
KC = D // P
FF = 2816
FC = FF // P
TILE = 2048
RING = 5
BANK = 512
HEADS = 16
HD = 64
DH = 8
KEYS = 128
TOP = 16
PH = 8
NEG = -1e30
DECAY = math.exp(-0.5)
LEVELS = 7

COLS = [("ffn_norm", 4 * KC), ("mix_norm", 2 * KC), ("mu", 6 * KC), ("w0", KC), ("a0", KC), ("k_k", KC),
        ("k_a", KC), ("r_k", KC), ("kv_norm", KC), ("mix_gain_2", KC), ("ffn_gain_2", KC),
        ("subln", 1), ("k_norm", 1), ("q_norm", 1), ("swa_q", 1), ("swa_k", 1)]
CONSTS = [("ident", P), ("iota", P), ("strict", P), ("upto", P), ("pairT", P), ("level", LEVELS * P),
          ("headsum", P), ("headsel", KC * HEADS), ("scan_keep", P), ("causal_dist", 3 * P),
          ("window_dist", 3 * P), ("before", 3 * P), ("before_neg", 3 * P)]


def offsets(table):
    out, at = {}, 0
    for name, n in table:
        out[name] = (at, at + n)
        at += n
    return out, at


class Lane:

    def __init__(self, engine, semaphore, linked):
        self.engine, self.semaphore, self.count, self.seen = engine, semaphore, 0, {}
        self.linked = linked

    def wait(self, *marks):
        for m in marks:
            if m is None:
                continue
            if isinstance(m, list):
                self.wait(*m)
                continue
            sem, value = m
            if self.seen.get(sem.name, 0) < value:
                self.engine.wait_ge(sem, value)
                self.seen[sem.name] = value

    def mark(self, instruction):
        instruction.then_inc(self.semaphore, 1)
        self.count += 1
        done = (self.semaphore, self.count)
        if self.linked:
            self.wait(done)
        return done


class Ring:

    def __init__(self, lane, buffer, semaphores, tiles):
        self.lane, self.buffer, self.sems, self.tiles = lane, buffer, semaphores, tiles
        self.loaded, self.taken, self.oldest, self.read = [], 0, 0, {}
        self.count = [0] * len(semaphores)
        for _ in semaphores:
            self.load()

    def load(self):
        n = len(self.loaded)
        slot = n % len(self.sems)
        for parts, at, src in self.tiles[n]:
            width = src.shape[1]
            self.lane.engine.dma_start(self.buffer[0:parts, slot, at:at + width], src).then_inc(self.sems[slot], 16)
            self.count[slot] += 16
        self.loaded.append((self.sems[slot], self.count[slot]))

    def take(self):
        n = self.taken
        self.taken += 1
        return n, self.loaded[n], self.buffer[:, n % len(self.sems), :]

    def release(self, n, mark):
        self.read[n] = mark
        while self.oldest in self.read:
            if len(self.loaded) < len(self.tiles):
                self.lane.wait(self.read[self.oldest])
                self.load()
            self.oldest += 1


class Banks:

    def __init__(self, psum):
        self.psum, self.freed = psum, [None] * 8
        self.use(range(8))

    def use(self, banks):
        self.order, self.at = list(banks), 0

    def take(self, lane):
        b = self.order[self.at % len(self.order)]
        self.at += 1
        lane.wait(self.freed[b])
        return b, self.psum[:, b, :]

    def free(self, b, mark):
        self.freed[b] = mark


class Core:
    pass


def tiles_of(ap):
    return [[(ap.shape[1], 0, ap[i])] for i in range(ap.shape[0])]


def block(nc, A, out, stack):
    sb = lambda name, shape: stack.enter_context(nc.sbuf_tensor(name, shape, F32))
    sem = lambda name: stack.enter_context(nc.semaphore(name))
    tensor, vector, scalar, pool, sync = nc.tensor, nc.vector, nc.scalar, nc.gpsimd, nc.sync

    x = sb("x", [P, TB, D])
    hT = sb("hT", [P, KC, T])
    ring = sb("ring", [P, RING, TILE])
    arena = sb("arena", [P, 17, TILE])
    col_at, n_cols = offsets(COLS)
    cols = sb("cols", [P, n_cols])
    const_at, n_consts = offsets(CONSTS)
    basic = sb("basic", [P, 2 * P])
    masks = sb("masks", [P, 11 * P])
    small = sb("small", [P, 256])
    minus_half = sb("minus_half", [P, 16])
    psum = stack.enter_context(nc.psum_tensor("psum", [P, 8, BANK], F32))

    PE, V, S, G, SP = (Lane(e, sem(n), linked) for e, n, linked in (
        (tensor, "tensor_done", False), (vector, "vector_done", True), (scalar, "scalar_done", True),
        (pool, "pool_done", True), (sync, "sync_done", False)))

    def col(name, n=0, k=KC):
        a = col_at[name][0] + n * k
        return cols[:, a:a + k]

    def unit(i):
        return arena[:, i, :]

    def fm(buffer):
        return buffer.rearrange("p (c t) -> p c t", t=T)

    def tm(buffer):
        return buffer.rearrange("p (b c) -> p b c", b=TB)

    def spread(ap, n):
        return ap.unsqueeze(2).to_broadcast([P, ap.shape[1], n])

    def across(ap, n):
        return ap.unsqueeze(1).to_broadcast([P, n, ap.shape[1]])

    def ffn_tiles(l, j):
        out = []
        for f in range(FC):
            out.append([(P, 0, A["ffn_in"][l, j, f])])
            if f % 2 == 0:
                out.append([(P, 0, A["ffn_out"][l, j, f // 2])])
        return out

    tiles = ffn_tiles(0, 0)
    tiles += [[(P, 0, A["lora_in"])], [(P, 0, A["g1"])], [(64, 0, A["lora_out"])]]
    tiles += tiles_of(A["w_r"]) + tiles_of(A["w_k"]) + tiles_of(A["w_v"])
    tiles += [[(P, 0, A["g2"][0:P, :]), (32, D, A["g2"][P:160, :])]]
    tiles += tiles_of(A["w_o"])
    tiles += ffn_tiles(0, 1) + tiles_of(A["w_kv"]) + ffn_tiles(1, 0)
    tiles += tiles_of(A["diff_w_q"]) + tiles_of(A["diff_w_o"]) + ffn_tiles(1, 1)
    tiles += tiles_of(A["in_q_a"]) + tiles_of(A["in_kv_a"]) + tiles_of(A["in_qk_b"]) + tiles_of(A["in_v_b"])
    tiles += tiles_of(A["in_gates"]) + tiles_of(A["up_swa"]) + tiles_of(A["up_sb"]) + tiles_of(A["w_out"])
    tiles += tiles_of(A["peer_q"]) + tiles_of(A["sub_keys"])
    for pair in range(KEYS // 2):
        tiles += [[(P, 0, A["peer_u"][pair])], [(P, 0, A["peer_v"][pair])]]

    def load(dst, src, *after):
        S.wait(*after)
        s = sem(f"load_{dst.tensor.name}_{len(loads)}")
        scalar.dma_start(dst, src).then_inc(s, 16)
        loads.append(s)
        return (s, 16)

    def row(name, dst, *after):
        a = A[name]
        return load(dst, bass.AP(a.tensor, a.offset, [[0, P], [1, a.shape[1]]]), *after)

    def consts(name, dst, *after):
        a, b = const_at[name]
        return load(dst, A["consts"][:, a:b], *after)

    loads = []
    x_loaded = [load(x[:, tb, :], A["x"][tb]) for tb in range(TB)]
    cols_loaded = load(cols[:, :], A["cols"])
    ident, iota = basic[:, 0:P], basic[:, P:2 * P]
    basic_loaded = load(basic[:, :], A["consts"][:, 0:2 * P])
    W = Ring(SP, ring, [sem(f"ring_{i}") for i in range(RING)], tiles)
    banks = Banks(psum)
    half_ready = V.mark(vector.memset(minus_half[:, :], -0.5))
    G.wait(half_ready)
    S.wait(basic_loaded, cols_loaded)
    PE.wait(basic_loaded)
    V.wait(cols_loaded, basic_loaded)

    def rsqrt(ap, n, ready):
        G.wait(ready, half_ready)
        return G.mark(pool.tensor_tensor(ap, ap, minus_half[:, 0:n], ALU.pow))

    def transposed(src, tb, dst, ready, gain=None, scale=None, n=KC, per=None):
        last = None
        for c0 in range(0, n, 4):
            m = min(4, n - c0)
            PE.wait(ready)
            b, ps = banks.take(PE)
            for c in range(m):
                ins = tensor.transpose(ps[:, c * P:(c + 1) * P], src[:, (c0 + c) * P:(c0 + c + 1) * P], ident)
            turned = PE.mark(ins)
            dstv = dst[:, c0:c0 + m, tb * P:(tb + 1) * P]
            psv = ps[:, 0:m * P].rearrange("p (c t) -> p c t", t=P)
            if gain is not None:
                V.wait(turned)
                last = V.mark(vector.tensor_tensor(dstv, psv, spread(gain[:, c0:c0 + m], P), ALU.mult))
            elif scale is not None:
                V.wait(turned)
                last = V.mark(vector.tensor_scalar(dstv, psv, scale[0], scale[1], ALU.mult, ALU.mult))
            else:
                S.wait(turned)
                last = S.mark(scalar.activation(dstv, psv, ACT.Copy))
            banks.free(b, last)
        return last

    def norm(gain, ready, free=None, eps=1e-6, xn=None):
        xn = tm(unit(0)) if xn is None else xn
        done = []
        for tb in range(TB):
            ss = small[:, tb:tb + 1]
            V.wait(ready[tb], free)
            m = V.mark(vector.scalar_tensor_tensor(out=xn[:, tb, :], in0=x[:, tb, :], scalar=1.0, in1=x[:, tb, :],
                                                   op0=ALU.mult, op1=ALU.mult, accum_out=ss))
            V.wait(m)
            m = V.mark(vector.tensor_scalar(ss, ss, 1.0 / D, eps, ALU.mult, ALU.add))
            m = rsqrt(ss, 1, m)
            V.wait(m)
            m = V.mark(vector.tensor_scalar(xn[:, tb, :], x[:, tb, :], ss, None, ALU.mult))
            done.append(transposed(xn[:, tb, :], tb, hT, m, gain=gain))
        return done

    def add_to_x(tb, n0, ps, factor, ready):
        V.wait(ready)
        xs = x[:, tb, n0:n0 + BANK]
        return V.mark(vector.scalar_tensor_tensor(out=xs, in0=ps, scalar=factor, in1=xs, op0=ALU.mult, op1=ALU.add))

    def ffn(l, j, ready):
        h_ready = norm(col("ffn_norm", 2 * l + j), ready)
        PE.wait(h_ready)
        banks.use(range(4, 8))
        PE.wait(banks.freed[0:4])
        act = unit(16).rearrange("p (b n) -> p b n", n=T)
        hidden, w_out, down_done = {}, {}, {}

        def gate_up(f):
            n, loaded, w = W.take()
            w = w.rearrange("p (k n) -> p k n", k=KC)
            if f % 2 == 0:
                w_out[f // 2] = W.take()
            b, ps = banks.take(PE)
            PE.wait(loaded)
            for part in range(2):
                for k in range(KC):
                    ins = tensor.matmul(ps[:, part * T:(part + 1) * T], w[:, k, part * P:(part + 1) * P], hT[:, k, :],
                                        start=(k == 0), stop=(k == KC - 1))
            done = PE.mark(ins)
            W.release(n, done)
            S.wait(done, hidden.get(f - 4))
            silu = S.mark(scalar.activation(act[:, 4 + f % 4, :], ps[:, 0:T], ACT.Silu))
            V.wait(silu, down_done.get(f - 4))
            hidden[f] = V.mark(vector.tensor_tensor(act[:, f % 4, :], act[:, 4 + f % 4, :], ps[:, T:2 * T], ALU.mult))
            banks.free(b, hidden[f])

        def down(f):
            n, loaded, w = w_out[f // 2]
            PE.wait(hidden[f], loaded)
            for tb in range(TB):
                for half in range(2):
                    at = (f % 2) * D + half * BANK
                    ins = tensor.matmul(psum[:, 2 * tb + half, :], act[:, f % 4, tb * P:(tb + 1) * P],
                                        w[:, at:at + BANK], start=(f == 0), stop=(f == FC - 1))
            down_done[f] = PE.mark(ins)
            if f % 2 == 1:
                W.release(n, down_done[f])

        gate_up(0)
        for f in range(1, FC):
            gate_up(f)
            down(f - 1)
        down(FC - 1)
        out_marks = []
        for tb in range(TB):
            for half in range(2):
                m = add_to_x(tb, half * BANK, psum[:, 2 * tb + half, :], 0.5, down_done[FC - 1])
                banks.free(2 * tb + half, m)
            out_marks.append(m)
        banks.use(range(8))
        return out_marks

    def project_tokens(src, groups, evac, ready, kcs=KC):
        out = []
        PE.wait(ready)
        for g in range(groups):
            got = [banks.take(PE) for _ in range(TB)]
            for k0 in range(0, kcs, 4):
                n, loaded, w = W.take()
                w = w.rearrange("p (k n) -> p k n", k=4)
                PE.wait(loaded)
                for tb in range(TB):
                    for k in range(4):
                        ins = tensor.matmul(got[tb][1], src[:, k0 + k, tb * P:(tb + 1) * P], w[:, k, :],
                                            start=(k0 + k == 0), stop=(k0 + k == kcs - 1))
                done = PE.mark(ins)
                W.release(n, done)
            for tb in range(TB):
                m = evac(tb, g, got[tb][1], done)
                banks.free(got[tb][0], m)
                out.append(m)
        return out

    def project_features(src, groups, evac, ready):
        out = []
        PE.wait(ready)
        for g in range(groups):
            n, loaded, w = W.take()
            w = w.rearrange("p (k n) -> p k n", k=KC)
            b, ps = banks.take(PE)
            PE.wait(loaded)
            for part in range(2):
                for k in range(KC):
                    ins = tensor.matmul(ps[:, part * T:(part + 1) * T], w[:, k, part * P:(part + 1) * P],
                                        src[:, k, :], start=(k == 0), stop=(k == KC - 1))
            done = PE.mark(ins)
            W.release(n, done)
            m = evac(g, ps, done)
            banks.free(b, m)
            out.append(m)
        return out

    def finish(ready):
        for tb in range(TB):
            s = sem(f"stored_{tb}")
            SP.wait(ready[tb])
            sync.dma_start(out[tb], x[:, tb, :]).then_inc(s, 16)
            sync.wait_ge(s, 16)

    env = Core()
    env.PE, env.V, env.S, env.G = PE, V, S, G
    env.W, env.A, env.banks, env.psum = W, A, banks, psum
    env.arena, env.unit, env.fm, env.tm = arena, unit, fm, tm
    env.col, env.small, env.masks, env.const_at = col, small, masks, const_at
    env.ident, env.iota, env.hT, env.tensor = ident, iota, hT, tensor
    env.vector, env.scalar, env.pool, env.spread = vector, scalar, pool, spread
    env.across, env.load, env.row, env.norm = across, load, row, norm
    env.transposed, env.rsqrt, env.add_to_x, env.project_tokens = transposed, rsqrt, add_to_x, project_tokens
    env.project_features = project_features
    x_ready = ffn(0, 0, x_loaded)
    x_ready = rwkv(env, x_ready)
    x_ready = ffn(0, 1, x_ready)
    kv_ready = shared_kv(env, x_ready)
    x_ready = ffn(1, 0, x_ready)
    x_ready = diff_attention(env, x_ready, kv_ready)
    x_ready = ffn(1, 1, x_ready)
    x_ready = mix_2(env, x_ready)
    x_ready = experts(env, x_ready)
    finish(x_ready)


def rwkv(k, x_ready):
    PE, V, S, G, W, banks, unit, fm, col = k.PE, k.V, k.S, k.G, k.W, k.banks, k.unit, k.fm, k.col
    tensor, vector, scalar, pool, hT, spread, across = (k.tensor, k.vector, k.scalar, k.pool, k.hT, k.spread, k.across)
    blk = lambda buffer: buffer.rearrange("p (c t) -> p c t", t=P)

    dx, mixed = fm(unit(16)), [fm(unit(1)), fm(unit(2))]
    rT, kT, aT, sig = fm(unit(3)), fm(unit(4)), fm(unit(5)), fm(unit(6))
    v_tok, g_tok = k.tm(unit(7)), k.tm(unit(8))
    kk = fm(unit(9))

    h_ready = k.norm(col("mix_norm", 0), x_ready)
    masks_ready = k.load(k.masks[:, :], k.A["consts"][:, 2 * P:13 * P])
    mask = lambda n: k.masks[:, n * P:(n + 1) * P]
    strict, upto, pair_t, headsum = mask(0), mask(1), mask(2), mask(10)
    level = [mask(3 + n) for n in range(LEVELS)]
    mid, end = k.small[:, 16:32], k.small[:, 32:48]
    carry_scale, stats = k.small[:, 48:56], k.small[:, 64:128]
    bonus = k.small[:, 128:160]
    a_sel, b_sel = k.const_at["headsel"]

    V.wait(h_ready)
    V.mark(vector.tensor_tensor(dx[:, :, 1:T], hT[:, :, 0:T - 1], hT[:, :, 1:T], ALU.subtract))
    dx_ready = V.mark(vector.tensor_scalar(dx[:, :, 0:1], hT[:, :, 0:1], -1.0, None, ALU.mult))
    mixed_read = [None, None]

    def mix(n, slot):
        mu = col("mu", n)
        V.wait(dx_ready, mixed_read[slot])
        for c in range(KC):
            m = V.mark(vector.scalar_tensor_tensor(out=mixed[slot][:, c, :], in0=dx[:, c, :], scalar=mu[:, c:c + 1],
                                                   in1=hT[:, c, :], op0=ALU.mult, op1=ALU.add))
        return m

    hidden_w, hidden_a = unit(10)[0:64, 0:T], unit(10)[0:64, T:2 * T]
    hidden_g, hidden_g2 = unit(10)[:, 2 * T:3 * T], unit(10)[0:32, 3 * T:4 * T]
    n_in, in_loaded, w_in = W.take()
    w_in = w_in[:, 0:KC * P].rearrange("p (k n) -> p k n", n=P)
    n_g1, g1_loaded, w_g1 = W.take()
    w_g1 = w_g1[:, 0:KC * 160].rearrange("p (k n) -> p k n", n=160)
    n_lo, lo_loaded, w_lo = W.take()

    def low_rank(weights, width, src, ready, dst, func, loaded):
        b, ps = banks.take(PE)
        PE.wait(ready, loaded)
        for c in range(KC):
            ins = tensor.matmul(ps[0:width, 0:T], weights(c), src[:, c, :], start=(c == 0), stop=(c == KC - 1))
        done = PE.mark(ins)
        S.wait(done)
        m = S.mark(scalar.activation(dst, ps[0:width, 0:T], func))
        banks.free(b, m)
        return done, m

    ready = mix(3, 0)
    mixed_read[0], w_hidden = low_rank(lambda c: w_in[:, c, 0:64], 64, mixed[0], ready, hidden_w, ACT.Tanh, in_loaded)
    ready = mix(4, 1)
    mixed_read[1], a_hidden = low_rank(lambda c: w_in[:, c, 64:P], 64, mixed[1], ready, hidden_a, ACT.Copy, in_loaded)
    W.release(n_in, mixed_read[1])
    ready = mix(5, 0)
    _, g_hidden = low_rank(lambda c: w_g1[:, c, 0:P], P, mixed[0], ready, hidden_g, ACT.Sigmoid, g1_loaded)
    mixed_read[0], g_hidden2 = low_rank(lambda c: w_g1[:, c, P:160], 32, mixed[0], ready, hidden_g2, ACT.Sigmoid,
                                        g1_loaded)
    W.release(n_g1, mixed_read[0])
    for what, hidden, base, dst in ((w_hidden, hidden_w, "w0", sig), (a_hidden, hidden_a, "a0", aT)):
        at = 0 if base == "w0" else D
        for c in range(0, KC, 2):
            b, ps = banks.take(PE)
            PE.wait(what, lo_loaded)
            for i in range(2):
                ins = tensor.matmul(ps[:, i * T:(i + 1) * T], w_lo[0:64, at + (c + i) * P:at + (c + i + 1) * P], hidden,
                                    start=True, stop=True)
            lo_read = PE.mark(ins)
            S.wait(lo_read)
            for i in range(2):
                m = S.mark(scalar.activation(dst[:, c + i, :], ps[:, i * T:(i + 1) * T], ACT.Sigmoid,
                                             bias=col(base)[:, c + i:c + i + 1]))
            banks.free(b, m)
        if base == "w0":
            sig_ready = m
        else:
            a_ready = m
    W.release(n_lo, lo_read)

    def to(dst):
        def evac(g, ps, ready):
            S.wait(ready)
            return S.mark(scalar.activation(dst[:, 2 * g:2 * g + 2, :], ps.rearrange("p (c t) -> p c t", t=T), ACT.Copy))
        return evac

    def to_tokens(dst):
        def evac(tb, g, ps, ready):
            S.wait(ready)
            return S.mark(scalar.activation(dst[:, tb, g * BANK:(g + 1) * BANK], ps, ACT.Copy))
        return evac

    ready = mix(0, 1)
    r_ready = k.project_features(mixed[1], 4, to(rT), ready)
    mixed_read[1] = (PE.semaphore, PE.count)
    ready = mix(1, 0)

    sums, centred, before = unit(10), unit(11), unit(12)
    keep = unit(13)
    V.wait(masks_ready, w_hidden, a_hidden)
    keep_row = k.load(keep[:, 0:P], k.A["consts"][:, k.const_at["scan_keep"][0]:k.const_at["scan_keep"][1]])
    V.wait(keep_row, sig_ready)
    m = V.mark(vector.tensor_copy(blk(keep)[:, 1:16, :], across(keep[:, 0:P], 15)))
    k_proj = k.project_features(mixed[0], 4, to(kT), ready)
    mixed_read[0] = (PE.semaphore, PE.count)
    ready_v = mix(2, 1)
    v_ready = k.project_tokens(mixed[1], 2, to_tokens(v_tok), ready_v)
    n_g2, g2_loaded, w_g2 = W.take()
    g_ready = []
    for tb in range(TB):
        for g in range(2):
            b, ps = banks.take(PE)
            PE.wait(g_hidden, g_hidden2, g2_loaded)
            tensor.matmul(ps, hidden_g[:, tb * P:(tb + 1) * P], w_g2[:, g * BANK:(g + 1) * BANK], start=True, stop=False)
            ins = tensor.matmul(ps, hidden_g2[:, tb * P:(tb + 1) * P], w_g2[0:32, D + g * BANK:D + (g + 1) * BANK],
                                start=False, stop=True)
            g2_read = PE.mark(ins)
            m2 = to_tokens(g_tok)(tb, g, ps, g2_read)
            banks.free(b, m2)
            g_ready.append(m2)
    W.release(n_g2, g2_read)

    V.wait(m, g2_read)
    m = V.mark(vector.tensor_tensor_scan(sums, keep, unit(6), 0.0, ALU.mult, ALU.add))
    V.wait(m)
    V.mark(vector.tensor_copy(mid, blk(sums)[:, :, P // 2 - 1]))
    m = V.mark(vector.tensor_copy(end, blk(sums)[:, :, P - 1]))
    V.wait(m)
    m = V.mark(vector.tensor_tensor(blk(centred), blk(sums), spread(mid, P), ALU.subtract))
    V.wait(m)
    m = V.mark(vector.tensor_tensor(before, centred, unit(6), ALU.subtract))
    mid_b, end_b = mid.rearrange("p (c b) -> p c b", b=TB), end.rearrange("p (c b) -> p c b", b=TB)
    V.mark(vector.tensor_tensor(carry_scale, end_b[:, :, 0], mid_b[:, :, 0], ALU.subtract))
    V.wait((V.semaphore, V.count))
    m = V.mark(vector.tensor_tensor(carry_scale, carry_scale, mid_b[:, :, 1], ALU.add))
    S.wait(m)
    p_in, p_before, p_inv = unit(10), unit(12), unit(13)
    S.mark(scalar.activation(p_in, centred, ACT.Exp, scale=-DECAY))
    S.mark(scalar.activation(p_before, before, ACT.Exp, scale=-DECAY))
    S.mark(scalar.activation(carry_scale, carry_scale, ACT.Exp, scale=-DECAY))
    p_ready = S.mark(scalar.activation(p_inv, centred, ACT.Exp, scale=DECAY))

    V.wait(k_proj, r_ready)
    m = V.mark(vector.tensor_tensor(kk, kT, spread(col("k_k"), T), ALU.mult))
    V.wait(m)
    square, norms = unit(14), unit(15)
    m = V.mark(vector.tensor_tensor(square, unit(9), unit(9), ALU.mult))
    for c in range(0, KC, 2):
        b, ps = banks.take(PE)
        PE.wait(m, masks_ready)
        m2 = PE.mark(tensor.matmul(ps, headsum, square[:, c * T:(c + 2) * T], start=True, stop=True))
        V.wait(m2)
        norm_in = V.mark(vector.tensor_scalar(norms[:, c * T:(c + 2) * T], ps, 1e-24, None, ALU.max))
        banks.free(b, norm_in)
    S.wait(norm_in)
    m = S.mark(scalar.activation(norms, norms, ACT.Sqrt))
    V.wait(a_ready, norm_in)
    rate = fm(unit(14))
    m3 = V.mark(vector.scalar_tensor_tensor(out=rate, in0=aT, scalar=-1.0, in1=spread(col("k_a"), T), op0=ALU.add,
                                            op1=ALU.mult))
    V.wait(m3)
    m3 = V.mark(vector.scalar_tensor_tensor(out=kT, in0=rate, scalar=1.0, in1=kT, op0=ALU.add, op1=ALU.mult))
    V.wait(m)
    m = V.mark(vector.reciprocal(norms, norms))
    V.wait(m)
    m = V.mark(vector.tensor_tensor(unit(9), unit(9), norms, ALU.mult))
    kk_ready = m
    V.wait(m3)
    rk = fm(unit(15))
    m = V.mark(vector.tensor_tensor(rk, rT, kT, ALU.mult))
    V.wait(m)
    m = V.mark(vector.tensor_tensor(rk, rk, spread(col("r_k"), T), ALU.mult))
    sel_ready = k.load(unit(0)[:, 0:KC * HEADS], k.A["consts"][:, a_sel:b_sel])
    sel = unit(0)[:, 0:KC * HEADS].rearrange("p (c h) -> p c h", h=HEADS)
    b, ps = banks.take(PE)
    PE.wait(m, sel_ready)
    for tb in range(TB):
        for c in range(KC):
            ins = tensor.matmul(ps[:, tb * HEADS:(tb + 1) * HEADS], rk[:, c, tb * P:(tb + 1) * P], sel[:, c, :],
                                start=(c == 0), stop=(c == KC - 1))
    bonus_done = PE.mark(ins)
    V.wait(p_ready, kk_ready)
    V.mark(vector.tensor_tensor(unit(3), unit(3), p_in, ALU.mult))
    V.mark(vector.tensor_tensor(unit(5), unit(5), unit(9), ALU.mult))
    V.wait((V.semaphore, V.count))
    V.mark(vector.tensor_tensor(unit(5), unit(5), p_inv, ALU.mult))
    V.mark(vector.tensor_tensor(unit(4), unit(4), p_inv, ALU.mult))
    scaled = V.mark(vector.scalar_tensor_tensor(out=unit(9), in0=unit(9), scalar=-1.0, in1=p_before, op0=ALU.mult,
                                                op1=ALU.mult))
    V.wait(bonus_done)
    bonus_ready = V.mark(vector.tensor_copy(bonus, ps[:, 0:TB * HEADS]))
    banks.free(b, bonus_ready)
    r_s, a_s, b_s, k_s = rT, kk, aT, kT

    b_tok, k_tok = unit(1)[:, 0:D], unit(1)[:, D:2 * D]
    for src, dst in ((b_s, b_tok), (k_s, k_tok)):
        for c0 in (0, 4):
            b, ps = banks.take(PE)
            PE.wait(scaled)
            for c in range(4):
                ins = tensor.transpose(ps[:, c * P:(c + 1) * P], src[:, c0 + c, 0:P], k.ident)
            m = PE.mark(ins)
            S.wait(m, mixed_read[0], mixed_read[1])
            tok_ready = S.mark(scalar.activation(dst[:, c0 * P:(c0 + 4) * P], ps, ACT.Copy))
            banks.free(b, tok_ready)

    ln = [unit(16)[:, 0:D], unit(16)[:, D:2 * D]]
    ln_ready = k.row("ln", unit(16), ready_v)
    heads4 = lambda buffer, g: buffer[:, g * 4 * P:(g + 1) * 4 * P].rearrange("p (h t) -> p h t", t=P)
    MT, TI, TIT, X = unit(10), unit(11), unit(12), unit(13)
    MAK, MRB, MRK = unit(14), unit(15), unit(0)
    wbuf, ubuf = unit(2)[:, 0:D], unit(2)[:, D:2 * D]
    y, y2 = unit(6)[:, 0:D], unit(6)[:, D:2 * D]
    read_before = [scaled, (PE.semaphore, PE.count), bonus_ready]

    def pair(c, h, tb, buffer):
        return buffer[h * HD:(h + 1) * HD, c, tb * P:(tb + 1) * P]

    S0 = unit(1)[:, 0:D]
    y_ready, state_ready = [], None
    for tb in range(TB):
        tit_ready = {}
        ti_ready, mt_ready = {}, {}

        def products(pair_of_groups, lhs, rhs):
            got = [banks.take(PE), banks.take(PE)]
            PE.wait(scaled)
            for i in range(4):
                for h in range(2):
                    c = 4 * pair_of_groups + i
                    ins = tensor.matmul(got[h][1][:, i * P:(i + 1) * P], pair(c, h, tb, lhs), pair(c, h, tb, rhs),
                                        start=True, stop=True)
            done = PE.mark(ins)
            return [(2 * pair_of_groups + h, got[h][0], got[h][1].rearrange("p (h t) -> p h t", t=P), done)
                    for h in range(2)]

        for gg in range(2):
            for g, b, ps, done in products(gg, a_s, b_s):
                V.wait(done, read_before)
                m = V.mark(vector.tensor_tensor(heads4(TI, g), ps, across(level[0], 4), ALU.mult))
                banks.free(b, m)
                G.wait(m)
                ti_ready[g] = G.mark(pool.tensor_tensor(heads4(TI, g), heads4(TI, g), across(k.ident, 4), ALU.add))
            for g, b, ps, done in products(gg, b_s, a_s):
                S.wait(done, read_before)
                mt_ready[g] = S.mark(scalar.activation(heads4(MT, g), ps, ACT.Copy))
                V.wait(mt_ready[g])
                m = V.mark(vector.tensor_tensor(heads4(TIT, g), ps, across(pair_t, 4), ALU.mult))
                banks.free(b, m)
                G.wait(m)
                tit_ready[g] = G.mark(pool.tensor_tensor(heads4(TIT, g), heads4(TIT, g), across(k.ident, 4), ALU.add))
            for dst, lhs, rhs, msk in ((MAK, k_s, a_s, strict), (MRB, b_s, r_s, upto), (MRK, k_s, r_s, upto)):
                for g, b, ps, done in products(gg, lhs, rhs):
                    V.wait(done)
                    masked = V.mark(vector.tensor_tensor(heads4(dst, g), ps, across(msk, 4), ALU.mult))
                    banks.free(b, masked)

        for n in range(1, LEVELS):
            x_done = {}
            for g in range(4):
                b, ps = banks.take(PE)
                PE.wait(mt_ready[g], ti_ready[g])
                for i in range(4):
                    ins = tensor.matmul(ps[:, i * P:(i + 1) * P], heads4(MT, g)[:, i, :], heads4(TI, g)[:, i, :],
                                        start=True, stop=True)
                done = PE.mark(ins)
                V.wait(done, tit_ready[g])
                x_done[g] = V.mark(vector.tensor_tensor(heads4(X, g), ps.rearrange("p (h t) -> p h t", t=P),
                                                        across(level[n], 4), ALU.mult))
                banks.free(b, x_done[g])
            for g in range(4):
                old_t, old_tt = ti_ready[g], tit_ready[g]
                b, ps = banks.take(PE)
                b2, ps2 = banks.take(PE)
                PE.wait(x_done[g], old_t, old_tt)
                for i in range(4):
                    ins = tensor.matmul(ps[:, i * P:(i + 1) * P], heads4(X, g)[:, i, :], heads4(TIT, g)[:, i, :],
                                        start=True, stop=True)
                if n < LEVELS - 1:
                    for i in range(4):
                        ins = tensor.matmul(ps2[:, i * P:(i + 1) * P], heads4(TIT, g)[:, i, :], heads4(X, g)[:, i, :],
                                            start=True, stop=True)
                done = PE.mark(ins)
                V.wait(done)
                tit_ready[g] = V.mark(vector.tensor_tensor(heads4(TIT, g), ps.rearrange("p (h t) -> p h t", t=P),
                                                           heads4(TIT, g), ALU.add))
                banks.free(b, tit_ready[g])
                if n < LEVELS - 1:
                    ti_ready[g] = V.mark(vector.tensor_tensor(heads4(TI, g), ps2.rearrange("p (h t) -> p h t", t=P),
                                                              heads4(TI, g), ALU.add))
                banks.free(b2, ti_ready[g] if n < LEVELS - 1 else tit_ready[g])

        def per_head(terms, dst, ready):
            last = None
            for half in range(2):
                b, ps = banks.take(PE)
                PE.wait(ready)
                for i in range(8):
                    head = 8 * half + i
                    todo = terms(head)
                    for j, (lhs, rhs) in enumerate(todo):
                        ins = tensor.matmul(ps[:, i * HD:(i + 1) * HD], lhs, rhs, start=(j == 0),
                                            stop=(j == len(todo) - 1))
                done = PE.mark(ins)
                S.wait(done)
                last = S.mark(scalar.activation(dst[:, half * BANK:(half + 1) * BANK], ps, ACT.Copy))
                banks.free(b, last)
            return last

        def mat(buffer, head):
            c, h = head // 2, head % 2
            at = (2 * (c // 4) + h) * 4 + c % 4
            return buffer[:, at * P:(at + 1) * P]

        hd = lambda buffer, head: buffer[:, head * HD:(head + 1) * HD]

        def carried(scaled_rows, head):
            if tb == 0:
                return []
            return [(scaled_rows[:, head // 2, tb * P:(tb + 1) * P], hd(S0, head))]

        w_ready = per_head(lambda n: [(mat(MAK, n), hd(v_tok[:, tb, :], n))] + carried(a_s, n), wbuf,
                           [masked, state_ready, v_ready])
        u_ready = per_head(lambda n: [(mat(TIT, n), hd(wbuf, n))], ubuf, [w_ready, list(tit_ready.values())])
        done_y = per_head(lambda n: [(mat(MRB, n), hd(ubuf, n)), (mat(MRK, n), hd(v_tok[:, tb, :], n))]
                          + carried(r_s, n), y, [u_ready, masked])
        if tb == 0:
            b, ps = banks.take(PE)
            PE.wait(tok_ready)
            for head in range(HEADS):
                c, h = head // 2, head % 2
                dst = ps[h * HD:(h + 1) * HD, c * HD:(c + 1) * HD]
                tensor.matmul(dst, hd(b_tok, head), hd(ubuf, head), start=True, stop=False)
                ins = tensor.matmul(dst, hd(k_tok, head), hd(v_tok[:, 0, :], head), start=False, stop=True)
            m = PE.mark(ins)
            V.wait(m, p_ready)
            V.mark(vector.memset(S0, 0.0))
            for h in range(2):
                half = slice(h * HD, (h + 1) * HD)
                state_ready = V.mark(vector.tensor_tensor(
                    S0[half, :].rearrange("p (c h i) -> p c h i", h=2, i=HD)[:, :, h, :],
                    ps[half, :].rearrange("p (c i) -> p c i", i=HD),
                    carry_scale[half, :].unsqueeze(2).to_broadcast([HD, KC, HD]), ALU.mult))
            banks.free(b, state_ready)
        read_before = [(PE.semaphore, PE.count)]

        byhead = lambda buffer: buffer.rearrange("p (h i) -> p h i", i=HD)
        mean, var = stats[:, 0:HEADS], stats[:, HEADS:2 * HEADS]
        V.wait(done_y, v_ready, g_ready, ln_ready)
        m = V.mark(vector.tensor_reduce(mean, byhead(y), AX.X, ALU.add))
        V.wait(m)
        m = V.mark(vector.tensor_scalar(mean, mean, 1.0 / HD, None, ALU.mult))
        V.wait(m)
        m = V.mark(vector.tensor_tensor(byhead(y), byhead(y), spread(mean, HD), ALU.subtract))
        V.wait(m)
        m = V.mark(vector.tensor_tensor(y2, y, y, ALU.mult))
        V.wait(m)
        m = V.mark(vector.tensor_reduce(var, byhead(y2), AX.X, ALU.add))
        V.wait(m)
        m = V.mark(vector.tensor_scalar(var, var, 1.0 / HD, 64e-5, ALU.mult, ALU.add))
        m = k.rsqrt(var, HEADS, m)
        V.wait(m)
        m = V.mark(vector.tensor_tensor(byhead(y), byhead(y), spread(var, HD), ALU.mult))
        V.wait(m)
        m = V.mark(vector.tensor_tensor(y, y, ln[0], ALU.mult))
        V.mark(vector.tensor_tensor(byhead(y2), byhead(v_tok[:, tb, :]),
                                    spread(bonus[:, tb * HEADS:(tb + 1) * HEADS], HD), ALU.mult))
        V.wait(m)
        m = V.mark(vector.tensor_tensor(y, y, ln[1], ALU.add))
        V.wait(m)
        m = V.mark(vector.tensor_tensor(y, y, y2, ALU.add))
        V.wait(m)
        m = V.mark(vector.tensor_tensor(y, y, g_tok[:, tb, :], ALU.mult))
        y_ready.append(k.transposed(y, tb, hT, m))

    out = {}

    def evac(tb, g, ps, ready):
        out[tb] = k.add_to_x(tb, g * BANK, ps, 1.0, ready)
        return out[tb]
    k.project_tokens(hT, 2, evac, y_ready)
    return [out[0], out[1]]


def head_norm(k, buffer, heads, eps, square, ss, ready, width=HD):
    V, vector = k.V, k.vector
    by_head = lambda b: b.rearrange("p (h i) -> p h i", i=width)
    V.wait(ready)
    m = V.mark(vector.tensor_tensor(square, buffer, buffer, ALU.mult))
    V.wait(m)
    m = V.mark(vector.tensor_reduce(ss, by_head(square), AX.X, ALU.add))
    V.wait(m)
    m = V.mark(vector.tensor_scalar(ss, ss, 1.0 / width, eps, ALU.mult, ALU.add))
    m = k.rsqrt(ss, heads, m)
    V.wait(m)
    return V.mark(vector.tensor_tensor(by_head(buffer), by_head(buffer), k.spread(ss, width), ALU.mult))


SHARED_KT, SHARED_V = 14, 15


def shared_kv(k, x_ready):
    V, S, unit, fm, tm = k.V, k.S, k.unit, k.fm, k.tm
    scalar = k.scalar
    h_ready = k.norm(k.col("kv_norm"), x_ready)
    k_tok, v_tok, kT = tm(unit(1)), tm(unit(SHARED_V)), fm(unit(SHARED_KT))

    def evac(tb, g, ps, ready):
        dst = k_tok if g < 2 else v_tok
        S.wait(ready)
        return S.mark(scalar.activation(dst[:, tb, g % 2 * BANK:(g % 2 + 1) * BANK], ps, ACT.Copy))
    marks = k.project_tokens(k.hT, 4, evac, h_ready)
    out = []
    for tb in range(TB):
        m = head_norm(k, k_tok[:, tb, :], HEADS, 1e-6, unit(2)[:, 0:D], k.small[:, 64:64 + HEADS], marks[3])
        out.append(k.transposed(k_tok[:, tb, :], tb, kT, m, scale=(k.col("k_norm", 0, 1), 1.0)))
    return out + [marks[-1]]


def softmax_attention(k, units, scores, soften, values, width):
    PE, S, banks, tensor, scalar = k.PE, k.S, k.banks, k.tensor, k.scalar
    softened, out = {}, []
    lag = 2
    for i in range(len(units) + lag):
        if i < len(units):
            softened[i] = soften(i, units[i], *scores(units[i]))
        if i >= lag:
            n = i - lag
            weights, keys, ready = softened.pop(n)
            b, ps = banks.take(PE)
            PE.wait(ready)
            for c in range(keys // P):
                ins = tensor.transpose(ps[:, c * P:(c + 1) * P], weights[:, c * P:(c + 1) * P], k.ident)
            done = PE.mark(ins)
            turned = k.unit(width)[:, (n % 4) * BANK:(n % 4) * BANK + keys]
            S.wait(done)
            m = S.mark(scalar.activation(turned, ps[:, 0:keys], ACT.Copy))
            banks.free(b, m)
            out.append(values(n, units[n], turned.rearrange("p (c q) -> p c q", q=P), m))
    return out


def diff_attention(k, x_ready, kv_ready):
    PE, V, S, banks, unit, fm, tm = k.PE, k.V, k.S, k.banks, k.unit, k.fm, k.tm
    tensor, vector, scalar, hT = k.tensor, k.vector, k.scalar, k.hT
    lam_init = 0.8 - 0.6 * math.exp(-0.3 * 1)
    kT, v_tok = fm(unit(SHARED_KT)), tm(unit(SHARED_V))
    h_ready = k.norm(k.col("mix_norm", 1), x_ready)
    a0 = k.const_at["causal_dist"][0]
    dist = k.masks[:, 0:3 * P]
    dist_ready = k.load(dist, k.A["consts"][:, a0:a0 + 3 * P], x_ready)

    lam = unit(3)[:, 0:4 * HD]
    lam_loaded = k.row("lam", lam, x_ready)
    sums, neg_lam = k.small[:, 16:18], k.small[:, 18:19]
    V.wait(lam_loaded)
    pairs = lam.rearrange("p (a b i) -> p a b i", a=2, b=2)
    V.mark(vector.tensor_tensor(unit(3)[:, BANK:BANK + 2 * HD].rearrange("p (a i) -> p a i", a=2), pairs[:, :, 0, :],
                                pairs[:, :, 1, :], ALU.mult))
    m = V.mark(vector.tensor_reduce(sums, unit(3)[:, BANK:BANK + 2 * HD].rearrange("p (a i) -> p a i", a=2), AX.X,
                                    ALU.add))
    S.wait(m)
    m = S.mark(scalar.activation(sums, sums, ACT.Exp))
    V.wait(m)
    V.mark(vector.tensor_tensor(neg_lam, sums[:, 1:2], sums[:, 0:1], ALU.subtract))
    lam_ready = V.mark(vector.tensor_scalar(neg_lam, neg_lam, lam_init, None, ALU.subtract))

    q_tok, qT = tm(unit(1)), fm(unit(4))

    def evac_q(tb, g, ps, ready):
        S.wait(ready)
        return S.mark(scalar.activation(q_tok[:, tb, g * BANK:(g + 1) * BANK], ps, ACT.Copy))
    marks = k.project_tokens(hT, 2, evac_q, h_ready)
    q_ready = []
    for tb in range(TB):
        m = head_norm(k, q_tok[:, tb, :], HEADS, 1e-6, unit(2)[:, 0:D], k.small[:, 64:64 + HEADS], marks)
        q_ready.append(k.transposed(q_tok[:, tb, :], tb, qT, m, scale=(k.col("q_norm", 0, 1), HD ** -0.5)))

    work = lambda i: unit(5 + i % 4)
    o_tok = tm(unit(10))
    stat = lambda i: k.small[:, 64 + 8 * (i % 4):72 + 8 * (i % 4)]
    attn_read = {}

    def scores(u):
        h, qb = u
        n = (qb + 1) * P
        got = [banks.take(PE), banks.take(PE)]
        PE.wait(q_ready, kv_ready)
        for m in range(2):
            rows = slice(m * HD, (m + 1) * HD)
            ins = tensor.matmul(got[m][1][:, 0:n], qT[rows, h, qb * P:(qb + 1) * P], kT[rows, h, 0:n], start=True,
                                stop=True)
        return got, n, PE.mark(ins)

    def soften(i, u, got, n, ready):
        h, qb = u
        s = work(i)[:, 0:2 * T].rearrange("p (m k) -> p m k", m=2)[:, :, 0:n]
        st = stat(i)
        V.wait(ready, dist_ready, lam_ready, attn_read.get(i - 4))
        slope = 2.0 ** (-8.0 * (h + 1) / DH)
        for m in range(2):
            done = V.mark(vector.scalar_tensor_tensor(out=s[:, m, :], in0=dist[:, qb * P:qb * P + n], scalar=slope,
                                                      in1=got[m][1][:, 0:n], op0=ALU.mult, op1=ALU.add))
            banks.free(got[m][0], done)
        top = V.mark(vector.tensor_reduce(st[:, 0:2], s, AX.X, ALU.max, negate=True))
        S.wait(top)
        for m in range(2):
            e = S.mark(scalar.activation(s[:, m, :], s[:, m, :], ACT.Exp, bias=st[:, m:m + 1],
                                         accum_out=st[:, 2 + m:3 + m]))
        V.wait(e)
        V.mark(vector.reciprocal(st[:, 4:6], st[:, 2:4]))
        V.mark(vector.tensor_scalar(s[:, 1, :], s[:, 1, :], st[:, 5:6], neg_lam, ALU.mult, ALU.mult))
        out = work(i)[:, 2 * T:2 * T + n]
        m = V.mark(vector.scalar_tensor_tensor(out=out, in0=s[:, 0, :], scalar=st[:, 4:5], in1=s[:, 1, :],
                                               op0=ALU.mult, op1=ALU.add))
        return out, n, m

    def values(i, u, turned, ready):
        h, qb = u
        b, ps = banks.take(PE)
        PE.wait(ready)
        attn_read[i] = (PE.semaphore, PE.count)
        for c in range(qb + 1):
            ins = tensor.matmul(ps[:, 0:P], turned[:, c, :], v_tok[:, c, h * P:(h + 1) * P], start=(c == 0),
                                stop=(c == qb))
        done = PE.mark(ins)
        S.wait(done)
        m = S.mark(scalar.activation(o_tok[:, qb, h * P:(h + 1) * P], ps[:, 0:P], ACT.Copy))
        banks.free(b, m)
        return m

    done = softmax_attention(k, [(h, qb) for h in range(DH) for qb in range(TB)], scores, soften, values, 9)
    o_ready = []
    for tb in range(TB):
        m = head_norm(k, o_tok[:, tb, :], DH, 1e-5, unit(2)[:, 0:D], k.small[:, 64:64 + DH], done, width=P)
        o_ready.append(k.transposed(o_tok[:, tb, :], tb, hT, m, scale=(k.col("subln", 0, 1), 1.0 - lam_init)))
    out = {}

    def evac(tb, g, ps, ready):
        out[tb] = k.add_to_x(tb, g * BANK, ps, 1.0, ready)
        return out[tb]
    k.project_tokens(hT, 2, evac, o_ready)
    return [out[0], out[1]]


def mix_2(k, x_ready):
    PE, V, S, W, banks, unit, fm, tm = k.PE, k.V, k.S, k.W, k.banks, k.unit, k.fm, k.tm
    tensor, vector, scalar, hT = k.tensor, k.vector, k.scalar, k.hT
    h_ready = k.norm(k.col("mix_gain_2"), x_ready)
    at = k.const_at
    window, before, before_neg = (k.masks[:, i * 3 * P:(i + 1) * 3 * P] for i in range(3))
    a = at["window_dist"][0]
    tables = k.load(k.masks[:, 0:9 * P], k.A["consts"][:, a:a + 9 * P], x_ready)
    bias = unit(15)
    bias_ready = k.row("gate_bias", bias, x_ready)
    sinks = k.small[:, 16:24]
    sinks_ready = k.row("sinks", sinks, x_ready)

    q_a, kv_a = unit(1).rearrange("p (b c) -> p b c", b=TB)[:, :, 0:BANK], unit(2)[:, 0:2 * T].rearrange(
        "p (b c) -> p b c", b=TB)
    k_dup = unit(2)[:, 2 * T:4 * T].rearrange("p (b g d i) -> p b g d i", b=TB, g=2, d=2)
    qbT, kbT = fm(unit(3))[:, 0:4, :], fm(unit(3))[:, 4:8, :]
    v_b = unit(4)[:, 0:D].rearrange("p (b c) -> p b c", b=TB)
    gates = [unit(5), unit(6)]
    qaT, kaT = fm(unit(7))[:, 0:4, :], fm(unit(7))[:, 4:6, :]

    def copy_to(dst, scale=None):
        def evac(tb, g, ps, ready):
            S.wait(ready)
            return S.mark(scalar.activation(dst[:, tb, :], ps, ACT.Copy))
        return evac
    qa_marks = k.project_tokens(hT, 1, copy_to(q_a), h_ready)
    n, loaded, w = W.take()
    w = w.rearrange("p (k n) -> p k n", k=KC)
    b, ps = banks.take(PE)
    PE.wait(loaded)
    for tb in range(TB):
        for c in range(KC):
            ins = tensor.matmul(ps[:, tb * T:(tb + 1) * T], hT[:, c, tb * P:(tb + 1) * P], w[:, c, :],
                                start=(c == 0), stop=(c == KC - 1))
    done = PE.mark(ins)
    W.release(n, done)
    S.wait(done)
    kva_ready = S.mark(scalar.activation(kv_a, ps.rearrange("p (b c) -> p b c", b=TB), ACT.Copy))
    banks.free(b, kva_ready)

    def evac_qk(g, ps, ready):
        S.wait(ready)
        src = ps.rearrange("p (c t) -> p c t", t=T)
        if g < 2:
            return S.mark(scalar.activation(qbT[:, 2 * g:2 * g + 2, :], src, ACT.Copy, scale=HD ** -0.5))
        return S.mark(scalar.activation(kbT[:, 2 * g - 4:2 * g - 2, :], src, ACT.Copy))
    qkb_ready = k.project_features(hT, 4, evac_qk, h_ready)
    vb_ready = k.project_tokens(hT, 1, copy_to(v_b), h_ready)

    qa_ready, ka_ready = [], []
    for tb in range(TB):
        m = head_norm(k, q_a[:, tb, :], 8, 1e-6, unit(8)[:, 0:BANK], k.small[:, 64:72], qa_marks)
        qa_ready.append(k.transposed(q_a[:, tb, :], tb, qaT, m, n=4, scale=(k.col("swa_q", 0, 1), HD ** -0.5)))
        m = head_norm(k, kv_a[:, tb, 0:P], 2, 1e-6, unit(8)[:, 0:P], k.small[:, 64:66], kva_ready)
        V.wait(m)
        for g in range(2):
            m = V.mark(vector.tensor_copy(k_dup[:, tb, g, :, :],
                                          k.across(kv_a[:, tb, g * HD:(g + 1) * HD], 2)))
        ka_ready.append(k.transposed(k_dup[:, tb, :, :, :].rearrange("p g d i -> p (g d i)"), tb, kaT, m, n=2,
                                     scale=(k.col("swa_k", 0, 1), 1.0)))

    def evac_gate(tb, g, ps, ready):
        V.wait(ready, bias_ready)
        dst = gates[tb][:, g * BANK:(g + 1) * BANK]
        m = V.mark(vector.tensor_tensor(dst, ps, bias[:, g * BANK:(g + 1) * BANK], ALU.add))
        S.wait(m)
        return S.mark(scalar.activation(dst, dst, ACT.Sigmoid)) and m
    k.project_tokens(hT, 4, evac_gate, h_ready)
    gates_ready = (S.semaphore, S.count)

    ya, yb = tm(unit(9))[:, :, 0:BANK], tm(unit(9))[:, :, BANK:D]
    work = lambda i: unit(10 + i % 4)
    stat = lambda i: k.small[:, 64 + 16 * (i % 4):80 + 16 * (i % 4)]
    units = [(c, qb) for c in range(4) for qb in range(TB)]
    read = {}

    def scores_of(qT, kT, kchunk, ready):
        def scores(u):
            c, qb = u
            n = (qb + 1) * P
            got = [banks.take(PE), banks.take(PE)]
            PE.wait(ready)
            for h in range(2):
                rows = slice(h * HD, (h + 1) * HD)
                ins = tensor.matmul(got[h][1][:, 0:n], qT[rows, c, qb * P:(qb + 1) * P], kT[rows, kchunk(c), 0:n],
                                    start=True, stop=True)
            return got, n, PE.mark(ins)
        return scores

    def soften_window(i, u, got, n, ready):
        c, qb = u
        s = work(i)[:, 0:2 * n].rearrange("p (h k) -> p h k", h=2)
        st = stat(i)
        V.wait(ready, tables, sinks_ready, read.get(i - 4))
        for h in range(2):
            slope = 2.0 ** (-8.0 * (2 * c + h + 1) / 8)
            done = V.mark(vector.scalar_tensor_tensor(out=s[:, h, :], in0=window[:, qb * P:qb * P + n], scalar=slope,
                                                      in1=got[h][1][:, 0:n], op0=ALU.mult, op1=ALU.add))
            banks.free(got[h][0], done)
        V.mark(vector.tensor_reduce(st[:, 0:2], s, AX.X, ALU.max))
        sink = sinks[:, 2 * c:2 * c + 2]
        V.mark(vector.tensor_tensor(st[:, 0:2], st[:, 0:2], sink, ALU.max))
        V.mark(vector.tensor_tensor(st[:, 2:4], sink, st[:, 0:2], ALU.subtract))
        m = V.mark(vector.tensor_scalar(st[:, 0:2], st[:, 0:2], -1.0, None, ALU.mult))
        S.wait(m)
        S.mark(scalar.activation(st[:, 2:4], st[:, 2:4], ACT.Exp))
        for h in range(2):
            m = S.mark(scalar.activation(s[:, h, :], s[:, h, :], ACT.Exp, bias=st[:, h:h + 1],
                                         accum_out=st[:, 4 + h:5 + h]))
        V.wait(m)
        V.mark(vector.tensor_tensor(st[:, 4:6], st[:, 4:6], st[:, 2:4], ALU.add))
        V.mark(vector.reciprocal(st[:, 4:6], st[:, 4:6]))
        for h in range(2):
            m = V.mark(vector.tensor_scalar(s[:, h, :], s[:, h, :], st[:, 4 + h:5 + h], None, ALU.mult))
        return work(i)[:, 0:2 * n], 2 * n, m

    def values_of(v, column, dst):
        def values(i, u, turned, ready):
            c, qb = u
            b, ps = banks.take(PE)
            PE.wait(ready)
            read[i] = (PE.semaphore, PE.count)
            blocks = qb + 1
            for h in range(2):
                for j in range(blocks):
                    at = column(2 * c + h)
                    ins = tensor.matmul(ps[:, h * HD:(h + 1) * HD], turned[:, h * blocks + j, :],
                                        v[:, j, at:at + HD], start=(j == 0), stop=(j == blocks - 1))
            done = PE.mark(ins)
            S.wait(done)
            m = S.mark(scalar.activation(dst[:, qb, 2 * c * HD:(2 * c + 2) * HD], ps[:, 0:P], ACT.Copy))
            banks.free(b, m)
            return m
        return values

    done_a = softmax_attention(k, units, scores_of(qaT, kaT, lambda c: c // 2, [qa_ready, ka_ready]), soften_window,
                               values_of(kv_a, lambda h: P + h // 4 * HD, ya), 14)

    def soften_stick(i, u, got, n, ready):
        c, qb = u
        z, e, lb, keep, total = (work(i)[:, j * 2 * T:j * 2 * T + 2 * n].rearrange("p (h k) -> p h k", h=2)
                                 for j in (0, 1, 2, 3, 3))
        pre = e
        V.wait(ready, tables, read.get(i - 4))
        for h in range(2):
            done = V.mark(vector.tensor_copy(z[:, h, :], got[h][1][:, 0:n]))
            banks.free(got[h][0], done)
        S.wait(done, (V.semaphore, V.count))
        S.mark(scalar.activation(e, z, ACT.Abs))
        S.mark(scalar.activation(e, e, ACT.Exp, scale=-1.0))
        m = S.mark(scalar.activation(e, e, ACT.Ln, bias=1.0))
        V.wait(m)
        V.mark(vector.scalar_tensor_tensor(out=lb, in0=z, scalar=0.0, in1=e, op0=ALU.min, op1=ALU.subtract))
        V.mark(vector.tensor_tensor(keep, lb, z, ALU.subtract))
        V.mark(vector.tensor_tensor(keep, keep, k.across(before[:, qb * P:qb * P + n], 2), ALU.mult))
        for h in range(2):
            V.mark(vector.tensor_tensor_scan(pre[:, h, :], keep[:, h, :], keep[:, h, :], 0.0, ALU.add, ALU.bypass))
        V.mark(vector.tensor_tensor(lb, lb, k.across(before_neg[:, qb * P:qb * P + n], 2), ALU.add))
        m = V.mark(vector.tensor_tensor(lb, lb, pre, ALU.subtract))
        S.wait(m)
        for h in range(2):
            m = S.mark(scalar.activation(lb[:, h, :], lb[:, h, :], ACT.Exp, bias=pre[:, h, n - 1:n]))
        return work(i)[:, 4 * T:4 * T + 2 * n], 2 * n, m

    read.clear()
    V.wait(done_a)
    done_b = softmax_attention(k, units, scores_of(qbT, kbT, lambda c: c, qkb_ready), soften_stick,
                               values_of(v_b, lambda h: h * HD, yb), 14)

    yaT, ybT = fm(unit(7))[:, 0:4, :], fm(unit(7))[:, 4:8, :]
    merged, part = tm(unit(8)), unit(10)[:, 0:BANK]
    ready = [k.transposed(ya[:, tb, :], tb, yaT, [done_a, done_b], n=4) for tb in range(TB)]
    ready += [k.transposed(yb[:, tb, :], tb, ybT, [done_a, done_b], n=4) for tb in range(TB)]

    def evac_a(tb, g, ps, ready):
        V.wait(ready, gates_ready)
        cols = slice(g * BANK, (g + 1) * BANK)
        return V.mark(vector.tensor_tensor(merged[:, tb, cols], ps, gates[tb][:, cols], ALU.mult))

    def evac_b(tb, g, ps, ready):
        V.wait(ready, gates_ready)
        cols = slice(g * BANK, (g + 1) * BANK)
        m = V.mark(vector.tensor_tensor(part, ps, gates[tb][:, D + g * BANK:D + (g + 1) * BANK], ALU.mult))
        V.mark(vector.tensor_tensor(merged[:, tb, cols], merged[:, tb, cols], part, ALU.add))
        return m
    k.project_tokens(yaT, 2, evac_a, ready, kcs=4)
    k.project_tokens(ybT, 2, evac_b, ready, kcs=4)
    merged_ready = (V.semaphore, V.count)
    ready = [k.transposed(merged[:, tb, :], tb, hT, merged_ready) for tb in range(TB)]
    out = {}

    def evac(tb, g, ps, ready):
        out[tb] = k.add_to_x(tb, g * BANK, ps, 1.0, ready)
        return out[tb]
    k.project_tokens(hT, 2, evac, ready)
    return [out[0], out[1]]


def top_sixteen(k, values, spare, top, index):
    V, vector = k.V, k.vector
    V.mark(vector.max(top[:, 0:8], values))
    V.mark(vector.max_index(index[:, 0:8], top[:, 0:8], values))
    V.mark(vector.match_replace(spare, top[:, 0:8], values, -3.0e38))
    V.mark(vector.max(top[:, 8:16], spare))
    return V.mark(vector.max_index(index[:, 8:16], top[:, 8:16], spare))


def experts(k, x_ready):
    PE, V, S, G, W, banks, unit, tm = k.PE, k.V, k.S, k.G, k.W, k.banks, k.unit, k.tm
    tensor, vector, scalar, pool, hT = k.tensor, k.vector, k.scalar, k.pool, k.hT
    h_ready = k.norm(k.col("ffn_gain_2"), x_ready)
    SETS = 2 * PH

    qT = k.arena[:, 1:3, :].rearrange("p u (c t) -> p (u c) t", t=T)

    def evac_q(g, ps, ready):
        S.wait(ready)
        return S.mark(scalar.activation(qT[:, 2 * g:2 * g + 2, :], ps.rearrange("p (c t) -> p c t", t=T), ACT.Copy))
    q_ready = k.project_features(hT, 8, evac_q, h_ready)
    n, loaded, keys = W.take()
    keys = keys.rearrange("p (s k) -> p s k", k=KEYS)
    score = [unit(3 + tb).rearrange("p (s k) -> p s k", k=KEYS) for tb in range(TB)]
    scored = [[], []]
    PE.wait(q_ready, loaded)
    for tb in range(TB):
        for s0 in range(0, SETS, 4):
            b, ps = banks.take(PE)
            for s in range(4):
                ins = tensor.matmul(ps[:, s * KEYS:(s + 1) * KEYS], qT[:, s0 + s, tb * P:(tb + 1) * P],
                                    keys[:, s0 + s, :], start=True, stop=True)
            done = PE.mark(ins)
            S.wait(done)
            m = S.mark(scalar.activation(score[tb][:, s0:s0 + 4, :], ps.rearrange("p (s k) -> p s k", k=KEYS),
                                         ACT.Copy))
            banks.free(b, m)
            scored[tb].append(m)
    W.release(n, done)

    picked = k.masks[:, 0:3 * T].rearrange("p (w t) -> p w t", w=3)
    for tb in range(TB):
        base = unit(5 + tb)
        top = base[:, 0:T].rearrange("p (h s n) -> p h s n", h=PH, s=2)
        index_raw = base[:, T:2 * T].bitcast(U32).rearrange("p (h s n) -> p h s n", h=PH, s=2)
        index = base[:, 2 * T:3 * T].rearrange("p (h s n) -> p h s n", h=PH, s=2)
        best = base[:, 3 * T:3 * T + P].rearrange("p (h n) -> p h n", h=PH)
        position = base[:, 3 * T + P:4 * T].bitcast(U32)
        part = [base[:, 4 * T + i * P:4 * T + (i + 1) * P] for i in range(2)]
        raw = base[:, 5 * T:5 * T + P].bitcast(U32)
        spare = unit(7 + tb)
        gate = base[:, 5 * T + P:6 * T].rearrange("p (h n) -> p h n", h=PH)
        chosen = [base[:, 6 * T + i * P:6 * T + (i + 1) * P] for i in range(2)]
        total = base[:, 7 * T:7 * T + PH]
        V.wait(scored[tb])
        for h in range(PH):
            for s in range(2):
                top_sixteen(k, score[tb][:, 2 * h + s, :], spare[:, 0:KEYS], top[:, h, s, :], index_raw[:, h, s, :])
        V.mark(vector.tensor_copy(base[:, 2 * T:3 * T], base[:, T:2 * T].bitcast(U32)))
        for h in range(PH):
            cand = spare[:, T:2 * T]
            V.mark(vector.tensor_tensor(cand.rearrange("p (a b) -> p a b", b=TOP), k.spread(top[:, h, 0, :], TOP),
                                        k.across(top[:, h, 1, :], TOP), ALU.add))
            top_sixteen(k, cand, spare[:, 0:T], best[:, h, :], position[:, h * TOP:(h + 1) * TOP])
        for side, op, by in ((0, ALU.logical_shift_right, 4), (1, ALU.bitwise_and, TOP - 1)):
            V.mark(vector.tensor_scalar(raw, position, by, None, op))
            V.mark(vector.tensor_copy(part[side], raw))
            hit = unit(9 + tb).rearrange("p (m n) -> p m n", n=TOP)
            V.mark(vector.tensor_tensor(hit, k.spread(part[side], TOP), k.across(k.iota[:, 0:TOP], P), ALU.is_equal))
            for h in range(PH):
                mine = hit[:, h * TOP:(h + 1) * TOP, :]
                V.mark(vector.tensor_tensor(mine, mine, k.across(index[:, h, side, :], TOP), ALU.mult))
            V.mark(vector.tensor_reduce(chosen[side], hit, AX.X, ALU.add))
        m = V.mark(vector.tensor_tensor(gate, best, best[:, :, 0:1].to_broadcast([P, PH, TOP]), ALU.subtract))
        S.wait(m)
        m = S.mark(scalar.activation(gate, gate, ACT.Exp))
        V.wait(m)
        V.mark(vector.tensor_reduce(total, gate, AX.X, ALU.add))
        V.mark(vector.reciprocal(total, total))
        m = V.mark(vector.tensor_tensor(gate, gate, k.spread(total, TOP), ALU.mult))
        b, ps = banks.take(PE)
        PE.wait(m)
        for i, src in enumerate((base[:, 5 * T + P:6 * T], chosen[0], chosen[1])):
            ins = tensor.transpose(ps[:, i * P:(i + 1) * P], src, k.ident)
        m = PE.mark(ins)
        V.wait(m)
        picked_ready = V.mark(vector.tensor_copy(picked[:, :, tb * P:(tb + 1) * P],
                                                 ps[:, 0:3 * P].rearrange("p (w t) -> p w t", w=3)))
        banks.free(b, picked_ready)

    gates = k.arena[:, 0:16, :].rearrange("p u (j t) -> p (u j) t", t=T)
    lot = 4
    onehot = unit(16).rearrange("p (b s l k) -> p b s l k", b=2, s=2, l=lot)
    used = {}
    S.wait(picked_ready)
    for q in range(T // lot):
        i_hot, j_hot = onehot[:, q % 2, 0, :, :], onehot[:, q % 2, 1, :, :]
        V.wait(used.get(q - 2))
        G.wait(picked_ready, used.get(q - 2))
        for n in range(lot):
            t = q * lot + n
            mi = V.mark(vector.tensor_scalar(i_hot[:, n, :], k.iota, picked[:, 1, t:t + 1], picked[:, 0, t:t + 1],
                                             ALU.is_equal, ALU.mult))
            mj = G.mark(pool.tensor_scalar(j_hot[:, n, :], k.iota, picked[:, 2, t:t + 1], None, ALU.is_equal))
        b, ps = banks.take(PE)
        PE.wait(mi, mj)
        for n in range(lot):
            ins = tensor.matmul(ps[:, n * KEYS:(n + 1) * KEYS], i_hot[:, n, :], j_hot[:, n, :], start=True, stop=True)
        used[q] = PE.mark(ins)
        S.wait(used[q])
        g_ready = S.mark(scalar.activation(gates[:, :, q * lot:(q + 1) * lot].rearrange("p j t -> p t j"),
                                           ps.rearrange("p (t j) -> p t j", t=lot), ACT.Copy))
        banks.free(b, g_ready)

    banks.use(range(4, 8))
    PE.wait(banks.freed[0:4])
    pairs = KEYS // 2
    active = unit(16).rearrange("p (b j t) -> p b j t", b=4, t=T)
    weighed, v_tile = {}, {}

    def activate(pair):
        n, loaded, u = W.take()
        v_tile[pair] = W.take()
        u = u.rearrange("p (j k i) -> p j k i", j=2, k=KC)
        b, ps = banks.take(PE)
        PE.wait(loaded)
        for jj in range(2):
            for c in range(KC):
                ins = tensor.matmul(ps[:, jj * T:(jj + 1) * T], u[:, jj, c, :], hT[:, c, :], start=(c == 0),
                                    stop=(c == KC - 1))
        done = PE.mark(ins)
        W.release(n, done)
        a = active[:, pair % 4, :, :]
        S.wait(done, weighed.get(pair - 4), used[T // lot - 1])
        m = S.mark(scalar.activation(a, ps.rearrange("p (j t) -> p j t", j=2), ACT.Gelu))
        banks.free(b, m)
        g = gates[:, 2 * pair:2 * pair + 2, :]
        V.wait(m, g_ready)
        weighed[pair] = V.mark(vector.tensor_tensor(g, g, a, ALU.mult))

    def add_up(pair):
        n, loaded, v = v_tile.pop(pair)
        PE.wait(weighed[pair], loaded)
        for jj in range(2):
            for tb in range(TB):
                for half in range(2):
                    at = jj * D + half * BANK
                    ins = tensor.matmul(psum[:, 2 * tb + half, :], gates[:, 2 * pair + jj, tb * P:(tb + 1) * P],
                                        v[:, at:at + BANK], start=(pair == 0 and jj == 0),
                                        stop=(pair == pairs - 1 and jj == 1))
        done = PE.mark(ins)
        W.release(n, done)
        return done

    psum = k.psum
    activate(0)
    for pair in range(1, pairs):
        activate(pair)
        add_up(pair - 1)
    done = add_up(pairs - 1)
    return [[k.add_to_x(tb, half * BANK, psum[:, 2 * tb + half, :], 1.0, done) for half in range(2)][-1]
            for tb in range(TB)]


def by_column(v):
    return v.reshape(-1, P).T


def feature_tiles(w):
    k, n = w.shape
    return w.reshape(k // P, P, n // T, T).transpose(2, 1, 0, 3).reshape(n // T, P, k // P * T)


def token_tiles(w):
    k, n = w.shape
    return w.reshape(k // 512, 4, P, n // BANK, BANK).transpose(3, 0, 2, 1, 4).reshape(-1, P, 4 * BANK)


def constants():
    i = np.arange(P)
    row, colm = i[:, None], i[None, :]
    parts = {
        "ident": (row == colm), "iota": np.broadcast_to(colm, (P, P)),
        "strict": row < colm, "upto": row <= colm,
    }
    def level(m):
        return (row // (2 * m) == colm // (2 * m)) & (row % (2 * m) >= m) & (colm % (2 * m) < m)
    parts["pairT"] = level(1).T
    parts["level"] = np.concatenate([level(2 ** n) for n in range(LEVELS)], axis=1)
    parts["headsum"] = row // HD == colm // HD
    sel = np.zeros((P, KC, HEADS))
    for c in range(KC):
        for h in range(2):
            sel[h * HD:(h + 1) * HD, c, 2 * c + h] = 1
    parts["headsel"] = sel.reshape(P, -1)
    parts["scan_keep"] = np.broadcast_to((colm != 0), (P, P))
    q = np.concatenate([np.broadcast_to(row, (P, P)), np.broadcast_to(row + P, (P, 2 * P))], axis=1)
    k = np.broadcast_to(np.concatenate([i, i, i + P])[None, :], (P, 3 * P))
    parts["causal_dist"] = np.where(q >= k, -(q - k).astype(np.float64), NEG)
    chunk = 64
    near = (k // chunk <= q // chunk) & (k // chunk >= q // chunk - 2)
    parts["window_dist"] = np.where(near, -np.abs(q - k).astype(np.float64), NEG)
    parts["before"] = k < q
    parts["before_neg"] = np.where(k < q, 0.0, NEG)
    return np.concatenate([parts[name].astype(np.float32) for name, _ in CONSTS], axis=1)


def kernel(**inputs):
    import concourse.bacc as bacc
    from contextlib import ExitStack
    from concourse.bass_utils import run_bass_kernel_spmd

    a = {k: np.asarray(v) for k, v in inputs.items()}
    arrays = {"x": a["x"].reshape(TB, P, D)}
    cat = lambda *v: np.concatenate(v, axis=1)
    arrays["cols"] = cat(
        by_column(a["ffn_norm"].reshape(-1)), by_column(a["mix_norm"].reshape(-1)), by_column(a["rwkv_mu"].reshape(-1)),
        *(by_column(a[n].reshape(-1)) for n in ("rwkv_w0", "rwkv_a0", "rwkv_k_k", "rwkv_k_a", "rwkv_r_k", "kv_norm",
                                                "mix_norm_gain_2", "ffn_norm_gain_2", "diff_subln")),
        *(np.tile(a[n].reshape(-1), 2)[:, None] for n in ("k_norm", "diff_q_norm", "swa_q_gain_2", "swa_k_gain_2")))
    arrays["consts"] = constants()
    arrays["ffn_in"] = a["ffn_w_in"].reshape(2, 2, KC, P, 2, FC, P).transpose(0, 1, 5, 3, 2, 4, 6).reshape(
        2, 2, FC, P, TILE)
    arrays["ffn_out"] = a["ffn_w_out"].reshape(2, 2, FC // 2, 2, P, D).transpose(0, 1, 2, 4, 3, 5).reshape(
        2, 2, FC // 2, P, TILE)
    rows = lambda w: w.reshape(KC, P, -1).transpose(1, 0, 2)
    arrays["lora_in"] = np.concatenate([rows(a["rwkv_w1"][0]), rows(a["rwkv_a1"][0])], axis=2).reshape(P, KC * P)
    arrays["g1"] = rows(a["rwkv_g1"][0]).reshape(P, KC * 160)
    arrays["lora_out"] = cat(a["rwkv_w2"][0], a["rwkv_a2"][0])
    arrays["g2"] = a["rwkv_g2"][0]
    w_rkv = a["rwkv_w_rkv"][0]
    arrays["w_r"], arrays["w_k"], arrays["w_v"] = feature_tiles(w_rkv[0]), feature_tiles(w_rkv[1]), token_tiles(w_rkv[2])
    arrays["w_o"] = token_tiles(a["rwkv_w_o"][0])
    arrays["ln"] = cat(a["rwkv_ln_g"], a["rwkv_ln_b"])
    arrays["w_kv"] = token_tiles(a["w_kv"])
    arrays["diff_w_q"] = token_tiles(a["diff_w_q"][0])
    arrays["diff_w_o"] = token_tiles(a["diff_w_o"][0])
    arrays["lam"] = a["diff_lambda"].reshape(1, 4 * HD)
    w = a["w_in_2"][0]
    arrays["in_q_a"] = token_tiles(w[:, 0:512])
    arrays["in_kv_a"] = feature_tiles(w[:, 512:768])
    arrays["in_qk_b"] = feature_tiles(w[:, 768:1792])
    arrays["in_v_b"] = token_tiles(w[:, 1792:2304])
    arrays["in_gates"] = token_tiles(w[:, 2304:])
    arrays["gate_bias"] = a["gate_bias_2"]
    arrays["sinks"] = a["swa_sinks_2"]
    arrays["up_swa"], arrays["up_sb"] = token_tiles(a["w_up_swa_2"][0]), token_tiles(a["w_up_sb_2"][0])
    arrays["w_out"] = token_tiles(a["w_out_2"][0])
    arrays["peer_q"] = feature_tiles(a["peer_w_q_2"][0])
    arrays["sub_keys"] = a["peer_sub_keys_2"][0].reshape(16, P, P).transpose(2, 0, 1).reshape(1, P, 16 * P)
    u = a["peer_u_2"][0].reshape(KEYS, KEYS // 2, 2, KC, P)
    arrays["peer_u"] = u.transpose(1, 4, 2, 3, 0).reshape(KEYS // 2, P, TILE)
    v = a["peer_v_2"][0].reshape(KEYS, KEYS // 2, 2, D)
    arrays["peer_v"] = v.transpose(1, 0, 2, 3).reshape(KEYS // 2, P, TILE)

    nc = bacc.Bacc("TRN2", target_bir_lowering=False, num_devices=1)
    handles, launch = {}, {}
    for name, value in arrays.items():
        launch[f"{name}_dram"] = np.ascontiguousarray(value)
        handles[name] = nc.dram_tensor(f"{name}_dram", value.shape, F32, kind="ExternalInput").ap()
    out = nc.dram_tensor("out_dram", (TB, P, D), F32, kind="ExternalOutput").ap()
    with ExitStack() as stack:
        block(nc, handles, out, stack)
    result = run_bass_kernel_spmd(nc, [launch], core_ids=[0])
    return result.results[0]["out_dram"].reshape(1, T, D)
```

```python
import math
from contextlib import ExitStack

import numpy as np

import concourse.bass as bass
import concourse.mybir as mybir
from concourse.alu_op_type import AluOpType as ALU

F32 = mybir.dt.float32
F32R = mybir.dt.float32r
U32 = mybir.dt.uint32
ACT = mybir.ActivationFunctionType
AX = mybir.AxisListType

P = 128
T = 256
TB = T // P
D = 1024
KC = D // P
FF = 2816
FC = FF // P
UNIT = 2048
TILE = 1024
RAW_SLOTS = 4
SPLIT_SLOTS = 3
BANK = 512
HEADS = 16
HD = 64
DH = 8
KEYS = 128
TOP = 16
PH = 8
NEG = -1e30
DECAY = math.exp(-0.5)
LEVELS = 7

COLS = [("ffn_norm", 4 * KC), ("mix_norm", 2 * KC), ("mu", 6 * KC), ("w0", KC), ("a0", KC), ("k_k", KC),
        ("k_a", KC), ("r_k", KC), ("kv_norm", KC), ("mix_gain_2", KC), ("ffn_gain_2", KC),
        ("subln", 1), ("k_norm", 1), ("q_norm", 1), ("swa_q", 1), ("swa_k", 1)]
CONSTS = [("ident", P), ("iota", P), ("strict", P), ("upto", P), ("pairT", P), ("level", LEVELS * P),
          ("headsum", P), ("headsel", KC * HEADS), ("scan_keep", P), ("causal_dist", 3 * P),
          ("window_dist", 3 * P), ("before", 3 * P), ("before_neg", 3 * P)]


def offsets(table):
    out, at = {}, 0
    for name, n in table:
        out[name] = (at, at + n)
        at += n
    return out, at


class Lane:

    def __init__(self, engine, semaphore, linked):
        self.engine, self.semaphore, self.count, self.seen = engine, semaphore, 0, {}
        self.linked = linked

    def wait(self, *marks):
        for m in marks:
            if m is None:
                continue
            if isinstance(m, list):
                self.wait(*m)
                continue
            sem, value = m
            if self.seen.get(sem.name, 0) < value:
                self.engine.wait_ge(sem, value)
                self.seen[sem.name] = value

    def mark(self, instruction):
        instruction.then_inc(self.semaphore, 1)
        self.count += 1
        done = (self.semaphore, self.count)
        if self.linked:
            self.wait(done)
        return done


class Weights:

    def __init__(self, lane, raw, raw_semaphores, high, low, S, V, tiles):
        self.lane, self.raw, self.sems, self.high, self.low = lane, raw, raw_semaphores, high, low
        self.S, self.V, self.tiles = S, V, tiles
        self.slots = high.shape[1]
        self.sent, self.parted, self.taken, self.used = 0, 0, 0, []
        self.ready = []
        for _ in raw_semaphores:
            self.load()

    def load(self):
        n = self.sent
        if n < len(self.tiles):
            slot = n % len(self.sems)
            self.lane.engine.dma_start(self.raw[:, slot, :], self.tiles[n]).then_inc(self.sems[slot], 16)
        self.sent += 1

    def split(self):
        n = self.parted
        self.parted += 1
        if n >= len(self.tiles):
            return
        S, V, slot, to = self.S, self.V, n % len(self.sems), n % self.slots
        loaded = (self.sems[slot], 16 * (n // len(self.sems) + 1))
        reader = self.used[n - self.slots] if n >= self.slots else None
        raw = self.raw[:, slot, :]
        S.wait(loaded, reader)
        m = S.mark(S.engine.activation(self.high[:, to, :], raw, ACT.Copy))
        V.wait(loaded, m, reader)
        m = V.mark(V.engine.tensor_tensor(self.low[:, to, :], raw, self.high[:, to, :].bitcast(F32), ALU.subtract))
        self.ready.append(m)
        self.lane.wait(m)
        self.load()

    def take(self, lane):
        n = self.taken
        self.taken += 1
        while self.parted <= n + 1:
            self.split()
        lane.wait(self.ready[n])
        return self.high[:, n % self.slots, :], self.low[:, n % self.slots, :]

    def release(self, mark):
        self.used.append(mark)
        while self.parted < len(self.used) + self.slots - 1:
            self.split()


class Banks:

    def __init__(self, psum):
        self.psum, self.freed = psum, [None] * 8
        self.use(range(8))

    def use(self, banks):
        self.order, self.at = list(banks), 0

    def take(self, lane):
        b = self.order[self.at % len(self.order)]
        self.at += 1
        lane.wait(self.freed[b])
        return b, self.psum[:, b, :]

    def free(self, b, mark):
        self.freed[b] = mark


class Core:
    pass


def block(nc, A, out, stack):
    sb = lambda name, shape, dtype=F32, room=stack: room.enter_context(nc.sbuf_tensor(name, shape, dtype))
    sem = lambda name: stack.enter_context(nc.semaphore(name))
    tensor, vector, scalar, pool, sync = nc.tensor, nc.vector, nc.scalar, nc.gpsimd, nc.sync

    x = sb("x", [P, TB, D])
    hT_high, hT_low = sb("hT_high", [P, KC, T], F32R), sb("hT_low", [P, KC, T], F32R)
    hT = (hT_high, hT_low)
    raw = sb("raw_tiles", [P, RAW_SLOTS, TILE])
    tile_high = sb("tile_high", [P, SPLIT_SLOTS, TILE], F32R)
    tile_low = sb("tile_low", [P, SPLIT_SLOTS, TILE], F32R)
    col_at, n_cols = offsets(COLS)
    cols = sb("cols", [P, n_cols])
    const_at, n_consts = offsets(CONSTS)
    ident = sb("ident", [P, P])[:, :]
    small = sb("small", [P, 256])
    minus_half = sb("minus_half", [P, 16])
    psum = stack.enter_context(nc.psum_tensor("psum", [P, 8, BANK], F32))

    PE, V, S, G, SP = (Lane(e, sem(n), linked) for e, n, linked in (
        (tensor, "tensor_done", False), (vector, "vector_done", True), (scalar, "scalar_done", True),
        (pool, "pool_done", True), (sync, "sync_done", False)))

    def col(name, n=0, k=KC):
        a = col_at[name][0] + n * k
        return cols[:, a:a + k]

    def fm(buffer):
        return buffer.rearrange("p (c t) -> p c t", t=T)

    def tm(buffer):
        return buffer.rearrange("p (b c) -> p b c", b=TB)

    def spread(ap, n):
        return ap.unsqueeze(2).to_broadcast([P, ap.shape[1], n])

    def across(ap, n):
        return ap.unsqueeze(1).to_broadcast([P, n, ap.shape[1]])

    def tiles_of(*names):
        return [A[name][i] for name in names for i in range(A[name].shape[0])]

    def ffn_tiles(l, j):
        out = []
        for f in range(FC + 1):
            if f < FC:
                out += [A["ffn_in"][l, j, f, 0], A["ffn_in"][l, j, f, 1]]
            if f > 0:
                out.append(A["ffn_out"][l, j, f - 1])
        return out

    tiles = ffn_tiles(0, 0) + tiles_of("w_r", "w_k", "w_v", "w_o") + ffn_tiles(0, 1) + tiles_of("w_kv")
    tiles += ffn_tiles(1, 0) + tiles_of("diff_w_q", "diff_w_o") + ffn_tiles(1, 1)
    tiles += tiles_of("in_q_a", "in_kv_a", "in_qk_b", "in_v_b", "in_gates", "up_swa", "up_sb", "w_out")
    tiles += tiles_of("peer_q", "peer_u", "peer_v")

    def load(dst, src, *after):
        S.wait(*after)
        s = sem(f"load_{dst.tensor.name}_{len(loads)}")
        scalar.dma_start(dst, src).then_inc(s, 16)
        loads.append(s)
        return (s, 16)

    def row(name, dst, *after):
        a = A[name]
        return load(dst, bass.AP(a.tensor, a.offset, [[0, P], [1, a.shape[1]]]), *after)

    def consts(name, dst, *after):
        a, b = const_at[name]
        return load(dst, A["consts"][:, a:b], *after)

    loads = []
    x_loaded = [load(x[:, tb, :], A["x"][tb]) for tb in range(TB)]
    cols_loaded = load(cols[:, :], A["cols"])
    ident_loaded = load(ident, A["consts"][:, 0:P])
    W = Weights(SP, raw, [sem(f"raw_{i}") for i in range(RAW_SLOTS)], tile_high, tile_low, S, V, tiles)
    banks = Banks(psum)
    half_ready = V.mark(vector.memset(minus_half[:, :], -0.5))
    G.wait(half_ready)
    S.wait(ident_loaded, cols_loaded)
    PE.wait(ident_loaded)
    V.wait(cols_loaded, ident_loaded)

    def rsqrt(ap, n, ready):
        G.wait(ready, half_ready)
        return G.mark(pool.tensor_tensor(ap, ap, minus_half[:, 0:n], ALU.pow))

    def transposed(src, tb, dst, ready, gain=None, scale=None, n=KC):
        last = None
        for c0 in range(0, n, 4):
            m = min(4, n - c0)
            PE.wait(ready)
            b, ps = banks.take(PE)
            for c in range(m):
                ins = tensor.transpose(ps[:, c * P:(c + 1) * P], src[:, (c0 + c) * P:(c0 + c + 1) * P], ident)
            turned = PE.mark(ins)
            dstv = dst[:, c0:c0 + m, tb * P:(tb + 1) * P]
            psv = ps[:, 0:m * P].rearrange("p (c t) -> p c t", t=P)
            if gain is not None:
                V.wait(turned)
                last = V.mark(vector.tensor_tensor(dstv, psv, spread(gain[:, c0:c0 + m], P), ALU.mult))
            elif scale is not None:
                V.wait(turned)
                last = V.mark(vector.tensor_scalar(dstv, psv, scale[0], scale[1], ALU.mult, ALU.mult))
            else:
                S.wait(turned)
                last = S.mark(scalar.activation(dstv, psv, ACT.Copy))
            banks.free(b, last)
        return last

    def split(high, low, source, ready):
        S.wait(ready)
        m = S.mark(scalar.activation(high, source, ACT.Copy))
        V.wait(m)
        return V.mark(vector.tensor_tensor(low, source, high.bitcast(F32), ALU.subtract))

    def transposed_split(src, tb, whole, ready, to=hT, at=0, n=KC, gain=None, scale=None):
        out = []
        for c0 in range(0, n, 4):
            m = transposed(src[:, c0 * P:(c0 + 4) * P], tb, whole[:, c0:c0 + 4, :], ready, n=4,
                           gain=None if gain is None else gain[:, c0:c0 + 4], scale=scale)
            part = (slice(None), slice(at + c0, at + c0 + 4), slice(tb * P, (tb + 1) * P))
            out.append(split(to[0][part], to[1][part], whole[:, c0:c0 + 4, tb * P:(tb + 1) * P], m))
        return out

    def norm(gain, ready, whole, xn):
        done = []
        for tb in range(TB):
            ss = small[:, tb:tb + 1]
            V.wait(ready[tb])
            m = V.mark(vector.scalar_tensor_tensor(out=xn[:, tb, :], in0=x[:, tb, :], scalar=1.0, in1=x[:, tb, :],
                                                   op0=ALU.mult, op1=ALU.mult, accum_out=ss))
            m = V.mark(vector.tensor_scalar(ss, ss, 1.0 / D, 1e-6, ALU.mult, ALU.add))
            m = rsqrt(ss, 1, m)
            V.wait(m)
            m = V.mark(vector.tensor_scalar(xn[:, tb, :], x[:, tb, :], ss, None, ALU.mult))
            done.append(transposed_split(xn[:, tb, :], tb, whole, m, gain=gain))
        return done

    def add_to_x(tb, n0, ps, factor, ready):
        V.wait(ready)
        xs = x[:, tb, n0:n0 + BANK]
        return V.mark(vector.scalar_tensor_tensor(out=xs, in0=ps, scalar=factor, in1=xs, op0=ALU.mult, op1=ALU.add))

    def products(out, still, moving, first, last):
        tensor.matmul(out, still[0], moving[0], start=first, stop=False)
        tensor.matmul(out, still[0], moving[1], start=False, stop=False)
        return tensor.matmul(out, still[1], moving[0], start=False, stop=last)

    def at(pair, *index):
        return (pair[0][index], pair[1][index])

    EVERY = slice(None)

    def feature_major(ps, src, ready=None):
        high, low = W.take(PE)
        tile = tuple(t.rearrange("p (k n) -> p k n", k=KC) for t in (high, low))
        for k in range(KC):
            ins = products(ps, at(tile, EVERY, k, EVERY), at(src, EVERY, k, EVERY), k == 0, k == KC - 1)
        done = PE.mark(ins)
        W.release(done)
        return done

    def ffn(l, j, ready):
        with ExitStack() as room:
            scratch = sb(f"norm_{l}{j}", [P, 2, UNIT], room=room)
            BUFS = 3
            act = sb(f"hidden_{l}{j}", [P, BUFS, 2, T], room=room)
            high, low = (sb(f"hidden_{n}_{l}{j}", [P, BUFS, T], F32R, room) for n in ("high", "low"))
            fence()
            h_ready = norm(col("ffn_norm", 2 * l + j), ready, fm(scratch[:, 0, :]), tm(scratch[:, 1, :]))
            PE.wait(h_ready)
            banks.use(range(4, 8))
            PE.wait(banks.freed[0:4])
            hidden, down_done = {}, {}

            def gate_up(f):
                b, ps = banks.take(PE)
                feature_major(ps[:, 0:T], hT)
                done = feature_major(ps[:, T:2 * T], hT)
                s, n = act[:, f % BUFS, 1, :], f % BUFS
                S.wait(done)
                silu = S.mark(scalar.activation(s, ps[:, 0:T], ACT.Silu))
                V.wait(silu)
                m = V.mark(vector.tensor_tensor(act[:, n, 0, :], s, ps[:, T:2 * T], ALU.mult))
                banks.free(b, m)
                hidden[f] = split(high[:, n, :], low[:, n, :], act[:, n, 0, :], [m, down_done.get(f - BUFS)])

            def down(f):
                w = W.take(PE)
                PE.wait(hidden[f])
                for tb in range(TB):
                    part = at((high, low), EVERY, f % BUFS, slice(tb * P, (tb + 1) * P))
                    for half in range(2):
                        ins = products(psum[:, 2 * tb + half, :], part, at(w, EVERY, slice(half * BANK, (half + 1) * BANK)),
                                       f == 0, f == FC - 1)
                down_done[f] = PE.mark(ins)
                W.release(down_done[f])

            gate_up(0)
            for f in range(1, FC):
                gate_up(f)
                down(f - 1)
            down(FC - 1)
            out_marks = []
            for tb in range(TB):
                for half in range(2):
                    m = add_to_x(tb, half * BANK, psum[:, 2 * tb + half, :], 0.5, down_done[FC - 1])
                    banks.free(2 * tb + half, m)
                out_marks.append(m)
            banks.use(range(8))
        return out_marks

    def project_tokens(src, groups, evac, ready, kcs=KC, first=0):
        out = []
        PE.wait(ready)
        for g in range(groups):
            got = [banks.take(PE) for _ in range(TB)]
            for k0 in range(0, kcs, 2):
                tile = tuple(t.rearrange("p (k n) -> p k n", k=2) for t in W.take(PE))
                for tb in range(TB):
                    for k in range(2):
                        ins = products(got[tb][1], at(src, EVERY, first + k0 + k, slice(tb * P, (tb + 1) * P)),
                                       at(tile, EVERY, k, EVERY), k0 + k == 0, k0 + k == kcs - 1)
                done = PE.mark(ins)
                W.release(done)
            for tb in range(TB):
                m = evac(tb, g, got[tb][1], done)
                banks.free(got[tb][0], m)
                out.append(m)
        return out

    def project_features(src, groups, evac, ready):
        out = []
        PE.wait(ready)
        for g in range(groups):
            b, ps = banks.take(PE)
            feature_major(ps[:, 0:T], src)
            done = feature_major(ps[:, T:2 * T], src)
            m = evac(g, ps, done)
            banks.free(b, m)
            out.append(m)
        return out

    def fence():
        now = [(lane.semaphore, lane.count) for lane in (PE, V, S, G) if lane.count]
        for lane in (V, S, G):
            lane.wait(now)

    def finish(ready):
        for tb in range(TB):
            s = sem(f"stored_{tb}")
            SP.wait(ready[tb])
            sync.dma_start(out[tb], x[:, tb, :]).then_inc(s, 16)
            sync.wait_ge(s, 16)

    env = Core()
    env.PE, env.V, env.S, env.G, env.W = PE, V, S, G, W
    env.A, env.banks, env.psum, env.sb, env.sem = A, banks, psum, sb, sem
    env.fm, env.tm, env.col, env.small, env.const_at = fm, tm, col, small, const_at
    env.ident, env.hT, env.tensor, env.vector, env.scalar = ident, hT, tensor, vector, scalar
    env.pool, env.spread, env.across, env.load, env.row = pool, spread, across, load, row
    env.norm, env.split, env.fence, env.at, env.products = norm, split, fence, at, products
    env.feature_major, env.transposed, env.transposed_split, env.rsqrt, env.add_to_x = feature_major, transposed, transposed_split, rsqrt, add_to_x
    env.project_tokens, env.project_features = project_tokens, project_features
    x_ready = ffn(0, 0, x_loaded)
    x_ready = rwkv(env, x_ready)
    x_ready = ffn(0, 1, x_ready)
    kv_room = ExitStack()
    shared, kv_ready = shared_kv(env, x_ready, kv_room)
    x_ready = ffn(1, 0, x_ready)
    x_ready = diff_attention(env, x_ready, shared, kv_ready)
    kv_room.close()
    x_ready = ffn(1, 1, x_ready)
    x_ready = mix_2(env, x_ready)
    x_ready = experts(env, x_ready)
    finish(x_ready)


def rwkv(k, x_ready):
    PE, V, S, G, banks, fm, col = k.PE, k.V, k.S, k.G, k.banks, k.fm, k.col
    tensor, vector, scalar, pool, spread, across = k.tensor, k.vector, k.scalar, k.pool, k.spread, k.across
    blk = lambda buffer: buffer.rearrange("p (c t) -> p c t", t=P)

    room, early = ExitStack(), ExitStack()
    arena = k.sb("rwkv", [P, 15, UNIT], room=room)
    masks = k.sb("masks", [P, 10 * P], room=room)
    other = tuple(k.sb(f"mixed_{n}", [P, KC, T], F32R, early) for n in ("high", "low"))
    k.fence()

    def unit(i):
        return arena[:, i, :]

    h, dx, whole = fm(unit(0)), fm(unit(14)), fm(unit(1))
    mixed = [k.hT, other]
    rT, kT, aT, sig = fm(unit(2)), fm(unit(3)), fm(unit(4)), fm(unit(5))
    v_tok, g_tok = k.tm(unit(6)), k.tm(unit(7))
    kk = fm(unit(8))

    w_in, w_g1, w_lo, w_g2 = unit(10)[:, 0:KC * P], unit(11)[:, 0:KC * 160], unit(12)[0:64, :], unit(13)
    A = k.A
    masks_ready = k.load(masks[:, :], A["consts"][:, 2 * P:12 * P])
    in_loaded = k.load(w_in, A["lora_in"])
    g1_loaded = k.load(w_g1, A["g1"])
    lo_loaded = k.load(w_lo, A["lora_out"])
    g2_loaded = [k.load(w_g2[:, 0:D], A["g2"][0:P, :]), k.load(w_g2[0:32, D:2 * D], A["g2"][P:160, :])]
    w_in = w_in.rearrange("p (k n) -> p k n", n=P)
    w_g1 = w_g1.rearrange("p (k n) -> p k n", n=160)
    h_ready = k.norm(col("mix_norm", 0), x_ready, h, k.tm(unit(9)))
    mask = lambda n: masks[:, n * P:(n + 1) * P]
    strict, upto, pair_t = mask(0), mask(1), mask(2)
    level = [mask(3 + n) for n in range(LEVELS)]
    mid, end = k.small[:, 16:32], k.small[:, 32:48]
    carry_scale, stats = k.small[:, 48:56], k.small[:, 64:128]
    bonus = k.small[:, 128:160]
    a_sel, b_sel = k.const_at["headsel"]

    V.wait(h_ready)
    V.mark(vector.tensor_tensor(dx[:, :, 1:T], h[:, :, 0:T - 1], h[:, :, 1:T], ALU.subtract))
    dx_ready = V.mark(vector.tensor_scalar(dx[:, :, 0:1], h[:, :, 0:1], -1.0, None, ALU.mult))
    mixed_read, whole_read = [None, None], [None]

    def mix(n):
        mu = col("mu", n)
        V.wait(dx_ready, whole_read[0])
        for c in range(KC):
            m = V.mark(vector.scalar_tensor_tensor(out=whole[:, c, :], in0=dx[:, c, :], scalar=mu[:, c:c + 1],
                                                   in1=h[:, c, :], op0=ALU.mult, op1=ALU.add))
        return m

    def mix_split(n, slot):
        m = mix(n)
        return k.split(mixed[slot][0][:, :, :], mixed[slot][1][:, :, :], whole, [m, mixed_read[slot]])

    hidden_w, hidden_a = unit(9)[0:64, 0:T], unit(9)[0:64, T:2 * T]
    hidden_g, hidden_g2 = unit(9)[:, 2 * T:3 * T], unit(9)[0:32, 3 * T:4 * T]

    def low_rank(weights, width, dst, func, *ready):
        b, ps = banks.take(PE)
        PE.wait(*ready)
        for c in range(KC):
            ins = tensor.matmul(ps[0:width, 0:T], weights(c), whole[:, c, :], start=(c == 0), stop=(c == KC - 1))
        done = PE.mark(ins)
        whole_read[0] = done
        S.wait(done)
        m = S.mark(scalar.activation(dst, ps[0:width, 0:T], func))
        banks.free(b, m)
        return m

    w_hidden = low_rank(lambda c: w_in[:, c, 0:64], 64, hidden_w, ACT.Tanh, mix(3), in_loaded)
    a_hidden = low_rank(lambda c: w_in[:, c, 64:P], 64, hidden_a, ACT.Copy, mix(4), in_loaded)
    ready = mix(5)
    g_hidden = [low_rank(lambda c: w_g1[:, c, 0:P], P, hidden_g, ACT.Sigmoid, ready, g1_loaded),
                low_rank(lambda c: w_g1[:, c, P:160], 32, hidden_g2, ACT.Sigmoid, ready, g1_loaded)]
    first_mix = mix_split(0, 1)
    for hidden, what, base, at, dst in ((w_hidden, hidden_w, "w0", 0, sig), (a_hidden, hidden_a, "a0", D, aT)):
        for c in range(0, KC, 2):
            b, ps = banks.take(PE)
            PE.wait(hidden, lo_loaded)
            for i in range(2):
                ins = tensor.matmul(ps[:, i * T:(i + 1) * T], w_lo[0:64, at + (c + i) * P:at + (c + i + 1) * P], what,
                                    start=True, stop=True)
            lo_read = PE.mark(ins)
            S.wait(lo_read)
            for i in range(2):
                a_ready = S.mark(scalar.activation(dst[:, c + i, :], ps[:, i * T:(i + 1) * T], ACT.Sigmoid,
                                                   bias=col(base)[:, c + i:c + i + 1]))
            banks.free(b, a_ready)
        if base == "w0":
            sig_ready = a_ready

    def to_tokens(dst):
        def evac(tb, g, ps, ready):
            S.wait(ready)
            return S.mark(scalar.activation(dst[:, tb, g * BANK:(g + 1) * BANK], ps, ACT.Copy))
        return evac

    g_ready = []
    for tb in range(TB):
        for g in range(2):
            b, ps = banks.take(PE)
            PE.wait(g_hidden, g2_loaded)
            tensor.matmul(ps, hidden_g[:, tb * P:(tb + 1) * P], w_g2[:, g * BANK:(g + 1) * BANK], start=True, stop=False)
            ins = tensor.matmul(ps, hidden_g2[:, tb * P:(tb + 1) * P], w_g2[0:32, D + g * BANK:D + (g + 1) * BANK],
                                start=False, stop=True)
            g2_read = PE.mark(ins)
            g_ready.append(to_tokens(g_tok)(tb, g, ps, g2_read))
            banks.free(b, g_ready[-1])

    def to(dst):
        def evac(g, ps, ready):
            S.wait(ready)
            return S.mark(scalar.activation(dst[:, 2 * g:2 * g + 2, :], ps.rearrange("p (c t) -> p c t", t=T), ACT.Copy))
        return evac

    r_ready = k.project_features(mixed[1], 4, to(rT), first_mix)
    mixed_read[1] = (PE.semaphore, PE.count)
    ready_k = mix_split(1, 0)

    sums, centred, before = unit(9), unit(10), unit(11)
    keep = unit(12)
    at = k.const_at["scan_keep"]
    keep_row = k.load(keep[:, 0:P], A["consts"][:, at[0]:at[1]], lo_read)
    V.wait(keep_row, sig_ready)
    m = V.mark(vector.tensor_copy(blk(keep)[:, 1:16, :], across(keep[:, 0:P], 15)))
    V.wait(m, g2_read)
    m = V.mark(vector.tensor_tensor_scan(sums, keep, unit(5), 0.0, ALU.mult, ALU.add))
    ready_v = mix_split(2, 1)
    k_proj = k.project_features(mixed[0], 4, to(kT), ready_k)
    v_ready = k.project_tokens(mixed[1], 2, to_tokens(v_tok), ready_v)
    early.close()
    late = k.sb("late", [P, 2, UNIT], room=room)

    V.wait(m)
    V.mark(vector.tensor_copy(mid, blk(sums)[:, :, P // 2 - 1]))
    m = V.mark(vector.tensor_copy(end, blk(sums)[:, :, P - 1]))
    V.wait(m)
    m = V.mark(vector.tensor_tensor(blk(centred), blk(sums), spread(mid, P), ALU.subtract))
    V.wait(m)
    m = V.mark(vector.tensor_tensor(before, centred, unit(5), ALU.subtract))
    mid_b, end_b = mid.rearrange("p (c b) -> p c b", b=TB), end.rearrange("p (c b) -> p c b", b=TB)
    V.mark(vector.tensor_tensor(carry_scale, end_b[:, :, 0], mid_b[:, :, 0], ALU.subtract))
    V.wait((V.semaphore, V.count))
    m = V.mark(vector.tensor_tensor(carry_scale, carry_scale, mid_b[:, :, 1], ALU.add))
    S.wait(m)
    p_in, p_before, p_inv = unit(9), unit(11), unit(12)
    S.mark(scalar.activation(p_in, centred, ACT.Exp, scale=-DECAY))
    S.mark(scalar.activation(p_before, before, ACT.Exp, scale=-DECAY))
    S.mark(scalar.activation(carry_scale, carry_scale, ACT.Exp, scale=-DECAY))
    p_ready = S.mark(scalar.activation(p_inv, centred, ACT.Exp, scale=DECAY))

    V.wait(k_proj, r_ready)
    m = V.mark(vector.tensor_tensor(kk, kT, spread(col("k_k"), T), ALU.mult))
    V.wait(m)
    square, norms = unit(13), unit(14)
    m = V.mark(vector.tensor_tensor(square, unit(8), unit(8), ALU.mult))
    headsum = unit(0)[:, P:2 * P]
    at = k.const_at["headsum"]
    headsum_ready = k.load(headsum, A["consts"][:, at[0]:at[1]], ready_v)
    for c in range(0, KC, 2):
        b, ps = banks.take(PE)
        PE.wait(m, headsum_ready)
        m2 = PE.mark(tensor.matmul(ps, headsum, square[:, c * T:(c + 2) * T], start=True, stop=True))
        V.wait(m2)
        norm_in = V.mark(vector.tensor_scalar(norms[:, c * T:(c + 2) * T], ps, 1e-24, None, ALU.max))
        banks.free(b, norm_in)
    S.wait(norm_in)
    m = S.mark(scalar.activation(norms, norms, ACT.Sqrt))
    V.wait(a_ready, norm_in)
    rate = fm(unit(13))
    m3 = V.mark(vector.scalar_tensor_tensor(out=rate, in0=aT, scalar=-1.0, in1=spread(col("k_a"), T), op0=ALU.add,
                                            op1=ALU.mult))
    V.wait(m3)
    m3 = V.mark(vector.scalar_tensor_tensor(out=kT, in0=rate, scalar=1.0, in1=kT, op0=ALU.add, op1=ALU.mult))
    V.wait(m)
    m = V.mark(vector.reciprocal(norms, norms))
    V.wait(m)
    m = V.mark(vector.tensor_tensor(unit(8), unit(8), norms, ALU.mult))
    kk_ready = m
    V.wait(m3)
    rk = fm(unit(14))
    m = V.mark(vector.tensor_tensor(rk, rT, kT, ALU.mult))
    V.wait(m)
    m = V.mark(vector.tensor_tensor(rk, rk, spread(col("r_k"), T), ALU.mult))
    sel_ready = k.load(unit(0)[:, 0:KC * HEADS], k.A["consts"][:, a_sel:b_sel])
    sel = unit(0)[:, 0:KC * HEADS].rearrange("p (c h) -> p c h", h=HEADS)
    b, ps = banks.take(PE)
    PE.wait(m, sel_ready)
    for tb in range(TB):
        for c in range(KC):
            ins = tensor.matmul(ps[:, tb * HEADS:(tb + 1) * HEADS], rk[:, c, tb * P:(tb + 1) * P], sel[:, c, :],
                                start=(c == 0), stop=(c == KC - 1))
    bonus_done = PE.mark(ins)
    V.wait(p_ready, kk_ready)
    V.mark(vector.tensor_tensor(unit(2), unit(2), p_in, ALU.mult))
    V.mark(vector.tensor_tensor(unit(4), unit(4), unit(8), ALU.mult))
    V.mark(vector.tensor_tensor(unit(4), unit(4), p_inv, ALU.mult))
    V.mark(vector.tensor_tensor(unit(3), unit(3), p_inv, ALU.mult))
    scaled = V.mark(vector.scalar_tensor_tensor(out=unit(8), in0=unit(8), scalar=-1.0, in1=p_before, op0=ALU.mult,
                                                op1=ALU.mult))
    V.wait(bonus_done)
    bonus_ready = V.mark(vector.tensor_copy(bonus, ps[:, 0:TB * HEADS]))
    banks.free(b, bonus_ready)
    r_s, a_s, b_s, k_s = rT, kk, aT, kT

    b_tok, k_tok = unit(1)[:, 0:D], unit(1)[:, D:2 * D]
    for src, dst in ((b_s, b_tok), (k_s, k_tok)):
        for c0 in (0, 4):
            b, ps = banks.take(PE)
            PE.wait(scaled)
            for c in range(4):
                ins = tensor.transpose(ps[:, c * P:(c + 1) * P], src[:, c0 + c, 0:P], k.ident)
            m = PE.mark(ins)
            S.wait(m)
            tok_ready = S.mark(scalar.activation(dst[:, c0 * P:(c0 + 4) * P], ps, ACT.Copy))
            banks.free(b, tok_ready)

    ln = [late[:, 1, 0:D], late[:, 1, D:2 * D]]
    ln_ready = k.row("ln", late[:, 1, :], (PE.semaphore, PE.count))
    heads4 = lambda buffer, g: buffer[:, g * 4 * P:(g + 1) * 4 * P].rearrange("p (h t) -> p h t", t=P)
    MT, TI, TIT, X = unit(9), unit(10), unit(11), unit(12)
    MAK, MRB, MRK = unit(13), unit(14), unit(0)
    wbuf, ubuf = late[:, 0, 0:D], late[:, 0, D:2 * D]
    y, y2 = unit(5)[:, 0:D], unit(5)[:, D:2 * D]
    y_whole = fm(unit(10))
    read_before = [scaled, (PE.semaphore, PE.count), bonus_ready]

    def pair(c, h, tb, buffer):
        return buffer[h * HD:(h + 1) * HD, c, tb * P:(tb + 1) * P]

    S0 = unit(1)[:, 0:D]
    y_ready, state_ready = [], None
    for tb in range(TB):
        tit_ready = {}
        ti_ready, mt_ready = {}, {}

        def products(pair_of_groups, lhs, rhs):
            got = [banks.take(PE), banks.take(PE)]
            PE.wait(scaled)
            for i in range(4):
                for h in range(2):
                    c = 4 * pair_of_groups + i
                    ins = tensor.matmul(got[h][1][:, i * P:(i + 1) * P], pair(c, h, tb, lhs), pair(c, h, tb, rhs),
                                        start=True, stop=True)
            done = PE.mark(ins)
            return [(2 * pair_of_groups + h, got[h][0], got[h][1].rearrange("p (h t) -> p h t", t=P), done)
                    for h in range(2)]

        for gg in range(2):
            for g, b, ps, done in products(gg, a_s, b_s):
                V.wait(done, read_before)
                m = V.mark(vector.tensor_tensor(heads4(TI, g), ps, across(level[0], 4), ALU.mult))
                banks.free(b, m)
                G.wait(m)
                ti_ready[g] = G.mark(pool.tensor_tensor(heads4(TI, g), heads4(TI, g), across(k.ident, 4), ALU.add))
            for g, b, ps, done in products(gg, b_s, a_s):
                S.wait(done, read_before)
                mt_ready[g] = S.mark(scalar.activation(heads4(MT, g), ps, ACT.Copy))
                V.wait(mt_ready[g])
                m = V.mark(vector.tensor_tensor(heads4(TIT, g), ps, across(pair_t, 4), ALU.mult))
                banks.free(b, m)
                G.wait(m)
                tit_ready[g] = G.mark(pool.tensor_tensor(heads4(TIT, g), heads4(TIT, g), across(k.ident, 4), ALU.add))
            for dst, lhs, rhs, msk in ((MAK, k_s, a_s, strict), (MRB, b_s, r_s, upto), (MRK, k_s, r_s, upto)):
                for g, b, ps, done in products(gg, lhs, rhs):
                    V.wait(done)
                    masked = V.mark(vector.tensor_tensor(heads4(dst, g), ps, across(msk, 4), ALU.mult))
                    banks.free(b, masked)

        for n in range(1, LEVELS):
            x_done = {}
            for g in range(4):
                b, ps = banks.take(PE)
                PE.wait(mt_ready[g], ti_ready[g])
                for i in range(4):
                    ins = tensor.matmul(ps[:, i * P:(i + 1) * P], heads4(MT, g)[:, i, :], heads4(TI, g)[:, i, :],
                                        start=True, stop=True)
                done = PE.mark(ins)
                V.wait(done, tit_ready[g])
                x_done[g] = V.mark(vector.tensor_tensor(heads4(X, g), ps.rearrange("p (h t) -> p h t", t=P),
                                                        across(level[n], 4), ALU.mult))
                banks.free(b, x_done[g])
            for g in range(4):
                old_t, old_tt = ti_ready[g], tit_ready[g]
                b, ps = banks.take(PE)
                b2, ps2 = banks.take(PE)
                PE.wait(x_done[g], old_t, old_tt)
                for i in range(4):
                    ins = tensor.matmul(ps[:, i * P:(i + 1) * P], heads4(X, g)[:, i, :], heads4(TIT, g)[:, i, :],
                                        start=True, stop=True)
                if n < LEVELS - 1:
                    for i in range(4):
                        ins = tensor.matmul(ps2[:, i * P:(i + 1) * P], heads4(TIT, g)[:, i, :], heads4(X, g)[:, i, :],
                                            start=True, stop=True)
                done = PE.mark(ins)
                V.wait(done)
                tit_ready[g] = V.mark(vector.tensor_tensor(heads4(TIT, g), ps.rearrange("p (h t) -> p h t", t=P),
                                                           heads4(TIT, g), ALU.add))
                banks.free(b, tit_ready[g])
                if n < LEVELS - 1:
                    ti_ready[g] = V.mark(vector.tensor_tensor(heads4(TI, g), ps2.rearrange("p (h t) -> p h t", t=P),
                                                              heads4(TI, g), ALU.add))
                banks.free(b2, ti_ready[g] if n < LEVELS - 1 else tit_ready[g])

        def per_head(terms, dst, ready):
            last = None
            for half in range(2):
                b, ps = banks.take(PE)
                PE.wait(ready)
                for i in range(8):
                    head = 8 * half + i
                    todo = terms(head)
                    for j, (lhs, rhs) in enumerate(todo):
                        ins = tensor.matmul(ps[:, i * HD:(i + 1) * HD], lhs, rhs, start=(j == 0),
                                            stop=(j == len(todo) - 1))
                done = PE.mark(ins)
                S.wait(done)
                last = S.mark(scalar.activation(dst[:, half * BANK:(half + 1) * BANK], ps, ACT.Copy))
                banks.free(b, last)
            return last

        def mat(buffer, head):
            c, h = head // 2, head % 2
            at = (2 * (c // 4) + h) * 4 + c % 4
            return buffer[:, at * P:(at + 1) * P]

        hd = lambda buffer, head: buffer[:, head * HD:(head + 1) * HD]

        def carried(scaled_rows, head):
            if tb == 0:
                return []
            return [(scaled_rows[:, head // 2, tb * P:(tb + 1) * P], hd(S0, head))]

        w_ready = per_head(lambda n: [(mat(MAK, n), hd(v_tok[:, tb, :], n))] + carried(a_s, n), wbuf,
                           [masked, state_ready, v_ready])
        u_ready = per_head(lambda n: [(mat(TIT, n), hd(wbuf, n))], ubuf, [w_ready, list(tit_ready.values())])
        done_y = per_head(lambda n: [(mat(MRB, n), hd(ubuf, n)), (mat(MRK, n), hd(v_tok[:, tb, :], n))]
                          + carried(r_s, n), y, [u_ready, masked])
        if tb == 0:
            b, ps = banks.take(PE)
            PE.wait(tok_ready)
            for head in range(HEADS):
                c, h = head // 2, head % 2
                dst = ps[h * HD:(h + 1) * HD, c * HD:(c + 1) * HD]
                tensor.matmul(dst, hd(b_tok, head), hd(ubuf, head), start=True, stop=False)
                ins = tensor.matmul(dst, hd(k_tok, head), hd(v_tok[:, 0, :], head), start=False, stop=True)
            m = PE.mark(ins)
            V.wait(m, p_ready)
            V.mark(vector.memset(S0, 0.0))
            for h in range(2):
                half = slice(h * HD, (h + 1) * HD)
                state_ready = V.mark(vector.tensor_tensor(
                    S0[half, :].rearrange("p (c h i) -> p c h i", h=2, i=HD)[:, :, h, :],
                    ps[half, :].rearrange("p (c i) -> p c i", i=HD),
                    carry_scale[half, :].unsqueeze(2).to_broadcast([HD, KC, HD]), ALU.mult))
            banks.free(b, state_ready)
        read_before = [(PE.semaphore, PE.count)]

        byhead = lambda buffer: buffer.rearrange("p (h i) -> p h i", i=HD)
        mean, var = stats[:, 0:HEADS], stats[:, HEADS:2 * HEADS]
        V.wait(done_y, v_ready, g_ready, ln_ready)
        m = V.mark(vector.tensor_reduce(mean, byhead(y), AX.X, ALU.add))
        V.wait(m)
        m = V.mark(vector.tensor_scalar(mean, mean, 1.0 / HD, None, ALU.mult))
        V.wait(m)
        m = V.mark(vector.tensor_tensor(byhead(y), byhead(y), spread(mean, HD), ALU.subtract))
        V.wait(m)
        m = V.mark(vector.tensor_tensor(y2, y, y, ALU.mult))
        V.wait(m)
        m = V.mark(vector.tensor_reduce(var, byhead(y2), AX.X, ALU.add))
        V.wait(m)
        m = V.mark(vector.tensor_scalar(var, var, 1.0 / HD, 64e-5, ALU.mult, ALU.add))
        m = k.rsqrt(var, HEADS, m)
        V.wait(m)
        m = V.mark(vector.tensor_tensor(byhead(y), byhead(y), spread(var, HD), ALU.mult))
        V.wait(m)
        m = V.mark(vector.tensor_tensor(y, y, ln[0], ALU.mult))
        V.mark(vector.tensor_tensor(byhead(y2), byhead(v_tok[:, tb, :]),
                                    spread(bonus[:, tb * HEADS:(tb + 1) * HEADS], HD), ALU.mult))
        V.wait(m)
        m = V.mark(vector.tensor_tensor(y, y, ln[1], ALU.add))
        V.wait(m)
        m = V.mark(vector.tensor_tensor(y, y, y2, ALU.add))
        V.wait(m)
        m = V.mark(vector.tensor_tensor(y, y, g_tok[:, tb, :], ALU.mult))
        y_ready.append(k.transposed_split(y, tb, y_whole, m))

    out = {}

    def evac(tb, g, ps, ready):
        out[tb] = k.add_to_x(tb, g * BANK, ps, 1.0, ready)
        return out[tb]
    k.project_tokens(k.hT, 2, evac, y_ready)
    room.close()
    return [out[0], out[1]]


def head_norm(k, buffer, heads, eps, square, ss, ready, width=HD):
    V, vector = k.V, k.vector
    by_head = lambda b: b.rearrange("p (h i) -> p h i", i=width)
    V.wait(ready)
    m = V.mark(vector.tensor_tensor(square, buffer, buffer, ALU.mult))
    V.wait(m)
    m = V.mark(vector.tensor_reduce(ss, by_head(square), AX.X, ALU.add))
    V.wait(m)
    m = V.mark(vector.tensor_scalar(ss, ss, 1.0 / width, eps, ALU.mult, ALU.add))
    m = k.rsqrt(ss, heads, m)
    V.wait(m)
    return V.mark(vector.tensor_tensor(by_head(buffer), by_head(buffer), k.spread(ss, width), ALU.mult))


def shared_kv(k, x_ready, keep):
    V, S, fm, tm, scalar = k.V, k.S, k.fm, k.tm, k.scalar
    shared = k.sb("shared_kv", [P, 2, UNIT], room=keep)
    kT, v_tok = fm(shared[:, 0, :]), tm(shared[:, 1, :])
    with ExitStack() as room:
        scratch = k.sb("kv_scratch", [P, 3, UNIT], room=room)
        k.fence()
        h_ready = k.norm(k.col("kv_norm"), x_ready, fm(scratch[:, 0, :]), tm(scratch[:, 1, :]))
        k_tok = tm(scratch[:, 2, :])

        def evac(tb, g, ps, ready):
            dst = k_tok if g < 2 else v_tok
            S.wait(ready)
            return S.mark(scalar.activation(dst[:, tb, g % 2 * BANK:(g % 2 + 1) * BANK], ps, ACT.Copy))
        marks = k.project_tokens(k.hT, 4, evac, h_ready)
        out = []
        for tb in range(TB):
            m = head_norm(k, k_tok[:, tb, :], HEADS, 1e-6, scratch[:, 0, 0:D], k.small[:, 64:64 + HEADS], marks[3])
            out.append(k.transposed(k_tok[:, tb, :], tb, kT, m, scale=(k.col("k_norm", 0, 1), 1.0)))
    return (kT, v_tok), out + [marks[-1]]


def softmax_attention(k, units, scores, soften, values, turned_at):
    PE, S, banks, tensor, scalar = k.PE, k.S, k.banks, k.tensor, k.scalar
    softened, out = {}, []
    lag = 2
    for i in range(len(units) + lag):
        if i < len(units):
            softened[i] = soften(i, units[i], *scores(units[i]))
        if i >= lag:
            n = i - lag
            weights, keys, ready = softened.pop(n)
            b, ps = banks.take(PE)
            PE.wait(ready)
            for c in range(keys // P):
                ins = tensor.transpose(ps[:, c * P:(c + 1) * P], weights[:, c * P:(c + 1) * P], k.ident)
            done = PE.mark(ins)
            turned = turned_at[:, (n % 4) * BANK:(n % 4) * BANK + keys]
            S.wait(done)
            m = S.mark(scalar.activation(turned, ps[:, 0:keys], ACT.Copy))
            banks.free(b, m)
            out.append(values(n, units[n], turned.rearrange("p (c q) -> p c q", q=P), m))
    return out


def diff_attention(k, x_ready, shared, kv_ready):
    PE, V, S, banks, fm, tm = k.PE, k.V, k.S, k.banks, k.fm, k.tm
    tensor, vector, scalar, hT = k.tensor, k.vector, k.scalar, k.hT
    room = ExitStack()
    arena = k.sb("differential", [P, 10, UNIT], room=room)
    dist = k.sb("causal_dist", [P, 3 * P], room=room)[:, :]
    k.fence()

    def unit(i):
        return arena[:, i, :]
    lam_init = 0.8 - 0.6 * math.exp(-0.3 * 1)
    kT, v_tok = shared
    h_ready = k.norm(k.col("mix_norm", 1), x_ready, fm(unit(0)), tm(unit(1)))
    a0 = k.const_at["causal_dist"][0]
    dist_ready = k.load(dist, k.A["consts"][:, a0:a0 + 3 * P], x_ready)

    lam = unit(3)[:, 0:4 * HD]
    lam_loaded = k.row("lam", lam, x_ready)
    sums, neg_lam = k.small[:, 16:18], k.small[:, 18:19]
    V.wait(lam_loaded)
    pairs = lam.rearrange("p (a b i) -> p a b i", a=2, b=2)
    V.mark(vector.tensor_tensor(unit(3)[:, BANK:BANK + 2 * HD].rearrange("p (a i) -> p a i", a=2), pairs[:, :, 0, :],
                                pairs[:, :, 1, :], ALU.mult))
    m = V.mark(vector.tensor_reduce(sums, unit(3)[:, BANK:BANK + 2 * HD].rearrange("p (a i) -> p a i", a=2), AX.X,
                                    ALU.add))
    S.wait(m)
    m = S.mark(scalar.activation(sums, sums, ACT.Exp))
    V.wait(m)
    V.mark(vector.tensor_tensor(neg_lam, sums[:, 1:2], sums[:, 0:1], ALU.subtract))
    lam_ready = V.mark(vector.tensor_scalar(neg_lam, neg_lam, lam_init, None, ALU.subtract))

    q_tok, qT = tm(unit(1)), fm(unit(4))

    def evac_q(tb, g, ps, ready):
        S.wait(ready)
        return S.mark(scalar.activation(q_tok[:, tb, g * BANK:(g + 1) * BANK], ps, ACT.Copy))
    marks = k.project_tokens(hT, 2, evac_q, h_ready)
    q_ready = []
    for tb in range(TB):
        m = head_norm(k, q_tok[:, tb, :], HEADS, 1e-6, unit(2)[:, 0:D], k.small[:, 64:64 + HEADS], marks)
        q_ready.append(k.transposed(q_tok[:, tb, :], tb, qT, m, scale=(k.col("q_norm", 0, 1), HD ** -0.5)))

    work = lambda i: unit(5 + i % 4)
    o_tok = tm(unit(1))
    stat = lambda i: k.small[:, 64 + 8 * (i % 4):72 + 8 * (i % 4)]
    attn_read = {}

    def scores(u):
        h, qb = u
        n = (qb + 1) * P
        got = [banks.take(PE), banks.take(PE)]
        PE.wait(q_ready, kv_ready)
        for m in range(2):
            rows = slice(m * HD, (m + 1) * HD)
            ins = tensor.matmul(got[m][1][:, 0:n], qT[rows, h, qb * P:(qb + 1) * P], kT[rows, h, 0:n], start=True,
                                stop=True)
        return got, n, PE.mark(ins)

    def soften(i, u, got, n, ready):
        h, qb = u
        s = work(i)[:, 0:2 * T].rearrange("p (m k) -> p m k", m=2)[:, :, 0:n]
        st = stat(i)
        V.wait(ready, dist_ready, lam_ready, attn_read.get(i - 4))
        slope = 2.0 ** (-8.0 * (h + 1) / DH)
        for m in range(2):
            done = V.mark(vector.scalar_tensor_tensor(out=s[:, m, :], in0=dist[:, qb * P:qb * P + n], scalar=slope,
                                                      in1=got[m][1][:, 0:n], op0=ALU.mult, op1=ALU.add))
            banks.free(got[m][0], done)
        top = V.mark(vector.tensor_reduce(st[:, 0:2], s, AX.X, ALU.max, negate=True))
        S.wait(top)
        for m in range(2):
            e = S.mark(scalar.activation(s[:, m, :], s[:, m, :], ACT.Exp, bias=st[:, m:m + 1],
                                         accum_out=st[:, 2 + m:3 + m]))
        V.wait(e)
        V.mark(vector.reciprocal(st[:, 4:6], st[:, 2:4]))
        V.mark(vector.tensor_scalar(s[:, 1, :], s[:, 1, :], st[:, 5:6], neg_lam, ALU.mult, ALU.mult))
        out = work(i)[:, 2 * T:2 * T + n]
        m = V.mark(vector.scalar_tensor_tensor(out=out, in0=s[:, 0, :], scalar=st[:, 4:5], in1=s[:, 1, :],
                                               op0=ALU.mult, op1=ALU.add))
        return out, n, m

    def values(i, u, turned, ready):
        h, qb = u
        b, ps = banks.take(PE)
        PE.wait(ready)
        attn_read[i] = (PE.semaphore, PE.count)
        for c in range(qb + 1):
            ins = tensor.matmul(ps[:, 0:P], turned[:, c, :], v_tok[:, c, h * P:(h + 1) * P], start=(c == 0),
                                stop=(c == qb))
        done = PE.mark(ins)
        S.wait(done)
        m = S.mark(scalar.activation(o_tok[:, qb, h * P:(h + 1) * P], ps[:, 0:P], ACT.Copy))
        banks.free(b, m)
        return m

    done = softmax_attention(k, [(h, qb) for h in range(DH) for qb in range(TB)], scores, soften, values, unit(9))
    o_ready = []
    for tb in range(TB):
        m = head_norm(k, o_tok[:, tb, :], DH, 1e-5, unit(2)[:, 0:D], k.small[:, 64:64 + DH], done, width=P)
        o_ready.append(k.transposed_split(o_tok[:, tb, :], tb, fm(unit(0)), m, scale=(k.col("subln", 0, 1), 1.0 - lam_init)))
    out = {}

    def evac(tb, g, ps, ready):
        out[tb] = k.add_to_x(tb, g * BANK, ps, 1.0, ready)
        return out[tb]
    k.project_tokens(hT, 2, evac, o_ready)
    room.close()
    return [out[0], out[1]]


def mix_2(k, x_ready):
    PE, V, S, W, banks, fm, tm = k.PE, k.V, k.S, k.W, k.banks, k.fm, k.tm
    tensor, vector, scalar, hT = k.tensor, k.vector, k.scalar, k.hT
    room = ExitStack()
    arena = k.sb("second_mix", [P, 15, UNIT], room=room)
    masks = k.sb("attention_masks", [P, 9 * P], room=room)
    k.fence()

    def unit(i):
        return arena[:, i, :]
    at = k.const_at
    window, before, before_neg = (masks[:, i * 3 * P:(i + 1) * 3 * P] for i in range(3))
    a = at["window_dist"][0]
    tables = k.load(masks[:, :], k.A["consts"][:, a:a + 9 * P], x_ready)
    bias = unit(0)
    bias_ready = k.row("gate_bias", bias, x_ready)
    sinks = k.small[:, 16:24]
    sinks_ready = k.row("sinks", sinks, x_ready)
    h_ready = k.norm(k.col("mix_gain_2"), x_ready, fm(unit(8)), tm(unit(9)))

    q_a, kv_a = unit(1).rearrange("p (b c) -> p b c", b=TB)[:, :, 0:BANK], unit(2)[:, 0:2 * T].rearrange(
        "p (b c) -> p b c", b=TB)
    k_dup = unit(2)[:, 2 * T:4 * T].rearrange("p (b g d i) -> p b g d i", b=TB, g=2, d=2)
    qbT, kbT = fm(unit(3))[:, 0:4, :], fm(unit(3))[:, 4:8, :]
    v_b = unit(4)[:, 0:D].rearrange("p (b c) -> p b c", b=TB)
    gates = [unit(5), unit(6)]
    qaT, kaT = fm(unit(7))[:, 0:4, :], fm(unit(7))[:, 4:6, :]

    def copy_to(dst, scale=None):
        def evac(tb, g, ps, ready):
            S.wait(ready)
            return S.mark(scalar.activation(dst[:, tb, :], ps, ACT.Copy))
        return evac
    qa_marks = k.project_tokens(hT, 1, copy_to(q_a), h_ready)
    got = [banks.take(PE) for _ in range(TB)]
    for k0 in range(0, KC, 4):
        tile = tuple(t.rearrange("p (k n) -> p k n", k=4) for t in W.take(PE))
        for tb in range(TB):
            for c in range(4):
                ins = k.products(got[tb][1][:, 0:T], k.at(hT, slice(None), k0 + c, slice(tb * P, (tb + 1) * P)),
                                 k.at(tile, slice(None), c, slice(None)), k0 + c == 0, k0 + c == KC - 1)
        done = PE.mark(ins)
        W.release(done)
    S.wait(done)
    for tb in range(TB):
        kva_ready = S.mark(scalar.activation(kv_a[:, tb, :], got[tb][1][:, 0:T], ACT.Copy))
        banks.free(got[tb][0], kva_ready)

    def evac_qk(g, ps, ready):
        S.wait(ready)
        src = ps.rearrange("p (c t) -> p c t", t=T)
        if g < 2:
            return S.mark(scalar.activation(qbT[:, 2 * g:2 * g + 2, :], src, ACT.Copy, scale=HD ** -0.5))
        return S.mark(scalar.activation(kbT[:, 2 * g - 4:2 * g - 2, :], src, ACT.Copy))
    qkb_ready = k.project_features(hT, 4, evac_qk, h_ready)
    vb_ready = k.project_tokens(hT, 1, copy_to(v_b), h_ready)

    qa_ready, ka_ready = [], []
    for tb in range(TB):
        m = head_norm(k, q_a[:, tb, :], 8, 1e-6, unit(8)[:, 0:BANK], k.small[:, 64:72], qa_marks)
        qa_ready.append(k.transposed(q_a[:, tb, :], tb, qaT, m, n=4, scale=(k.col("swa_q", 0, 1), HD ** -0.5)))
        m = head_norm(k, kv_a[:, tb, 0:P], 2, 1e-6, unit(8)[:, 0:P], k.small[:, 64:66], kva_ready)
        V.wait(m)
        for g in range(2):
            m = V.mark(vector.tensor_copy(k_dup[:, tb, g, :, :],
                                          k.across(kv_a[:, tb, g * HD:(g + 1) * HD], 2)))
        ka_ready.append(k.transposed(k_dup[:, tb, :, :, :].rearrange("p g d i -> p (g d i)"), tb, kaT, m, n=2,
                                     scale=(k.col("swa_k", 0, 1), 1.0)))

    def evac_gate(tb, g, ps, ready):
        V.wait(ready, bias_ready)
        dst = gates[tb][:, g * BANK:(g + 1) * BANK]
        m = V.mark(vector.tensor_tensor(dst, ps, bias[:, g * BANK:(g + 1) * BANK], ALU.add))
        S.wait(m)
        return S.mark(scalar.activation(dst, dst, ACT.Sigmoid)) and m
    k.project_tokens(hT, 4, evac_gate, h_ready)
    gates_ready = (S.semaphore, S.count)

    ya, yb = tm(unit(9))[:, :, 0:BANK], tm(unit(9))[:, :, BANK:D]
    work = lambda i: unit(10 + i % 4)
    stat = lambda i: k.small[:, 64 + 16 * (i % 4):80 + 16 * (i % 4)]
    units = [(c, qb) for c in range(4) for qb in range(TB)]
    read = {}

    def scores_of(qT, kT, kchunk, ready):
        def scores(u):
            c, qb = u
            n = (qb + 1) * P
            got = [banks.take(PE), banks.take(PE)]
            PE.wait(ready)
            for h in range(2):
                rows = slice(h * HD, (h + 1) * HD)
                ins = tensor.matmul(got[h][1][:, 0:n], qT[rows, c, qb * P:(qb + 1) * P], kT[rows, kchunk(c), 0:n],
                                    start=True, stop=True)
            return got, n, PE.mark(ins)
        return scores

    def soften_window(i, u, got, n, ready):
        c, qb = u
        s = work(i)[:, 0:2 * n].rearrange("p (h k) -> p h k", h=2)
        st = stat(i)
        V.wait(ready, tables, sinks_ready, read.get(i - 4))
        for h in range(2):
            slope = 2.0 ** (-8.0 * (2 * c + h + 1) / 8)
            done = V.mark(vector.scalar_tensor_tensor(out=s[:, h, :], in0=window[:, qb * P:qb * P + n], scalar=slope,
                                                      in1=got[h][1][:, 0:n], op0=ALU.mult, op1=ALU.add))
            banks.free(got[h][0], done)
        V.mark(vector.tensor_reduce(st[:, 0:2], s, AX.X, ALU.max))
        sink = sinks[:, 2 * c:2 * c + 2]
        V.mark(vector.tensor_tensor(st[:, 0:2], st[:, 0:2], sink, ALU.max))
        V.mark(vector.tensor_tensor(st[:, 2:4], sink, st[:, 0:2], ALU.subtract))
        m = V.mark(vector.tensor_scalar(st[:, 0:2], st[:, 0:2], -1.0, None, ALU.mult))
        S.wait(m)
        S.mark(scalar.activation(st[:, 2:4], st[:, 2:4], ACT.Exp))
        for h in range(2):
            m = S.mark(scalar.activation(s[:, h, :], s[:, h, :], ACT.Exp, bias=st[:, h:h + 1],
                                         accum_out=st[:, 4 + h:5 + h]))
        V.wait(m)
        V.mark(vector.tensor_tensor(st[:, 4:6], st[:, 4:6], st[:, 2:4], ALU.add))
        V.mark(vector.reciprocal(st[:, 4:6], st[:, 4:6]))
        for h in range(2):
            m = V.mark(vector.tensor_scalar(s[:, h, :], s[:, h, :], st[:, 4 + h:5 + h], None, ALU.mult))
        return work(i)[:, 0:2 * n], 2 * n, m

    def values_of(v, column, dst):
        def values(i, u, turned, ready):
            c, qb = u
            b, ps = banks.take(PE)
            PE.wait(ready)
            read[i] = (PE.semaphore, PE.count)
            blocks = qb + 1
            for h in range(2):
                for j in range(blocks):
                    at = column(2 * c + h)
                    ins = tensor.matmul(ps[:, h * HD:(h + 1) * HD], turned[:, h * blocks + j, :],
                                        v[:, j, at:at + HD], start=(j == 0), stop=(j == blocks - 1))
            done = PE.mark(ins)
            S.wait(done)
            m = S.mark(scalar.activation(dst[:, qb, 2 * c * HD:(2 * c + 2) * HD], ps[:, 0:P], ACT.Copy))
            banks.free(b, m)
            return m
        return values

    done_a = softmax_attention(k, units, scores_of(qaT, kaT, lambda c: c // 2, [qa_ready, ka_ready]), soften_window,
                               values_of(kv_a, lambda h: P + h // 4 * HD, ya), unit(14))

    def soften_stick(i, u, got, n, ready):
        c, qb = u
        z, e, lb, keep, total = (work(i)[:, j * 2 * T:j * 2 * T + 2 * n].rearrange("p (h k) -> p h k", h=2)
                                 for j in (0, 1, 2, 3, 3))
        pre = e
        V.wait(ready, tables, read.get(i - 4))
        for h in range(2):
            done = V.mark(vector.tensor_copy(z[:, h, :], got[h][1][:, 0:n]))
            banks.free(got[h][0], done)
        S.wait(done, (V.semaphore, V.count))
        S.mark(scalar.activation(e, z, ACT.Abs))
        S.mark(scalar.activation(e, e, ACT.Exp, scale=-1.0))
        m = S.mark(scalar.activation(e, e, ACT.Ln, bias=1.0))
        V.wait(m)
        V.mark(vector.scalar_tensor_tensor(out=lb, in0=z, scalar=0.0, in1=e, op0=ALU.min, op1=ALU.subtract))
        V.mark(vector.tensor_tensor(keep, lb, z, ALU.subtract))
        V.mark(vector.tensor_tensor(keep, keep, k.across(before[:, qb * P:qb * P + n], 2), ALU.mult))
        for h in range(2):
            V.mark(vector.tensor_tensor_scan(pre[:, h, :], keep[:, h, :], keep[:, h, :], 0.0, ALU.add, ALU.bypass))
        V.mark(vector.tensor_tensor(lb, lb, k.across(before_neg[:, qb * P:qb * P + n], 2), ALU.add))
        m = V.mark(vector.tensor_tensor(lb, lb, pre, ALU.subtract))
        S.wait(m)
        for h in range(2):
            m = S.mark(scalar.activation(lb[:, h, :], lb[:, h, :], ACT.Exp, bias=pre[:, h, n - 1:n]))
        return work(i)[:, 4 * T:4 * T + 2 * n], 2 * n, m

    read.clear()
    V.wait(done_a)
    done_b = softmax_attention(k, units, scores_of(qbT, kbT, lambda c: c, qkb_ready), soften_stick,
                               values_of(v_b, lambda h: h * HD, yb), unit(14))

    merged, part = tm(unit(8)), unit(10)[:, 0:BANK]
    whole = fm(unit(11))
    PE_done = (PE.semaphore, PE.count)
    ready = [done_a, done_b, PE_done]
    for y, first in ((ya, 0), (yb, 4)):
        for tb in range(TB):
            ready.append(k.transposed_split(y[:, tb, :], tb, whole, list(ready), at=first, n=4))

    def evac_a(tb, g, ps, ready):
        V.wait(ready, gates_ready)
        cols = slice(g * BANK, (g + 1) * BANK)
        return V.mark(vector.tensor_tensor(merged[:, tb, cols], ps, gates[tb][:, cols], ALU.mult))

    def evac_b(tb, g, ps, ready):
        V.wait(ready, gates_ready)
        cols = slice(g * BANK, (g + 1) * BANK)
        m = V.mark(vector.tensor_tensor(part, ps, gates[tb][:, D + g * BANK:D + (g + 1) * BANK], ALU.mult))
        V.mark(vector.tensor_tensor(merged[:, tb, cols], merged[:, tb, cols], part, ALU.add))
        return m
    k.project_tokens(hT, 2, evac_a, ready, kcs=4)
    k.project_tokens(hT, 2, evac_b, ready, kcs=4, first=4)
    merged_ready = (V.semaphore, V.count)
    ready = [k.transposed_split(merged[:, tb, :], tb, whole, [merged_ready, (PE.semaphore, PE.count)])
             for tb in range(TB)]
    out = {}

    def evac(tb, g, ps, ready):
        out[tb] = k.add_to_x(tb, g * BANK, ps, 1.0, ready)
        return out[tb]
    k.project_tokens(hT, 2, evac, ready)
    room.close()
    return [out[0], out[1]]


def top_sixteen(k, values, spare, top, index):
    V, vector = k.V, k.vector
    V.mark(vector.max(top[:, 0:8], values))
    V.mark(vector.max_index(index[:, 0:8], top[:, 0:8], values))
    V.mark(vector.match_replace(spare, top[:, 0:8], values, -3.0e38))
    V.mark(vector.max(top[:, 8:16], spare))
    return V.mark(vector.max_index(index[:, 8:16], top[:, 8:16], spare))


def experts(k, x_ready):
    PE, V, S, G, W, banks, tm = k.PE, k.V, k.S, k.G, k.W, k.banks, k.tm
    tensor, vector, scalar, pool, hT, psum = k.tensor, k.vector, k.scalar, k.pool, k.hT, k.psum
    SETS = 2 * PH
    room, before = ExitStack(), ExitStack()
    picked = k.sb("picked", [P, 3, T], room=room)
    iota = k.sb("iota", [P, P], room=room)[:, :]
    first_rows = k.sb("active_first", [P, 64, T], room=room)
    arena = k.sb("queries", [P, 8, UNIT], room=before)
    k.fence()
    iota_ready = k.load(iota, k.A["consts"][:, P:2 * P], x_ready)
    keys = arena[:, 7, :]
    loaded = k.load(keys, k.A["sub_keys"], x_ready)
    keys = keys.rearrange("p (s k) -> p s k", k=KEYS)
    h_ready = k.norm(k.col("ffn_gain_2"), x_ready, k.fm(arena[:, 0, :]), tm(arena[:, 1, :]))

    qT = arena[:, 1:3, :].rearrange("p u (c t) -> p (u c) t", t=T)

    def evac_q(g, ps, ready):
        S.wait(ready)
        return S.mark(scalar.activation(qT[:, 2 * g:2 * g + 2, :], ps.rearrange("p (c t) -> p c t", t=T), ACT.Copy))
    q_ready = k.project_features(hT, 8, evac_q, h_ready)
    score = [arena[:, 3 + tb, :].rearrange("p (s k) -> p s k", k=KEYS) for tb in range(TB)]
    scored = [[], []]
    PE.wait(q_ready, loaded)
    for tb in range(TB):
        for s0 in range(0, SETS, 4):
            b, ps = banks.take(PE)
            for s in range(4):
                ins = tensor.matmul(ps[:, s * KEYS:(s + 1) * KEYS], qT[:, s0 + s, tb * P:(tb + 1) * P],
                                    keys[:, s0 + s, :], start=True, stop=True)
            done = PE.mark(ins)
            S.wait(done)
            m = S.mark(scalar.activation(score[tb][:, s0:s0 + 4, :], ps.rearrange("p (s k) -> p s k", k=KEYS),
                                         ACT.Copy))
            banks.free(b, m)
            scored[tb].append(m)

    picked_ready = []

    def picks(tb):
        base = arena[:, 5 + tb, :]
        top = base[:, 0:T].rearrange("p (h s n) -> p h s n", h=PH, s=2)
        index_raw = base[:, T:2 * T].bitcast(U32).rearrange("p (h s n) -> p h s n", h=PH, s=2)
        index = base[:, 2 * T:3 * T].rearrange("p (h s n) -> p h s n", h=PH, s=2)
        best = base[:, 3 * T:3 * T + P].rearrange("p (h n) -> p h n", h=PH)
        position = base[:, 3 * T + P:4 * T].bitcast(U32)
        part = [base[:, 4 * T + i * P:4 * T + (i + 1) * P] for i in range(2)]
        raw = base[:, 5 * T:5 * T + P].bitcast(U32)
        gate = base[:, 5 * T + P:6 * T].rearrange("p (h n) -> p h n", h=PH)
        chosen = [base[:, 6 * T + i * P:6 * T + (i + 1) * P] for i in range(2)]
        total = base[:, 7 * T:7 * T + PH]
        spare = arena[:, 0, :] if tb else arena[:, 1, :]
        V.wait(scored[tb])
        for h in range(PH):
            for s in range(2):
                top_sixteen(k, score[tb][:, 2 * h + s, :], spare[:, 0:KEYS], top[:, h, s, :], index_raw[:, h, s, :])
            yield
        V.mark(vector.tensor_copy(base[:, 2 * T:3 * T], base[:, T:2 * T].bitcast(U32)))
        for h in range(PH):
            cand = spare[:, T:2 * T]
            V.mark(vector.tensor_tensor(cand.rearrange("p (a b) -> p a b", b=TOP), k.spread(top[:, h, 0, :], TOP),
                                        k.across(top[:, h, 1, :], TOP), ALU.add))
            top_sixteen(k, cand, spare[:, 0:T], best[:, h, :], position[:, h * TOP:(h + 1) * TOP])
            yield
        V.wait(iota_ready)
        for side, op, by in ((0, ALU.logical_shift_right, 4), (1, ALU.bitwise_and, TOP - 1)):
            V.mark(vector.tensor_scalar(raw, position, by, None, op))
            V.mark(vector.tensor_copy(part[side], raw))
            hit = spare.rearrange("p (m n) -> p m n", n=TOP)
            V.mark(vector.tensor_tensor(hit, k.spread(part[side], TOP), k.across(iota[:, 0:TOP], P), ALU.is_equal))
            yield
            for h in range(PH):
                mine = hit[:, h * TOP:(h + 1) * TOP, :]
                V.mark(vector.tensor_tensor(mine, mine, k.across(index[:, h, side, :], TOP), ALU.mult))
            yield
            V.mark(vector.tensor_reduce(chosen[side], hit, AX.X, ALU.add))
            yield
        m = V.mark(vector.tensor_tensor(gate, best, best[:, :, 0:1].to_broadcast([P, PH, TOP]), ALU.subtract))
        S.wait(m)
        m = S.mark(scalar.activation(gate, gate, ACT.Exp))
        V.wait(m)
        V.mark(vector.tensor_reduce(total, gate, AX.X, ALU.add))
        V.mark(vector.reciprocal(total, total))
        m = V.mark(vector.tensor_tensor(gate, gate, k.spread(total, TOP), ALU.mult))
        b, ps = banks.take(PE)
        PE.wait(m)
        for i, src in enumerate((base[:, 5 * T + P:6 * T], chosen[0], chosen[1])):
            ins = tensor.transpose(ps[:, i * P:(i + 1) * P], src, k.ident)
        m = PE.mark(ins)
        V.wait(m)
        picked_ready.append(V.mark(vector.tensor_copy(picked[:, :, tb * P:(tb + 1) * P],
                                                      ps[:, 0:3 * P].rearrange("p (w t) -> p w t", w=3))))
        banks.free(b, picked_ready[-1])
        yield

    def steps():
        for tb in range(TB):
            yield from picks(tb)
    todo = steps()

    def activate(j, dst):
        b, ps = banks.take(PE)
        k.feature_major(ps[:, 0:T], hT)
        done = k.feature_major(ps[:, T:2 * T], hT)
        S.wait(done)
        m = S.mark(scalar.activation(dst, ps.rearrange("p (j t) -> p j t", j=2), ACT.Gelu))
        banks.free(b, m)

    for j in range(0, 64, 2):
        activate(j, first_rows[:, j:j + 2, :])
        for _ in range(2):
            next(todo, None)
    for _ in todo:
        pass
    before.close()
    last_rows = k.sb("active_last", [P, 64, T], room=room)
    k.fence()
    for j in range(64, KEYS, 2):
        activate(j, last_rows[:, j - 64:j - 62, :])
    rows = (first_rows, last_rows)

    lot = 4
    activated = (S.semaphore, S.count)
    read_h = (PE.semaphore, PE.count)
    hots = ExitStack()
    onehot = k.sb("onehot", [P, 2, 2, lot, KEYS], room=hots)
    G.wait(picked_ready, iota_ready)
    V.wait(activated, read_h)
    G.wait(read_h)
    used = {}
    prepared = {}

    def prepare(q):
        i_hot, j_hot = onehot[:, q % 2, 0, :, :], onehot[:, q % 2, 1, :, :]
        V.wait(used.get(q - 2))
        G.wait(used.get(q - 2))
        for n in range(lot):
            t = q * lot + n
            mi = V.mark(vector.tensor_scalar(i_hot[:, n, :], iota, picked[:, 1, t:t + 1], picked[:, 0, t:t + 1],
                                             ALU.is_equal, ALU.mult))
        mj = G.mark(pool.tensor_tensor(j_hot, k.across(iota, lot), k.spread(picked[:, 2, q * lot:(q + 1) * lot], KEYS),
                                       ALU.subtract))
        S.wait(mj)
        S.mark(scalar.activation(j_hot, j_hot, ACT.Abs))
        mj = S.mark(scalar.activation(j_hot, j_hot, ACT.Relu, scale=-1.0, bias=1.0))
        b, ps = banks.take(PE)
        PE.wait(mi, mj)
        for n in range(lot):
            ins = tensor.matmul(ps[:, n * KEYS:(n + 1) * KEYS], i_hot[:, n, :], j_hot[:, n, :], start=True, stop=True)
        used[q] = PE.mark(ins)
        prepared[q] = (b, ps)

    def weigh(q):
        b, ps = prepared.pop(q)
        V.wait(used[q])
        for half in range(2):
            a = rows[half][:, :, q * lot:(q + 1) * lot].rearrange("p j t -> p t j")
            m = V.mark(vector.tensor_tensor(a, ps.rearrange("p (t j) -> p t j", t=lot)[:, :, half * 64:(half + 1) * 64],
                                            a, ALU.mult))
        banks.free(b, m)
        return m

    prepare(0)
    for q in range(1, T // lot):
        prepare(q)
        weigh(q - 1)
    weighed = weigh(T // lot - 1)
    hots.close()

    parts = tuple(k.sb(f"weights_{n}", [P, 2, 2, T], F32R, room) for n in ("high", "low"))
    k.fence()
    banks.use(range(4, 8))
    PE.wait(banks.freed[0:4])
    part_ready, part_read = {}, {}

    def part(pair):
        source = rows[pair // 32][:, 2 * pair % 64:2 * pair % 64 + 2, :]
        part_ready[pair] = k.split(parts[0][:, pair % 2, :, :], parts[1][:, pair % 2, :, :], source,
                                   [weighed, part_read.get(pair - 2)])

    part(0)
    for pair in range(KEYS // 2):
        if pair + 1 < KEYS // 2:
            part(pair + 1)
        PE.wait(part_ready[pair])
        for jj in range(2):
            w = W.take(PE)
            for tb in range(TB):
                still = k.at(parts, slice(None), pair % 2, jj, slice(tb * P, (tb + 1) * P))
                for half in range(2):
                    ins = k.products(psum[:, 2 * tb + half, :], still,
                                     k.at(w, slice(None), slice(half * BANK, (half + 1) * BANK)),
                                     pair == 0 and jj == 0, pair == KEYS // 2 - 1 and jj == 1)
            done = PE.mark(ins)
            W.release(done)
        part_read[pair] = done
    out = [[k.add_to_x(tb, half * BANK, psum[:, 2 * tb + half, :], 1.0, done) for half in range(2)][-1]
           for tb in range(TB)]
    room.close()
    return out


def by_column(v):
    return v.reshape(-1, P).T


def feature_tiles(w):
    k, n = w.shape
    return w.reshape(KC, P, n // P, P).transpose(2, 1, 0, 3).reshape(n // P, P, TILE)


def token_tiles(w, width=BANK):
    k, n = w.shape
    rows = TILE // width
    return w.reshape(k // (rows * P), rows, P, n // width, width).transpose(3, 0, 2, 1, 4).reshape(-1, P, TILE)


def constants():
    i = np.arange(P)
    row, colm = i[:, None], i[None, :]
    parts = {
        "ident": (row == colm), "iota": np.broadcast_to(colm, (P, P)),
        "strict": row < colm, "upto": row <= colm,
    }
    def level(m):
        return (row // (2 * m) == colm // (2 * m)) & (row % (2 * m) >= m) & (colm % (2 * m) < m)
    parts["pairT"] = level(1).T
    parts["level"] = np.concatenate([level(2 ** n) for n in range(LEVELS)], axis=1)
    parts["headsum"] = row // HD == colm // HD
    sel = np.zeros((P, KC, HEADS))
    for c in range(KC):
        for h in range(2):
            sel[h * HD:(h + 1) * HD, c, 2 * c + h] = 1
    parts["headsel"] = sel.reshape(P, -1)
    parts["scan_keep"] = np.broadcast_to((colm != 0), (P, P))
    q = np.concatenate([np.broadcast_to(row, (P, P)), np.broadcast_to(row + P, (P, 2 * P))], axis=1)
    k = np.broadcast_to(np.concatenate([i, i, i + P])[None, :], (P, 3 * P))
    parts["causal_dist"] = np.where(q >= k, -(q - k).astype(np.float64), NEG)
    chunk = 64
    near = (k // chunk <= q // chunk) & (k // chunk >= q // chunk - 2)
    parts["window_dist"] = np.where(near, -np.abs(q - k).astype(np.float64), NEG)
    parts["before"] = k < q
    parts["before_neg"] = np.where(k < q, 0.0, NEG)
    return np.concatenate([parts[name].astype(np.float32) for name, _ in CONSTS], axis=1)


def kernel(**inputs):
    import concourse.bacc as bacc
    from concourse.bass_utils import run_bass_kernel_spmd

    a = {k: np.asarray(v) for k, v in inputs.items()}
    arrays = {"x": a["x"].reshape(TB, P, D)}
    cat = lambda *v: np.concatenate(v, axis=1)
    arrays["cols"] = cat(
        by_column(a["ffn_norm"].reshape(-1)), by_column(a["mix_norm"].reshape(-1)), by_column(a["rwkv_mu"].reshape(-1)),
        *(by_column(a[n].reshape(-1)) for n in ("rwkv_w0", "rwkv_a0", "rwkv_k_k", "rwkv_k_a", "rwkv_r_k", "kv_norm",
                                                "mix_norm_gain_2", "ffn_norm_gain_2", "diff_subln")),
        *(np.tile(a[n].reshape(-1), 2)[:, None] for n in ("k_norm", "diff_q_norm", "swa_q_gain_2", "swa_k_gain_2")))
    arrays["consts"] = constants()
    arrays["ffn_in"] = a["ffn_w_in"].reshape(2, 2, KC, P, 2, FC, P).transpose(0, 1, 5, 4, 3, 2, 6).reshape(
        2, 2, FC, 2, P, TILE)
    arrays["ffn_out"] = a["ffn_w_out"].reshape(2, 2, FC, P, D)
    rows = lambda w: w.reshape(KC, P, -1).transpose(1, 0, 2)
    arrays["lora_in"] = np.concatenate([rows(a["rwkv_w1"][0]), rows(a["rwkv_a1"][0])], axis=2).reshape(P, KC * P)
    arrays["g1"] = rows(a["rwkv_g1"][0]).reshape(P, KC * 160)
    arrays["lora_out"] = cat(a["rwkv_w2"][0], a["rwkv_a2"][0])
    arrays["g2"] = a["rwkv_g2"][0]
    w_rkv = a["rwkv_w_rkv"][0]
    arrays["w_r"], arrays["w_k"], arrays["w_v"] = feature_tiles(w_rkv[0]), feature_tiles(w_rkv[1]), token_tiles(w_rkv[2])
    arrays["w_o"] = token_tiles(a["rwkv_w_o"][0])
    arrays["ln"] = cat(a["rwkv_ln_g"], a["rwkv_ln_b"])
    arrays["w_kv"] = token_tiles(a["w_kv"])
    arrays["diff_w_q"] = token_tiles(a["diff_w_q"][0])
    arrays["diff_w_o"] = token_tiles(a["diff_w_o"][0])
    arrays["lam"] = a["diff_lambda"].reshape(1, 4 * HD)
    w = a["w_in_2"][0]
    arrays["in_q_a"] = token_tiles(w[:, 0:512])
    arrays["in_kv_a"] = token_tiles(w[:, 512:768], 256)
    arrays["in_qk_b"] = feature_tiles(w[:, 768:1792])
    arrays["in_v_b"] = token_tiles(w[:, 1792:2304])
    arrays["in_gates"] = token_tiles(w[:, 2304:])
    arrays["gate_bias"] = a["gate_bias_2"]
    arrays["sinks"] = a["swa_sinks_2"]
    arrays["up_swa"], arrays["up_sb"] = token_tiles(a["w_up_swa_2"][0]), token_tiles(a["w_up_sb_2"][0])
    arrays["w_out"] = token_tiles(a["w_out_2"][0])
    arrays["peer_q"] = feature_tiles(a["peer_w_q_2"][0])
    arrays["sub_keys"] = a["peer_sub_keys_2"][0].reshape(16, P, P).transpose(2, 0, 1).reshape(P, 16 * P)
    u = a["peer_u_2"][0].reshape(KEYS, KEYS, KC, P)
    arrays["peer_u"] = u.transpose(1, 3, 2, 0).reshape(KEYS, P, TILE)
    arrays["peer_v"] = a["peer_v_2"][0].reshape(KEYS, KEYS, D).transpose(1, 0, 2)

    nc = bacc.Bacc("TRN2", target_bir_lowering=False, num_devices=1)
    handles, launch = {}, {}
    for name, value in arrays.items():
        launch[f"{name}_dram"] = np.ascontiguousarray(value)
        handles[name] = nc.dram_tensor(f"{name}_dram", value.shape, F32, kind="ExternalInput").ap()
    out = nc.dram_tensor("out_dram", (TB, P, D), F32, kind="ExternalOutput").ap()
    with ExitStack() as stack:
        block(nc, handles, out, stack)
    result = run_bass_kernel_spmd(nc, [launch], core_ids=[0])
    return result.results[0]["out_dram"].reshape(1, T, D)
```

```python
import math
from contextlib import ExitStack

import numpy as np

import concourse.bass as bass
import concourse.mybir as mybir
from concourse.alu_op_type import AluOpType as ALU

F32 = mybir.dt.float32
F32R = mybir.dt.float32r
U32 = mybir.dt.uint32
ACT = mybir.ActivationFunctionType
AX = mybir.AxisListType

P = 128
T = 256
TB = T // P
D = 1024
KC = D // P
FF = 2816
FC = FF // P
UNIT = 2048
TILE = 1024
RAW_SLOTS = 4
SPLIT_SLOTS = 3
BANK = 512
HEADS = 16
HD = 64
DH = 8
KEYS = 128
TOP = 16
PH = 8
NEG = -1e30
DECAY = math.exp(-0.5)
LEVELS = 7

COLS = [("ffn_norm", 4 * KC), ("mix_norm", 2 * KC), ("mu", 6 * KC), ("w0", KC), ("a0", KC), ("k_k", KC),
        ("k_a", KC), ("r_k", KC), ("kv_norm", KC), ("mix_gain_2", KC), ("ffn_gain_2", KC),
        ("subln", 1), ("k_norm", 1), ("q_norm", 1), ("swa_q", 1), ("swa_k", 1)]
CONSTS = [("ident", P), ("iota", P), ("strict", P), ("upto", P), ("pairT", P), ("level", LEVELS * P),
          ("headsel", KC * HEADS), ("headspread", KC * P), ("scan_keep", P), ("causal_dist", 3 * P),
          ("window_dist", 3 * P), ("before", 3 * P), ("before_neg", 3 * P)]


def offsets(table):
    out, at = {}, 0
    for name, n in table:
        out[name] = (at, at + n)
        at += n
    return out, at


class Lane:

    def __init__(self, engine, semaphore, linked):
        self.engine, self.semaphore, self.count, self.seen = engine, semaphore, 0, {}
        self.linked = linked

    def wait(self, *marks):
        for m in marks:
            if m is None:
                continue
            if isinstance(m, list):
                self.wait(*m)
                continue
            sem, value = m
            if self.seen.get(sem.name, 0) < value:
                self.engine.wait_ge(sem, value)
                self.seen[sem.name] = value

    def mark(self, instruction, alone=False):
        instruction.then_inc(self.semaphore, 1)
        self.count += 1
        done = (self.semaphore, self.count)
        if self.linked and not alone:
            self.wait(done)
        return done


class Weights:

    def __init__(self, lane, raw, raw_semaphores, high, low, S, V, G, tiles):
        self.lane, self.raw, self.sems, self.high, self.low = lane, raw, raw_semaphores, high, low
        self.S, self.V, self.G, self.tiles = S, V, G, tiles
        self.pool_share = 0
        self.slots = high.shape[1]
        self.sent, self.parted, self.taken, self.used = 0, 0, 0, []
        self.ready = []
        self.asides = []
        for _ in raw_semaphores:
            self.load()

    def load(self):
        n = self.sent
        if n < len(self.tiles):
            slot = n % len(self.sems)
            self.lane.engine.dma_start(self.raw[:, slot, :], self.tiles[n]).then_inc(self.sems[slot], 16)
        self.sent += 1

    def split(self):
        n = self.parted
        self.parted += 1
        if n >= len(self.tiles):
            return
        S, V, slot, to = self.S, self.V, n % len(self.sems), n % self.slots
        loaded = (self.sems[slot], 16 * (n // len(self.sems) + 1))
        reader = self.used[n - self.slots] if n >= self.slots else None
        raw = self.raw[:, slot, :]
        S.wait(loaded, reader)
        m = S.mark(S.engine.activation(self.high[:, to, :], raw, ACT.Copy), alone=True)
        if self.pool_share and n % self.pool_share == 0:
            V = self.G
        V.wait(loaded, m, reader)
        m = V.mark(V.engine.tensor_tensor(self.low[:, to, :], raw, self.high[:, to, :].bitcast(F32), ALU.subtract),
                   alone=True)
        self.ready.append(m)
        self.lane.wait(m)
        self.load()
        self.step_aside()

    def take(self, lane):
        n = self.taken
        self.taken += 1
        while self.parted <= n + 1:
            self.split()
        lane.wait(self.ready[n])
        return self.high[:, n % self.slots, :], self.low[:, n % self.slots, :]

    def step_aside(self):
        while self.asides:
            if next(self.asides[0], "over") != "over":
                return
            self.asides.pop(0)

    def finish_aside(self):
        while self.asides:
            self.step_aside()

    def release(self, mark):
        self.used.append(mark)
        while self.parted < len(self.used) + self.slots - 1:
            self.split()


class Banks:

    def __init__(self, psum):
        self.psum, self.freed, self.held = psum, [None] * 8, set()
        self.use(range(8))

    def use(self, banks):
        self.order, self.at = list(banks), 0

    def take(self, lane):
        b = self.order[self.at % len(self.order)]
        self.at += 1
        assert b not in self.held, "a bank is taken before its reader is queued"
        self.held.add(b)
        lane.wait(self.freed[b])
        return b, self.psum[:, b, :]

    def free(self, b, mark):
        self.freed[b] = mark
        self.held.discard(b)


class Core:
    pass


def block(nc, A, out, stack):
    sb = lambda name, shape, dtype=F32, room=stack: room.enter_context(nc.sbuf_tensor(name, shape, dtype))
    sem = lambda name: stack.enter_context(nc.semaphore(name))
    tensor, vector, scalar, pool, sync = nc.tensor, nc.vector, nc.scalar, nc.gpsimd, nc.sync

    x = sb("x", [P, TB, D])
    hT_high, hT_low = sb("hT_high", [P, KC, T], F32R), sb("hT_low", [P, KC, T], F32R)
    hT = (hT_high, hT_low)
    raw = sb("raw_tiles", [P, RAW_SLOTS, TILE])
    tile_high = sb("tile_high", [P, SPLIT_SLOTS, TILE], F32R)
    tile_low = sb("tile_low", [P, SPLIT_SLOTS, TILE], F32R)
    col_at, n_cols = offsets(COLS)
    cols = sb("cols", [P, n_cols])
    const_at, n_consts = offsets(CONSTS)
    ident = sb("ident", [P, P])[:, :]
    small = sb("small", [P, 256])
    minus_half = sb("minus_half", [P, 16])
    psum = stack.enter_context(nc.psum_tensor("psum", [P, 8, BANK], F32))

    PE, V, S, G, SP = (Lane(e, sem(n), linked) for e, n, linked in (
        (tensor, "tensor_done", False), (vector, "vector_done", True), (scalar, "scalar_done", True),
        (pool, "pool_done", True), (sync, "sync_done", False)))

    def col(name, n=0, k=KC):
        a = col_at[name][0] + n * k
        return cols[:, a:a + k]

    def fm(buffer):
        return buffer.rearrange("p (c t) -> p c t", t=T)

    def tm(buffer):
        return buffer.rearrange("p (b c) -> p b c", b=TB)

    def spread(ap, n):
        return ap.unsqueeze(2).to_broadcast([P, ap.shape[1], n])

    def across(ap, n):
        return ap.unsqueeze(1).to_broadcast([P, n, ap.shape[1]])

    def tiles_of(*names):
        return [A[name][i] for name in names for i in range(A[name].shape[0])]

    def ffn_tiles(l, j):
        out = []
        for f in range(FC + 1):
            if f < FC:
                out += [A["ffn_in"][l, j, f, 0], A["ffn_in"][l, j, f, 1]]
            if f > 0:
                out.append(A["ffn_out"][l, j, f - 1])
        return out

    tiles = ffn_tiles(0, 0) + tiles_of("w_k", "w_r", "w_v", "w_o") + ffn_tiles(0, 1) + tiles_of("w_kv")
    tiles += ffn_tiles(1, 0) + tiles_of("diff_w_q", "diff_w_o") + ffn_tiles(1, 1)
    tiles += tiles_of("in_q_a", "in_kv_a", "in_qk_b", "in_v_b", "in_gates", "up_swa", "up_sb", "w_out")
    tiles += tiles_of("peer_q", "peer_u", "peer_v")

    def load(dst, src, *after):
        S.wait(*after)
        s = sem(f"load_{dst.tensor.name}_{len(loads)}")
        scalar.dma_start(dst, src).then_inc(s, 16)
        loads.append(s)
        return (s, 16)

    def row(name, dst, *after):
        a = A[name]
        return load(dst, bass.AP(a.tensor, a.offset, [[0, P], [1, a.shape[1]]]), *after)

    loads = []
    x_loaded = [load(x[:, tb, :], A["x"][tb]) for tb in range(TB)]
    cols_loaded = load(cols[:, :], A["cols"])
    ident_loaded = load(ident, A["consts"][:, 0:P])
    W = Weights(SP, raw, [sem(f"raw_{i}") for i in range(RAW_SLOTS)], tile_high, tile_low, S, V, G, tiles)
    banks = Banks(psum)
    half_ready = V.mark(vector.memset(minus_half[:, :], -0.5))
    G.wait(half_ready)
    S.wait(ident_loaded, cols_loaded)
    PE.wait(ident_loaded)
    V.wait(cols_loaded, ident_loaded)

    def rsqrt(ap, n, ready):
        G.wait(ready, half_ready)
        return G.mark(pool.tensor_tensor(ap, ap, minus_half[:, 0:n], ALU.pow))

    def transposed(src, tb, dst, ready, gain=None, scale=None, n=KC):
        last = None
        for c0 in range(0, n, 4):
            m = min(4, n - c0)
            PE.wait(ready)
            b, ps = banks.take(PE)
            for c in range(m):
                ins = tensor.transpose(ps[:, c * P:(c + 1) * P], src[:, (c0 + c) * P:(c0 + c + 1) * P], ident)
            turned = PE.mark(ins)
            dstv = dst[:, c0:c0 + m, tb * P:(tb + 1) * P]
            psv = ps[:, 0:m * P].rearrange("p (c t) -> p c t", t=P)
            if gain is not None:
                V.wait(turned)
                last = V.mark(vector.tensor_tensor(dstv, psv, spread(gain[:, c0:c0 + m], P), ALU.mult))
            elif scale is not None:
                V.wait(turned)
                last = V.mark(vector.tensor_scalar(dstv, psv, scale[0], scale[1], ALU.mult, ALU.mult))
            else:
                S.wait(turned)
                last = S.mark(scalar.activation(dstv, psv, ACT.Copy))
            banks.free(b, last)
        return last

    def split(high, low, source, ready):
        S.wait(ready)
        m = S.mark(scalar.activation(high, source, ACT.Copy), alone=True)
        V.wait(m)
        return V.mark(vector.tensor_tensor(low, source, high.bitcast(F32), ALU.subtract), alone=True)

    def transposed_split(src, whole, ready, to=hT, first=0, n=KC, gain=None, scale=None, blocks=range(TB),
                         each=None):
        out, turned = [], []

        def split_oldest():
            c0, tb, m = turned.pop(0)
            part = (slice(None), slice(first + c0, first + c0 + 4), slice(tb * P, (tb + 1) * P))
            out.append(split(to[0][part], to[1][part], whole[:, c0:c0 + 4, tb * P:(tb + 1) * P], m))
        for i, tb in enumerate(blocks):
            for c0 in range(0, n, 4):
                m = transposed(src[:, i, c0 * P:(c0 + 4) * P], tb, whole[:, c0:c0 + 4, :],
                               [ready, each[i]] if each else ready, n=4,
                               gain=None if gain is None else gain[:, c0:c0 + 4], scale=scale)
                turned.append((c0, tb, m))
                if len(turned) > 1:
                    split_oldest()
        split_oldest()
        V.wait(out[-1])
        return out

    def norm(gain, ready, whole, xn):
        scaled = []
        for tb in range(TB):
            ss = small[:, tb:tb + 1]
            S.wait(ready[tb])
            m = S.mark(scalar.activation(xn[:, tb, :], x[:, tb, :], ACT.Square, accum_out=ss), alone=True)
            V.wait(m)
            m = V.mark(vector.tensor_scalar(ss, ss, 1.0 / D, 1e-6, ALU.mult, ALU.add), alone=True)
            scaled.append(rsqrt(ss, 1, m))
        V.wait(scaled[0], ready[0])
        S.wait(scaled[1], ready[1])
        scaled = [V.mark(vector.tensor_scalar(xn[:, 0, :], x[:, 0, :], small[:, 0:1], None, ALU.mult), alone=True),
                  S.mark(scalar.activation(xn[:, 1, :], x[:, 1, :], ACT.Copy, scale=small[:, 1:2]), alone=True)]
        return transposed_split(xn, whole, None, gain=gain, each=scaled)

    def add_to_x(tb, n0, ps, factor, ready):
        V.wait(ready)
        xs = x[:, tb, n0:n0 + BANK]
        return V.mark(vector.scalar_tensor_tensor(out=xs, in0=ps, scalar=factor, in1=xs, op0=ALU.mult, op1=ALU.add),
                      alone=True)

    def products(out, still, moving, first, last):
        tensor.matmul(out, still[0], moving[0], start=first, stop=False)
        tensor.matmul(out, still[0], moving[1], start=False, stop=False)
        return tensor.matmul(out, still[1], moving[0], start=False, stop=last)

    def at(pair, *index):
        return (pair[0][index], pair[1][index])

    EVERY = slice(None)

    def feature_major(ps, src):
        high, low = W.take(PE)
        tile = tuple(t.rearrange("p (k n) -> p k n", k=KC) for t in (high, low))
        for k in range(KC):
            ins = products(ps, at(tile, EVERY, k, EVERY), at(src, EVERY, k, EVERY), k == 0, k == KC - 1)
        done = PE.mark(ins)
        W.release(done)
        return done

    def ffn(l, j, ready):
        with ExitStack() as room:
            scratch = sb(f"norm_{l}{j}", [P, 2, UNIT], room=room)
            BUFS = 3
            act = sb(f"hidden_{l}{j}", [P, BUFS, 2, T], room=room)
            high, low = (sb(f"hidden_{n}_{l}{j}", [P, BUFS, T], F32R, room) for n in ("high", "low"))
            fence()
            h_ready = norm(col("ffn_norm", 2 * l + j), ready, fm(scratch[:, 0, :]), tm(scratch[:, 1, :]))
            PE.wait(h_ready)
            banks.use(range(4, 8))
            PE.wait(banks.freed[0:4])
            hidden, down_done = {}, {}

            def gate_up(f):
                b, ps = banks.take(PE)
                feature_major(ps[:, 0:T], hT)
                done = feature_major(ps[:, T:2 * T], hT)
                s, n = act[:, f % BUFS, 1, :], f % BUFS
                S.wait(done)
                silu = S.mark(scalar.activation(s, ps[:, 0:T], ACT.Silu), alone=True)
                V.wait(silu)
                m = V.mark(vector.tensor_tensor(act[:, n, 0, :], s, ps[:, T:2 * T], ALU.mult))
                banks.free(b, m)
                hidden[f] = split(high[:, n, :], low[:, n, :], act[:, n, 0, :], [m, down_done.get(f - BUFS)])

            def down(f):
                w = W.take(PE)
                PE.wait(hidden[f])
                for tb in range(TB):
                    part = at((high, low), EVERY, f % BUFS, slice(tb * P, (tb + 1) * P))
                    for half in range(2):
                        ins = products(psum[:, 2 * tb + half, :], part, at(w, EVERY, slice(half * BANK, (half + 1) * BANK)),
                                       f == 0, f == FC - 1)
                down_done[f] = PE.mark(ins)
                W.release(down_done[f])

            gate_up(0)
            for f in range(1, FC):
                gate_up(f)
                down(f - 1)
            down(FC - 1)
            out_marks = []
            for tb in range(TB):
                for half in range(2):
                    m = add_to_x(tb, half * BANK, psum[:, 2 * tb + half, :], 0.5, down_done[FC - 1])
                    banks.free(2 * tb + half, m)
                out_marks.append(m)
            banks.use(range(8))
        return out_marks

    def project_tokens(src, groups, evac, ready, kcs=KC, first=0):
        out = []
        PE.wait(ready)
        for g in range(groups):
            got = [banks.take(PE) for _ in range(TB)]
            for k0 in range(0, kcs, 2):
                tile = tuple(t.rearrange("p (k n) -> p k n", k=2) for t in W.take(PE))
                for tb in range(TB):
                    for k in range(2):
                        ins = products(got[tb][1], at(src, EVERY, first + k0 + k, slice(tb * P, (tb + 1) * P)),
                                       at(tile, EVERY, k, EVERY), k0 + k == 0, k0 + k == kcs - 1)
                done = PE.mark(ins)
                W.release(done)
            for tb in range(TB):
                m = evac(tb, g, got[tb][1], done)
                banks.free(got[tb][0], m)
                out.append(m)
        return out

    def project_features(src, groups, evac, ready):
        out = []
        PE.wait(ready)
        for g in range(groups):
            b, ps = banks.take(PE)
            feature_major(ps[:, 0:T], src)
            done = feature_major(ps[:, T:2 * T], src)
            m = evac(g, ps, done)
            banks.free(b, m)
            out.append(m)
        return out

    def fence():
        now = [(lane.semaphore, lane.count) for lane in (PE, V, S, G) if lane.count]
        for lane in (V, S, G):
            lane.wait(now)

    def finish(ready):
        for tb in range(TB):
            s = sem(f"stored_{tb}")
            SP.wait(ready[tb])
            sync.dma_start(out[tb], x[:, tb, :]).then_inc(s, 16)
            sync.wait_ge(s, 16)

    env = Core()
    env.PE, env.V, env.S, env.G, env.W = PE, V, S, G, W
    env.A, env.banks, env.psum, env.sb, env.sem = A, banks, psum, sb, sem
    env.fm, env.tm, env.col, env.small, env.const_at = fm, tm, col, small, const_at
    env.ident, env.hT, env.tensor, env.vector, env.scalar = ident, hT, tensor, vector, scalar
    env.pool, env.minus_half, env.spread, env.across, env.load, env.row = pool, minus_half, spread, across, load, row
    env.norm, env.split, env.fence, env.at, env.products = norm, split, fence, at, products
    env.feature_major, env.transposed, env.transposed_split, env.rsqrt, env.add_to_x = feature_major, transposed, transposed_split, rsqrt, add_to_x
    env.project_tokens, env.project_features = project_tokens, project_features
    x_ready = ffn(0, 0, x_loaded)
    x_ready = rwkv(env, x_ready)
    x_ready = ffn(0, 1, x_ready)
    kv_room = ExitStack()
    shared, kv_ready = shared_kv(env, x_ready, kv_room)
    x_ready = ffn(1, 0, x_ready)
    x_ready = diff_attention(env, x_ready, shared, kv_ready)
    kv_room.close()
    x_ready = ffn(1, 1, x_ready)
    W.pool_share = 3
    x_ready = mix_2(env, x_ready)
    x_ready = experts(env, x_ready)
    finish(x_ready)


def rwkv(k, x_ready):
    PE, V, S, G, W, banks, fm, col = k.PE, k.V, k.S, k.G, k.W, k.banks, k.fm, k.col
    tensor, vector, scalar, pool, spread, across = k.tensor, k.vector, k.scalar, k.pool, k.spread, k.across
    blk = lambda buffer: buffer.rearrange("p (c t) -> p c t", t=P)

    room, early = ExitStack(), ExitStack()
    arena = k.sb("rwkv", [P, 15, UNIT], room=room)
    masks = k.sb("masks", [P, 10 * P], room=room)
    other = tuple(k.sb(f"mixed_{n}", [P, KC, T], F32R, early) for n in ("high", "low"))
    k.fence()

    def unit(i):
        return arena[:, i, :]

    h, dx, whole = fm(unit(0)), fm(unit(14)), fm(unit(1))
    mixed = [k.hT, other]
    rT, kT, aT, sig = fm(unit(2)), fm(unit(3)), fm(unit(4)), fm(unit(5))
    v_tok, g_tok = k.tm(unit(6)), k.tm(unit(7))
    kk = fm(unit(8))

    w_in, w_g1, w_lo, w_g2 = unit(10)[:, 0:KC * P], unit(11)[:, 0:KC * 160], unit(12)[0:64, :], unit(13)
    A = k.A
    masks_ready = k.load(masks[:, :], A["consts"][:, 2 * P:12 * P])
    in_loaded = k.load(w_in, A["lora_in"])
    g1_loaded = k.load(w_g1, A["g1"])
    lo_loaded = k.load(w_lo, A["lora_out"])
    g2_loaded = [k.load(w_g2[:, 0:D], A["g2"][0:P, :]), k.load(w_g2[0:32, D:2 * D], A["g2"][P:160, :])]
    w_in = w_in.rearrange("p (k n) -> p k n", n=P)
    w_g1 = w_g1.rearrange("p (k n) -> p k n", n=160)
    h_ready = k.norm(col("mix_norm", 0), x_ready, h, k.tm(unit(9)))
    mask = lambda n: masks[:, n * P:(n + 1) * P]
    strict, upto, pair_t = mask(0), mask(1), mask(2)
    level = [mask(3 + n) for n in range(LEVELS)]
    mid, end = k.small[:, 16:32], k.small[:, 32:48]
    carry_scale, stats = k.small[:, 48:56], k.small[:, 64:128]
    bonus = k.small[:, 128:160]
    a_sel, b_sel = k.const_at["headsel"]

    V.wait(h_ready)
    V.mark(vector.tensor_tensor(dx[:, :, 1:T], h[:, :, 0:T - 1], h[:, :, 1:T], ALU.subtract))
    dx_ready = V.mark(vector.tensor_scalar(dx[:, :, 0:1], h[:, :, 0:1], -1.0, None, ALU.mult))
    mixed_read, whole_read = [None, None], []

    def mix(n, chunks=range(KC)):
        mu = col("mu", n)
        V.wait(dx_ready, whole_read)
        for c in chunks:
            m = V.mark(vector.scalar_tensor_tensor(out=whole[:, c, :], in0=dx[:, c, :], scalar=mu[:, c:c + 1],
                                                   in1=h[:, c, :], op0=ALU.mult, op1=ALU.add), alone=c != chunks[-1])
        return m

    def mix_split(n, slot):
        out = []
        for chunks in (range(0, KC // 2), range(KC // 2, KC)):
            m = mix(n, chunks)
            yield
            part = slice(chunks[0], chunks[-1] + 1)
            out.append(k.split(mixed[slot][0][:, part, :], mixed[slot][1][:, part, :], whole[:, part, :],
                               [m, mixed_read[slot]]))
            yield
        whole_read[:] = out
        return out

    hidden_w, hidden_a = unit(9)[0:64, 0:T], unit(9)[0:64, T:2 * T]
    hidden_g, hidden_g2 = unit(9)[:, 2 * T:3 * T], unit(9)[0:32, 3 * T:4 * T]

    def low_rank(weights, width, dst, func, *ready):
        b, ps = banks.take(PE)
        PE.wait(*ready)
        for c in range(KC):
            ins = tensor.matmul(ps[0:width, 0:T], weights(c), whole[:, c, :], start=(c == 0), stop=(c == KC - 1))
        done = PE.mark(ins)
        whole_read[:] = [done]
        S.wait(done)
        m = S.mark(scalar.activation(dst, ps[0:width, 0:T], func))
        banks.free(b, m)
        return m

    w_hidden = low_rank(lambda c: w_in[:, c, 0:64], 64, hidden_w, ACT.Tanh, mix(3), in_loaded)
    a_hidden = low_rank(lambda c: w_in[:, c, 64:P], 64, hidden_a, ACT.Copy, mix(4), in_loaded)
    ready = mix(5)
    g_hidden = [low_rank(lambda c: w_g1[:, c, 0:P], P, hidden_g, ACT.Sigmoid, ready, g1_loaded),
                low_rank(lambda c: w_g1[:, c, P:160], 32, hidden_g2, ACT.Sigmoid, ready, g1_loaded)]
    first_mix = finished(mix_split(1, 1))
    for hidden, what, base, at, dst in ((w_hidden, hidden_w, "w0", 0, sig), (a_hidden, hidden_a, "a0", D, aT)):
        for c in range(0, KC, 2):
            b, ps = banks.take(PE)
            PE.wait(hidden, lo_loaded)
            for i in range(2):
                ins = tensor.matmul(ps[:, i * T:(i + 1) * T], w_lo[0:64, at + (c + i) * P:at + (c + i + 1) * P], what,
                                    start=True, stop=True)
            lo_read = PE.mark(ins)
            S.wait(lo_read)
            for i in range(2):
                a_ready = S.mark(scalar.activation(dst[:, c + i, :], ps[:, i * T:(i + 1) * T], ACT.Sigmoid,
                                                   bias=col(base)[:, c + i:c + i + 1]))
            banks.free(b, a_ready)
        if base == "w0":
            sig_ready = a_ready

    def to_tokens(dst):
        def evac(tb, g, ps, ready):
            S.wait(ready)
            return S.mark(scalar.activation(dst[:, tb, g * BANK:(g + 1) * BANK], ps, ACT.Copy))
        return evac

    g_ready = []
    for tb in range(TB):
        for g in range(2):
            b, ps = banks.take(PE)
            PE.wait(g_hidden, g2_loaded)
            tensor.matmul(ps, hidden_g[:, tb * P:(tb + 1) * P], w_g2[:, g * BANK:(g + 1) * BANK], start=True, stop=False)
            ins = tensor.matmul(ps, hidden_g2[:, tb * P:(tb + 1) * P], w_g2[0:32, D + g * BANK:D + (g + 1) * BANK],
                                start=False, stop=True)
            g2_read = PE.mark(ins)
            g_ready.append(to_tokens(g_tok)(tb, g, ps, g2_read))
            banks.free(b, g_ready[-1])

    sums, centred, before = unit(9), unit(10), unit(11)
    p_in, p_before, p_inv = unit(9), unit(11), unit(12)
    keep, square, rate = unit(12), unit(13), unit(14)
    one_less_k_a = k.small[:, 160:168]
    inverse_norm = unit(10)[0:HEADS, 0:T]
    b_tok, k_tok = unit(1)[:, 0:D], unit(1)[:, D:2 * D]
    at_keep = k.const_at["scan_keep"]
    keep_row = k.load(keep[:, 0:P], A["consts"][:, at_keep[0]:at_keep[1]], lo_read)
    made = {}

    def decays():
        V.wait(keep_row, sig_ready, g2_read)
        m = V.mark(vector.tensor_copy(blk(keep)[:, 1:16, :], across(keep[:, 0:P], 15)))
        yield
        V.wait(m)
        V.mark(vector.tensor_tensor_scan(sums, keep, unit(5), 0.0, ALU.mult, ALU.add))
        V.mark(vector.tensor_copy(mid, blk(sums)[:, :, P // 2 - 1]), alone=True)
        V.mark(vector.tensor_copy(end, blk(sums)[:, :, P - 1]))
        yield
        m = V.mark(vector.tensor_tensor(blk(centred), blk(sums), spread(mid, P), ALU.subtract))
        G.wait(m, g2_read)
        before_made = G.mark(pool.tensor_tensor(before, centred, unit(5), ALU.subtract))
        mid_b, end_b = mid.rearrange("p (c b) -> p c b", b=TB), end.rearrange("p (c b) -> p c b", b=TB)
        V.mark(vector.tensor_tensor(carry_scale, end_b[:, :, 0], mid_b[:, :, 0], ALU.subtract))
        m = V.mark(vector.tensor_tensor(carry_scale, carry_scale, mid_b[:, :, 1], ALU.add))
        V.mark(vector.tensor_scalar(one_less_k_a, col("k_a"), -1.0, 1.0, ALU.mult, ALU.add))
        yield
        S.wait(m)
        S.mark(scalar.activation(p_in, centred, ACT.Exp, scale=-DECAY), alone=True)
        yield
        S.mark(scalar.activation(p_inv, centred, ACT.Exp, scale=DECAY), alone=True)
        S.mark(scalar.activation(carry_scale, carry_scale, ACT.Exp, scale=-DECAY), alone=True)
        yield
        S.wait(before_made)
        made["decays"] = S.mark(scalar.activation(p_before, before, ACT.Exp, scale=-DECAY))
        yield

    def mixed_r():
        made["r"] = yield from mix_split(0, 0)

    def mixed_v():
        made["v"] = yield from mix_split(2, 1)
        made["sel"] = k.load(unit(0)[:, 0:KC * HEADS], A["consts"][:, a_sel:b_sel], made["v"])
        at = k.const_at["headspread"]
        made["headspread"] = k.load(unit(0)[0:HEADS, D:2 * D], A["consts"][0:HEADS, at[0]:at[1]])
    sel = unit(0)[:, 0:KC * HEADS].rearrange("p (c h) -> p c h", h=HEADS)

    def key_chain():
        S.wait(g2_read, kk_scaled)
        for c in (0, KC // 2):
            m = S.mark(scalar.activation(square[:, c * T:(c + 4) * T], kk[:, c:c + 4, :].rearrange("p c t -> p (c t)"),
                                         ACT.Square), alone=True)
            yield
        b, ps = banks.take(PE)
        PE.wait(m, made["sel"])
        for c in range(KC):
            ins = tensor.matmul(ps[0:HEADS, 0:T], sel[:, c, :], square[:, c * T:(c + 1) * T], start=(c == 0),
                                stop=(c == KC - 1))
        sums_done = PE.mark(ins)
        yield
        V.wait(sums_done, made["decays"])
        m = V.mark(vector.tensor_scalar(inverse_norm, ps[0:HEADS, 0:T], 1e-24, None, ALU.max))
        banks.free(b, m)
        made["bonus_sel"] = V.mark(vector.tensor_tensor(sel, sel, spread(col("r_k"), HEADS), ALU.mult))
        S.wait(m)
        root = S.mark(scalar.activation(inverse_norm, inverse_norm, ACT.Sqrt), alone=True)
        S.wait((V.semaphore, V.count))
        for c in range(KC):
            m = S.mark(scalar.activation(rate[:, c * T:(c + 1) * T], aT[:, c, :], ACT.Identity,
                                         scale=col("k_a")[:, c:c + 1], bias=one_less_k_a[:, c:c + 1]), alone=True)
            if c % 4 == 3:
                yield
        V.wait(root)
        inverse_made = V.mark(vector.reciprocal(inverse_norm, inverse_norm), alone=True)
        V.wait(m)
        made["k'"] = V.mark(vector.tensor_tensor(unit(3), unit(3), rate, ALU.mult))
        yield
        for c in range(0, KC, 2):
            b, ps = banks.take(PE)
            PE.wait(inverse_made, made["headspread"])
            for i in range(2):
                ins = tensor.matmul(ps[:, i * T:(i + 1) * T], unit(0)[0:HEADS, D + (c + i) * P:D + (c + i + 1) * P],
                                    inverse_norm, start=True, stop=True)
            done = PE.mark(ins)
            V.wait(done)
            flat = unit(8)[:, c * T:(c + 2) * T]
            m = V.mark(vector.tensor_tensor(flat, flat, ps, ALU.mult), alone=c + 2 < KC)
            banks.free(b, m)
            if c % 4 == 2:
                yield

    def scale_steps():
        rk = fm(unit(13))
        G.wait(made["k'"], r_proj, (PE.semaphore, PE.count))
        rk_made = G.mark(pool.tensor_tensor(rk, rT, kT, ALU.mult))
        V.wait(made["decays"])
        V.mark(vector.tensor_tensor(unit(4), unit(4), unit(8), ALU.mult))
        yield
        V.mark(vector.tensor_tensor(unit(4), unit(4), p_inv, ALU.mult), alone=True)
        yield
        V.mark(vector.scalar_tensor_tensor(out=unit(8), in0=unit(8), scalar=-1.0, in1=p_before, op0=ALU.mult,
                                           op1=ALU.mult), alone=True)
        yield
        b, ps = banks.take(PE)
        PE.wait(rk_made, made["bonus_sel"])
        for tb in range(TB):
            for c in range(KC):
                ins = tensor.matmul(ps[:, tb * HEADS:(tb + 1) * HEADS], rk[:, c, tb * P:(tb + 1) * P], sel[:, c, :],
                                    start=(c == 0), stop=(c == KC - 1))
        bonus_done = PE.mark(ins)
        V.wait(rk_made)
        V.mark(vector.tensor_tensor(unit(3), unit(3), p_inv, ALU.mult), alone=True)
        yield
        made["scaled"] = V.mark(vector.tensor_tensor(unit(2), unit(2), p_in, ALU.mult))
        V.wait(bonus_done)
        made["bonus"] = V.mark(vector.tensor_copy(bonus, ps[:, 0:TB * HEADS]))
        banks.free(b, made["bonus"])
        yield

    kk_scaled = []

    def evac_k(g, ps, ready):
        S.wait(ready)
        m = S.mark(scalar.activation(kT[:, 2 * g:2 * g + 2, :], ps.rearrange("p (c t) -> p c t", t=T), ACT.Copy),
                   alone=True)
        for i in range(2):
            c = 2 * g + i
            m = S.mark(scalar.activation(kk[:, c, :], ps[:, i * T:(i + 1) * T], ACT.Identity,
                                         scale=col("k_k")[:, c:c + 1]), alone=True)
        kk_scaled.append(m)
        return m

    def evac_r(g, ps, ready):
        S.wait(ready)
        return S.mark(scalar.activation(rT[:, 2 * g:2 * g + 2, :], ps.rearrange("p (c t) -> p c t", t=T), ACT.Copy),
                      alone=True)

    W.asides += [mixed_r(), decays()]
    k.project_features(mixed[1], 4, evac_k, first_mix)
    mixed_read[1] = (PE.semaphore, PE.count)
    while "r" not in made:
        W.step_aside()
    W.asides += [mixed_v(), key_chain()]
    r_proj = k.project_features(mixed[0], 4, evac_r, made["r"])
    while "v" not in made:
        W.step_aside()
    W.asides.append(scale_steps())
    v_ready = k.project_tokens(mixed[1], 2, to_tokens(v_tok), made["v"])
    W.finish_aside()
    early.close()
    late = k.sb("late", [P, 2, UNIT], room=room)
    scaled, bonus_ready, p_ready = made["scaled"], made["bonus"], made["decays"]
    r_s, a_s, b_s, k_s = rT, kk, aT, kT

    for src, dst in ((b_s, b_tok), (k_s, k_tok)):
        for c0 in (0, 4):
            b, ps = banks.take(PE)
            PE.wait(scaled)
            for c in range(4):
                ins = tensor.transpose(ps[:, c * P:(c + 1) * P], src[:, c0 + c, 0:P], k.ident)
            m = PE.mark(ins)
            S.wait(m)
            tok_ready = S.mark(scalar.activation(dst[:, c0 * P:(c0 + 4) * P], ps, ACT.Copy), alone=True)
            banks.free(b, tok_ready)

    ln = [late[:, 1, 0:D], late[:, 1, D:2 * D]]
    ln_ready = k.row("ln", late[:, 1, :], (PE.semaphore, PE.count))
    heads4 = lambda buffer, g: buffer[:, g * 4 * P:(g + 1) * 4 * P].rearrange("p (h t) -> p h t", t=P)
    MT, TI, TIT, X = unit(9), unit(10), unit(11), unit(12)
    MAK, MRB, MRK = unit(13), unit(14), unit(0)
    wbuf, ubuf = late[:, 0, 0:D], late[:, 0, D:2 * D]
    y, y2 = unit(5)[:, 0:D], unit(5)[:, D:2 * D]
    y_whole = rT
    read_before = [scaled, (PE.semaphore, PE.count), bonus_ready]

    def pair(c, h, tb, buffer):
        return buffer[h * HD:(h + 1) * HD, c, tb * P:(tb + 1) * P]

    S0 = unit(1)[:, 0:D]
    y_ready, state_ready = [], None

    def per_head(half, terms, dst, ready):
        b, ps = banks.take(PE)
        PE.wait(ready)
        for i in range(8):
            todo = terms(8 * half + i)
            for j, (lhs, rhs) in enumerate(todo):
                ins = tensor.matmul(ps[:, i * HD:(i + 1) * HD], lhs, rhs, start=(j == 0), stop=(j == len(todo) - 1))
        done = PE.mark(ins)
        S.wait(done)
        m = S.mark(scalar.activation(dst[:, half * BANK:(half + 1) * BANK], ps, ACT.Copy), alone=True)
        banks.free(b, m)
        return m

    def mat(buffer, head):
        c, h = head // 2, head % 2
        at = (2 * (c // 4) + h) * 4 + c % 4
        return buffer[:, at * P:(at + 1) * P]

    hd = lambda buffer, head: buffer[:, head * HD:(head + 1) * HD]
    factors_ready = {}

    def output_factors(tb):
        g_of, by_head = g_tok[:, tb, :], lambda b: b.rearrange("p (h i) -> p h i", i=HD)
        G.wait(ln_ready, g_ready, v_ready, bonus_ready, y_ready)
        G.mark(pool.tensor_tensor(by_head(y2), by_head(v_tok[:, tb, :]), spread(bonus[:, tb * HEADS:(tb + 1) * HEADS], HD),
                                  ALU.mult))
        yield
        G.mark(pool.tensor_tensor(y2, y2, ln[1], ALU.add))
        yield
        G.mark(pool.tensor_tensor(y2, y2, g_of, ALU.mult))
        yield
        factors_ready[tb] = G.mark(pool.tensor_tensor(g_of, g_of, ln[0], ALU.mult))
        yield

    def head_norm_steps(tb, half, ready):
        cols = slice(half * BANK, (half + 1) * BANK)
        yh, by_head = y[:, cols], y[:, cols].rearrange("p (h i) -> p h i", i=HD)
        mean, var = stats[:, 16 * half:16 * half + 8], stats[:, 16 * half + 8:16 * half + 16]
        squares = k_s[:, 4 * half:4 * half + 4, tb * P:(tb + 1) * P]
        V.wait(ready)
        V.mark(vector.tensor_reduce(mean, by_head, AX.X, ALU.add))
        V.mark(vector.tensor_scalar(mean, mean, 1.0 / HD, None, ALU.mult))
        yield
        m = V.mark(vector.tensor_tensor(by_head, by_head, spread(mean, HD), ALU.subtract))
        S.wait(m)
        m = S.mark(scalar.activation(squares, yh.rearrange("p (c t) -> p c t", t=P), ACT.Square), alone=True)
        yield
        V.wait(m)
        V.mark(vector.tensor_reduce(var.rearrange("p (c h) -> p c h", h=2),
                                    squares.rearrange("p c (h i) -> p c h i", i=HD), AX.X, ALU.add))
        m = V.mark(vector.tensor_scalar(var, var, 1.0 / HD, 64e-5, ALU.mult, ALU.add))
        m = k.rsqrt(var, 8, m)
        yield
        V.wait(m)
        V.mark(vector.tensor_tensor(by_head, by_head, spread(var, HD), ALU.mult))
        yield
        V.wait(factors_ready[tb])
        V.mark(vector.tensor_tensor(yh, yh, g_tok[:, tb, cols], ALU.mult))
        m = V.mark(vector.tensor_tensor(yh, yh, y2[:, cols], ALU.add))
        yield
        y_ready.append(k.transposed_split(yh.unsqueeze(1), y_whole[:, 4 * half:4 * half + 4, :], m, n=4,
                                          first=4 * half, blocks=[tb]))
        if half == 1 and tb == 0:
            beside.append(output_factors(1))
        yield

    def step_beside():
        if beside and next(beside[0], "over") == "over":
            beside.pop(0)

    beside = [output_factors(0)]
    for tb in range(TB):
        tit_ready = {}
        ti_ready, mt_ready = {}, {}

        def products(pair_of_groups, lhs, rhs):
            got = [banks.take(PE), banks.take(PE)]
            PE.wait(scaled)
            for i in range(4):
                for h in range(2):
                    c = 4 * pair_of_groups + i
                    ins = tensor.matmul(got[h][1][:, i * P:(i + 1) * P], pair(c, h, tb, lhs), pair(c, h, tb, rhs),
                                        start=True, stop=True)
            done = PE.mark(ins)
            return [(2 * pair_of_groups + h, got[h][0], got[h][1].rearrange("p (h t) -> p h t", t=P), done)
                    for h in range(2)]

        for gg in range(2):
            for g, b, ps, done in products(gg, a_s, b_s):
                V.wait(done, read_before)
                m = V.mark(vector.tensor_tensor(heads4(TI, g), ps, across(level[0], 4), ALU.mult), alone=True)
                banks.free(b, m)
                G.wait(m)
                ti_ready[g] = G.mark(pool.tensor_tensor(heads4(TI, g), heads4(TI, g), across(k.ident, 4), ALU.add))
            for g, b, ps, done in products(gg, b_s, a_s):
                S.wait(done, read_before)
                mt_ready[g] = S.mark(scalar.activation(heads4(MT, g), ps, ACT.Copy), alone=True)
                V.wait(mt_ready[g])
                m = V.mark(vector.tensor_tensor(heads4(TIT, g), ps, across(pair_t, 4), ALU.mult), alone=True)
                banks.free(b, m)
                G.wait(m)
                tit_ready[g] = G.mark(pool.tensor_tensor(heads4(TIT, g), heads4(TIT, g), across(k.ident, 4), ALU.add))
            for dst, lhs, rhs, msk in ((MAK, k_s, a_s, strict), (MRB, b_s, r_s, upto), (MRK, k_s, r_s, upto)):
                for g, b, ps, done in products(gg, lhs, rhs):
                    V.wait(done)
                    masked = V.mark(vector.tensor_tensor(heads4(dst, g), ps, across(msk, 4), ALU.mult), alone=True)
                    banks.free(b, masked)
                step_beside()

        def carried(scaled_rows, head):
            if tb == 0:
                return []
            return [(scaled_rows[:, head // 2, tb * P:(tb + 1) * P], hd(S0, head))]

        w_ready = [per_head(half, lambda n: [(mat(MAK, n), hd(v_tok[:, tb, :], n))] + carried(a_s, n), wbuf,
                            [masked, state_ready, v_ready]) for half in range(2)]

        for n in range(1, LEVELS):
            x_done = {}
            for g in range(4):
                b, ps = banks.take(PE)
                PE.wait(mt_ready[g], ti_ready[g])
                for i in range(4):
                    ins = tensor.matmul(ps[:, i * P:(i + 1) * P], heads4(MT, g)[:, i, :], heads4(TI, g)[:, i, :],
                                        start=True, stop=True)
                done = PE.mark(ins)
                V.wait(done, tit_ready[g])
                x_done[g] = V.mark(vector.tensor_tensor(heads4(X, g), ps.rearrange("p (h t) -> p h t", t=P),
                                                        across(level[n], 4), ALU.mult), alone=True)
                banks.free(b, x_done[g])
            for g in range(4):
                old_t, old_tt = ti_ready[g], tit_ready[g]
                b, ps = banks.take(PE)
                b2, ps2 = banks.take(PE)
                PE.wait(x_done[g], old_t, old_tt)
                for i in range(4):
                    ins = tensor.matmul(ps[:, i * P:(i + 1) * P], heads4(X, g)[:, i, :], heads4(TIT, g)[:, i, :],
                                        start=True, stop=True)
                if n < LEVELS - 1:
                    for i in range(4):
                        ins = tensor.matmul(ps2[:, i * P:(i + 1) * P], heads4(TIT, g)[:, i, :], heads4(X, g)[:, i, :],
                                            start=True, stop=True)
                done = PE.mark(ins)
                V.wait(done)
                tit_ready[g] = V.mark(vector.tensor_tensor(heads4(TIT, g), ps.rearrange("p (h t) -> p h t", t=P),
                                                           heads4(TIT, g), ALU.add), alone=True)
                banks.free(b, tit_ready[g])
                if n < LEVELS - 1:
                    ti_ready[g] = V.mark(vector.tensor_tensor(heads4(TI, g), ps2.rearrange("p (h t) -> p h t", t=P),
                                                              heads4(TI, g), ALU.add), alone=True)
                banks.free(b2, ti_ready[g] if n < LEVELS - 1 else tit_ready[g])
                if g % 2:
                    step_beside()

        u_ready = [per_head(half, lambda n: [(mat(TIT, n), hd(wbuf, n))], ubuf,
                            [w_ready[half], tit_ready[2 * half], tit_ready[2 * half + 1]]) for half in range(2)]
        if tb == 0:
            b, ps = banks.take(PE)
            PE.wait(tok_ready, u_ready)
            for head in range(HEADS):
                c, h = head // 2, head % 2
                dst = ps[h * HD:(h + 1) * HD, c * HD:(c + 1) * HD]
                tensor.matmul(dst, hd(b_tok, head), hd(ubuf, head), start=True, stop=False)
                ins = tensor.matmul(dst, hd(k_tok, head), hd(v_tok[:, 0, :], head), start=False, stop=True)
            m = PE.mark(ins)
            V.wait(m, p_ready)
            V.mark(vector.memset(S0, 0.0))
            for h in range(2):
                half = slice(h * HD, (h + 1) * HD)
                state_ready = V.mark(vector.tensor_tensor(
                    S0[half, :].rearrange("p (c h i) -> p c h i", h=2, i=HD)[:, :, h, :],
                    ps[half, :].rearrange("p (c i) -> p c i", i=HD),
                    carry_scale[half, :].unsqueeze(2).to_broadcast([HD, KC, HD]), ALU.mult))
            banks.free(b, state_ready)
        for half in range(2):
            done_y = per_head(half, lambda n: [(mat(MRB, n), hd(ubuf, n)), (mat(MRK, n), hd(v_tok[:, tb, :], n))]
                              + carried(r_s, n), y, [u_ready[half], masked])
            beside.append(head_norm_steps(tb, half, done_y))
        read_before = [(PE.semaphore, PE.count)]
    while beside:
        beside[:] = [steps for steps in beside if next(steps, "over") != "over"]

    out = {}

    def evac(tb, g, ps, ready):
        out[tb] = k.add_to_x(tb, g * BANK, ps, 1.0, ready)
        return out[tb]
    k.project_tokens(k.hT, 2, evac, y_ready)
    room.close()
    return [out[0], out[1]]


def head_norm(k, buffer, heads, eps, square, ss, ready, width=HD):
    V, vector = k.V, k.vector
    by_head = lambda b: b.rearrange("p (h i) -> p h i", i=width)
    V.wait(ready)
    V.mark(vector.tensor_tensor(square, buffer, buffer, ALU.mult))
    yield
    V.mark(vector.tensor_reduce(ss, by_head(square), AX.X, ALU.add))
    m = V.mark(vector.tensor_scalar(ss, ss, 1.0 / width, eps, ALU.mult, ALU.add))
    m = k.rsqrt(ss, heads, m)
    yield
    V.wait(m)
    return V.mark(vector.tensor_tensor(by_head(buffer), by_head(buffer), k.spread(ss, width), ALU.mult))


def finished(steps):
    while True:
        try:
            next(steps)
        except StopIteration as end:
            return end.value


def shared_kv(k, x_ready, keep):
    V, S, W, fm, tm, scalar = k.V, k.S, k.W, k.fm, k.tm, k.scalar
    shared = k.sb("shared_kv", [P, 2, UNIT], room=keep)
    kT, v_tok = fm(shared[:, 0, :]), tm(shared[:, 1, :])
    with ExitStack() as room:
        scratch = k.sb("kv_scratch", [P, 3, UNIT], room=room)
        k.fence()
        h_ready = k.norm(k.col("kv_norm"), x_ready, fm(scratch[:, 0, :]), tm(scratch[:, 1, :]))
        k_tok = tm(scratch[:, 2, :])
        keys_ready = []

        def key_steps(tb, g, ready):
            mine = k_tok[:, tb, g * BANK:(g + 1) * BANK]
            m = yield from head_norm(k, mine, 8, 1e-6, scratch[:, 0, 0:BANK], k.small[:, 64:72], ready)
            yield
            keys_ready.append(k.transposed(mine, tb, kT[:, 4 * g:4 * g + 4, :], m, n=4,
                                           scale=(k.col("k_norm", 0, 1), 1.0)))

        def evac(tb, g, ps, ready):
            S.wait(ready)
            dst = k_tok if g < 2 else v_tok
            m = S.mark(scalar.activation(dst[:, tb, g % 2 * BANK:(g % 2 + 1) * BANK], ps, ACT.Copy), alone=True)
            if g < 2:
                W.asides.append(key_steps(tb, g, [m, h_ready]))
            return m
        marks = k.project_tokens(k.hT, 4, evac, h_ready)
        W.finish_aside()
    return (kT, v_tok), keys_ready + [marks[-1]]


def attention(k, units, turned_at, beside=None, out=None, by_vector=()):
    PE, V, S, banks, tensor, scalar = k.PE, k.V, k.S, k.banks, k.tensor, k.scalar
    out = [] if out is None else out

    def stages(n, scores, soften, values):
        scored = scores()
        yield
        weights, keys, ready = yield from soften(n, *scored)
        PE.wait(ready)
        b, ps = banks.take(PE)
        for c in range(keys // P):
            ins = tensor.transpose(ps[:, c * P:(c + 1) * P], weights[:, c * P:(c + 1) * P], k.ident)
        done = PE.mark(ins)
        k.weights_read[n] = done
        yield
        turned = turned_at[:, (n % 4) * BANK:(n % 4) * BANK + keys]
        if n in by_vector:
            V.wait(done)
            m = V.mark(k.vector.tensor_copy(turned, ps[:, 0:keys]), alone=True)
        else:
            S.wait(done)
            m = S.mark(scalar.activation(turned, ps[:, 0:keys], ACT.Copy), alone=True)
        banks.free(b, m)
        PE.wait(m)
        b, done, take_out = values(turned.rearrange("p (c q) -> p c q", q=P))
        yield
        S.wait(done)
        m = S.mark(take_out(), alone=True)
        banks.free(b, m)
        out.append(m)

    k.weights_read = {}
    live, waiting = [], [stages(n, *unit) for n, unit in enumerate(units)]
    while live or waiting:
        if waiting:
            live.append(waiting.pop(0))
        live = [unit for unit in live if next(unit, "over") != "over"]
        if beside is not None:
            next(beside, None)
    for _ in beside or ():
        pass
    return out


def diff_attention(k, x_ready, shared, kv_ready):
    PE, V, S, W, banks, fm, tm = k.PE, k.V, k.S, k.W, k.banks, k.fm, k.tm
    tensor, vector, scalar, hT = k.tensor, k.vector, k.scalar, k.hT
    room = ExitStack()
    arena = k.sb("differential", [P, 10, UNIT], room=room)
    dist = k.sb("causal_dist", [P, 3 * P], room=room)[:, :]
    k.fence()

    def unit(i):
        return arena[:, i, :]
    lam_init = 0.8 - 0.6 * math.exp(-0.3 * 1)
    kT, v_tok = shared
    h_ready = k.norm(k.col("mix_norm", 1), x_ready, fm(unit(0)), tm(unit(1)))
    a0 = k.const_at["causal_dist"][0]
    dist_ready = k.load(dist, k.A["consts"][:, a0:a0 + 3 * P], x_ready)

    lam = unit(3)[:, 0:4 * HD]
    lam_loaded = k.row("lam", lam, x_ready)
    sums, neg_lam = k.small[:, 16:18], k.small[:, 18:19]
    V.wait(lam_loaded)
    pairs = lam.rearrange("p (a b i) -> p a b i", a=2, b=2)
    V.mark(vector.tensor_tensor(unit(3)[:, BANK:BANK + 2 * HD].rearrange("p (a i) -> p a i", a=2), pairs[:, :, 0, :],
                                pairs[:, :, 1, :], ALU.mult))
    m = V.mark(vector.tensor_reduce(sums, unit(3)[:, BANK:BANK + 2 * HD].rearrange("p (a i) -> p a i", a=2), AX.X,
                                    ALU.add))
    S.wait(m)
    m = S.mark(scalar.activation(sums, sums, ACT.Exp))
    V.wait(m)
    V.mark(vector.tensor_tensor(neg_lam, sums[:, 1:2], sums[:, 0:1], ALU.subtract))
    lam_ready = V.mark(vector.tensor_scalar(neg_lam, neg_lam, lam_init, None, ALU.subtract))

    q_tok, qT = tm(unit(1)), fm(unit(4))
    q_ready = []

    def query_steps(tb, g, ready):
        mine = q_tok[:, tb, g * BANK:(g + 1) * BANK]
        m = yield from head_norm(k, mine, 8, 1e-6, unit(2)[:, 0:BANK], k.small[:, 64:72], ready)
        yield
        q_ready.append(k.transposed(mine, tb, qT[:, 4 * g:4 * g + 4, :], m, n=4,
                                    scale=(k.col("q_norm", 0, 1), HD ** -0.5)))

    def evac_q(tb, g, ps, ready):
        S.wait(ready)
        m = S.mark(scalar.activation(q_tok[:, tb, g * BANK:(g + 1) * BANK], ps, ACT.Copy), alone=True)
        W.asides.append(query_steps(tb, g, m))
        return m
    k.project_tokens(hT, 2, evac_q, h_ready)
    W.finish_aside()

    work = lambda i: unit(5 + i % 4)
    o_tok = tm(unit(1))
    stat = lambda i: k.small[:, 64 + 8 * (i % 4):72 + 8 * (i % 4)]

    def unit_of(h, qb):
        n = (qb + 1) * P
        slope = 2.0 ** (-8.0 * (h + 1) / DH)

        def scores():
            got = [banks.take(PE), banks.take(PE)]
            PE.wait(q_ready, kv_ready)
            for m in range(2):
                rows = slice(m * HD, (m + 1) * HD)
                ins = tensor.matmul(got[m][1][:, 0:n], qT[rows, h, qb * P:(qb + 1) * P], kT[rows, h, 0:n],
                                    start=True, stop=True)
            return got, PE.mark(ins)

        def soften(i, got, ready):
            s = work(i)[:, 0:2 * T].rearrange("p (m k) -> p m k", m=2)[:, :, 0:n]
            st = stat(i)
            V.wait(ready, dist_ready, lam_ready, k.weights_read.get(i - 4))
            for m in range(2):
                done = V.mark(vector.scalar_tensor_tensor(out=s[:, m, :], in0=dist[:, qb * P:qb * P + n],
                                                          scalar=slope, in1=got[m][1][:, 0:n], op0=ALU.mult,
                                                          op1=ALU.add), alone=m == 0)
                banks.free(got[m][0], done)
            top = V.mark(vector.tensor_reduce(st[:, 0:2], s, AX.X, ALU.max, negate=True), alone=True)
            yield
            S.wait(top)
            for m in range(2):
                e = S.mark(scalar.activation(s[:, m, :], s[:, m, :], ACT.Exp, bias=st[:, m:m + 1],
                                             accum_out=st[:, 2 + m:3 + m]), alone=True)
            yield
            V.wait(e)
            V.mark(vector.reciprocal(st[:, 4:6], st[:, 2:4]))
            V.mark(vector.tensor_scalar(s[:, 1, :], s[:, 1, :], st[:, 5:6], neg_lam, ALU.mult, ALU.mult))
            weights = work(i)[:, 2 * T:2 * T + n]
            m = V.mark(vector.scalar_tensor_tensor(out=weights, in0=s[:, 0, :], scalar=st[:, 4:5], in1=s[:, 1, :],
                                                   op0=ALU.mult, op1=ALU.add))
            return weights, n, m

        def values(turned):
            b, ps = banks.take(PE)
            for c in range(qb + 1):
                ins = tensor.matmul(ps[:, 0:P], turned[:, c, :], v_tok[:, c, h * P:(h + 1) * P], start=(c == 0),
                                    stop=(c == qb))
            take_out = lambda: scalar.activation(o_tok[:, qb, h * P:(h + 1) * P], ps[:, 0:P], ACT.Copy)
            return b, PE.mark(ins), take_out
        return scores, soften, values

    o_ready = []

    def output_steps(attended):
        for first in (0, DH // 2):
            while len(attended) < (first + DH // 2) * TB:
                yield
            normed = []
            for tb in range(TB):
                mine = o_tok[:, tb, first * P:(first + DH // 2) * P]
                normed.append((yield from head_norm(k, mine, DH // 2, 1e-5, unit(2)[:, tb * BANK:(tb + 1) * BANK],
                                                    k.small[:, 128 + 4 * tb:132 + 4 * tb], list(attended), width=P)))
                yield
            o_ready.append(k.transposed_split(o_tok[:, :, first * P:(first + DH // 2) * P],
                                              fm(unit(0))[:, first:first + DH // 2, :], None, first=first, n=DH // 2,
                                              scale=(k.col("subln", 0, 1), 1.0 - lam_init), each=normed))
    attended = []
    attention(k, [unit_of(h, qb) for h in range(DH) for qb in range(TB)], unit(9), output_steps(attended), attended)
    out = {}

    def evac(tb, g, ps, ready):
        out[tb] = k.add_to_x(tb, g * BANK, ps, 1.0, ready)
        return out[tb]
    k.project_tokens(hT, 2, evac, o_ready)
    room.close()
    return [out[0], out[1]]


def mix_2(k, x_ready):
    PE, V, S, W, banks, fm, tm = k.PE, k.V, k.S, k.W, k.banks, k.fm, k.tm
    tensor, vector, scalar, hT = k.tensor, k.vector, k.scalar, k.hT
    room = ExitStack()
    arena = k.sb("second_mix", [P, 15, UNIT], room=room)
    masks = k.sb("attention_masks", [P, 9 * P], room=room)
    k.fence()

    def unit(i):
        return arena[:, i, :]
    at = k.const_at
    window, before, before_neg = (masks[:, i * 3 * P:(i + 1) * 3 * P] for i in range(3))
    a = at["window_dist"][0]
    tables = k.load(masks[:, :], k.A["consts"][:, a:a + 9 * P], x_ready)
    bias = unit(0)
    bias_ready = k.row("gate_bias", bias, x_ready)
    sinks = k.small[:, 16:24]
    sinks_ready = k.row("sinks", sinks, x_ready)
    h_ready = k.norm(k.col("mix_gain_2"), x_ready, fm(unit(8)), tm(unit(9)))

    q_a, kv_a = unit(1).rearrange("p (b c) -> p b c", b=TB)[:, :, 0:BANK], unit(2)[:, 0:2 * T].rearrange(
        "p (b c) -> p b c", b=TB)
    k_dup = unit(2)[:, 2 * T:4 * T].rearrange("p (b g d i) -> p b g d i", b=TB, g=2, d=2)
    qbT, kbT = fm(unit(3))[:, 0:4, :], fm(unit(3))[:, 4:8, :]
    v_b = unit(4)[:, 0:D].rearrange("p (b c) -> p b c", b=TB)
    gates = [unit(5), unit(6)]
    qaT, kaT = fm(unit(7))[:, 0:4, :], fm(unit(7))[:, 4:6, :]

    def copy_to(dst, scale=None):
        def evac(tb, g, ps, ready):
            S.wait(ready)
            return S.mark(scalar.activation(dst[:, tb, :], ps, ACT.Copy))
        return evac

    qa_ready, ka_ready = [], []

    def query_steps(tb, ready):
        m = yield from head_norm(k, q_a[:, tb, :], 8, 1e-6, unit(8)[:, 0:BANK], k.small[:, 64:72], ready)
        yield
        qa_ready.append(k.transposed(q_a[:, tb, :], tb, qaT, m, n=4, scale=(k.col("swa_q", 0, 1), HD ** -0.5)))

    def key_steps(tb, ready):
        m = yield from head_norm(k, kv_a[:, tb, 0:P], 2, 1e-6, unit(8)[:, 0:P], k.small[:, 64:66], ready)
        V.wait(m)
        for g in range(2):
            m = V.mark(vector.tensor_copy(k_dup[:, tb, g, :, :], k.across(kv_a[:, tb, g * HD:(g + 1) * HD], 2)))
        yield
        ka_ready.append(k.transposed(k_dup[:, tb, :, :, :].rearrange("p g d i -> p (g d i)"), tb, kaT, m, n=2,
                                     scale=(k.col("swa_k", 0, 1), 1.0)))
    qa_marks = k.project_tokens(hT, 1, copy_to(q_a), h_ready)
    W.asides += [query_steps(tb, [qa_marks[tb], h_ready]) for tb in range(TB)]
    got = [banks.take(PE) for _ in range(TB)]
    for k0 in range(0, KC, 4):
        tile = tuple(t.rearrange("p (k n) -> p k n", k=4) for t in W.take(PE))
        for tb in range(TB):
            for c in range(4):
                ins = k.products(got[tb][1][:, 0:T], k.at(hT, slice(None), k0 + c, slice(tb * P, (tb + 1) * P)),
                                 k.at(tile, slice(None), c, slice(None)), k0 + c == 0, k0 + c == KC - 1)
        done = PE.mark(ins)
        W.release(done)
    S.wait(done)
    for tb in range(TB):
        kva_ready = S.mark(scalar.activation(kv_a[:, tb, :], got[tb][1][:, 0:T], ACT.Copy), alone=True)
        banks.free(got[tb][0], kva_ready)
        W.asides.append(key_steps(tb, kva_ready))

    def evac_qk(g, ps, ready):
        S.wait(ready)
        src = ps.rearrange("p (c t) -> p c t", t=T)
        if g < 2:
            return S.mark(scalar.activation(qbT[:, 2 * g:2 * g + 2, :], src, ACT.Copy, scale=HD ** -0.5))
        return S.mark(scalar.activation(kbT[:, 2 * g - 4:2 * g - 2, :], src, ACT.Copy))
    qkb_ready = k.project_features(hT, 4, evac_qk, h_ready)
    vb_ready = k.project_tokens(hT, 1, copy_to(v_b), h_ready)
    W.finish_aside()

    gates_ready = []

    def gate_steps():
        for g in range(4):
            for k0 in range(0, KC, 2):
                tile = tuple(t.rearrange("p (k n) -> p k n", k=2) for t in W.take(PE))
                for tb in range(TB):
                    PE.wait(banks.freed[tb])
                    for c in range(2):
                        ins = k.products(k.psum[:, tb, :], k.at(hT, slice(None), k0 + c, slice(tb * P, (tb + 1) * P)),
                                         k.at(tile, slice(None), c, slice(None)), k0 + c == 0, k0 + c == KC - 1)
                done = PE.mark(ins)
                W.release(done)
                yield
            for tb in range(TB):
                dst = gates[tb][:, g * BANK:(g + 1) * BANK]
                V.wait(done, bias_ready)
                m = V.mark(vector.tensor_tensor(dst, k.psum[:, tb, :], bias[:, g * BANK:(g + 1) * BANK], ALU.add),
                           alone=True)
                banks.free(tb, m)
            S.wait(m)
            for tb in range(TB):
                dst = gates[tb][:, g * BANK:(g + 1) * BANK]
                gates_ready.append(S.mark(scalar.activation(dst, dst, ACT.Sigmoid), alone=True))

    ya, yb = tm(unit(9))[:, :, 0:BANK], tm(unit(9))[:, :, BANK:D]
    work = lambda i: unit(10 + i % 4)
    stat = lambda i: k.small[:, 64 + 16 * (i % 4):80 + 16 * (i % 4)]

    def pair_of_heads(c, qb, qT, kT, kchunk, ready, soften_pair, v, v_column, dst):
        n = (qb + 1) * P

        def scores():
            got = [banks.take(PE), banks.take(PE)]
            PE.wait(ready)
            for h in range(2):
                rows = slice(h * HD, (h + 1) * HD)
                ins = tensor.matmul(got[h][1][:, 0:n], qT[rows, c, qb * P:(qb + 1) * P], kT[rows, kchunk, 0:n],
                                    start=True, stop=True)
            return got, PE.mark(ins)

        def values(turned):
            b, ps = banks.take(PE)
            blocks = qb + 1
            for h in range(2):
                for j in range(blocks):
                    ins = tensor.matmul(ps[:, h * HD:(h + 1) * HD], turned[:, h * blocks + j, :],
                                        v[:, j, v_column(2 * c + h):v_column(2 * c + h) + HD], start=(j == 0),
                                        stop=(j == blocks - 1))
            take_out = lambda: scalar.activation(dst[:, qb, 2 * c * HD:(2 * c + 2) * HD], ps[:, 0:P], ACT.Copy)
            return b, PE.mark(ins), take_out
        return scores, lambda i, got, done: soften_pair(i, c, qb, n, got, done), values

    def soften_window(i, c, qb, n, got, ready):
        s = work(i)[:, 0:2 * n].rearrange("p (h k) -> p h k", h=2)
        st = stat(i)
        V.wait(ready, tables, sinks_ready, k.weights_read.get(i - 4))
        for h in range(2):
            slope = 2.0 ** (-8.0 * (2 * c + h + 1) / 8)
            done = V.mark(vector.scalar_tensor_tensor(out=s[:, h, :], in0=window[:, qb * P:qb * P + n], scalar=slope,
                                                      in1=got[h][1][:, 0:n], op0=ALU.mult, op1=ALU.add),
                          alone=h == 0)
            banks.free(got[h][0], done)
        V.mark(vector.tensor_reduce(st[:, 0:2], s, AX.X, ALU.max))
        sink = sinks[:, 2 * c:2 * c + 2]
        V.mark(vector.tensor_tensor(st[:, 0:2], st[:, 0:2], sink, ALU.max))
        V.mark(vector.tensor_tensor(st[:, 2:4], sink, st[:, 0:2], ALU.subtract))
        m = V.mark(vector.tensor_scalar(st[:, 0:2], st[:, 0:2], -1.0, None, ALU.mult), alone=True)
        yield
        S.wait(m)
        S.mark(scalar.activation(st[:, 2:4], st[:, 2:4], ACT.Exp), alone=True)
        for h in range(2):
            m = S.mark(scalar.activation(s[:, h, :], s[:, h, :], ACT.Exp, bias=st[:, h:h + 1],
                                         accum_out=st[:, 4 + h:5 + h]), alone=True)
        yield
        V.wait(m)
        V.mark(vector.tensor_tensor(st[:, 4:6], st[:, 4:6], st[:, 2:4], ALU.add))
        V.mark(vector.reciprocal(st[:, 4:6], st[:, 4:6]))
        for h in range(2):
            m = V.mark(vector.tensor_scalar(s[:, h, :], s[:, h, :], st[:, 4 + h:5 + h], None, ALU.mult), alone=True)
        return work(i)[:, 0:2 * n], 2 * n, m

    def soften_stick(i, c, qb, n, got, ready):
        z, e, lb, keep = (work(i)[:, j * 2 * T:j * 2 * T + 2 * n].rearrange("p (h k) -> p h k", h=2)
                          for j in range(4))
        pre = e
        V.wait(ready, tables, k.weights_read.get(i - 4))
        for h in range(2):
            done = V.mark(vector.tensor_copy(z[:, h, :], got[h][1][:, 0:n]), alone=True)
            banks.free(got[h][0], done)
        yield
        S.wait(done)
        S.mark(scalar.activation(e, z, ACT.Abs))
        S.mark(scalar.activation(e, e, ACT.Exp, scale=-1.0))
        m = S.mark(scalar.activation(e, e, ACT.Ln, bias=1.0), alone=True)
        yield
        V.wait(m)
        V.mark(vector.scalar_tensor_tensor(out=lb, in0=z, scalar=0.0, in1=e, op0=ALU.min, op1=ALU.subtract))
        V.mark(vector.tensor_tensor(keep, lb, z, ALU.subtract))
        V.mark(vector.tensor_tensor(keep, keep, k.across(before[:, qb * P:qb * P + n], 2), ALU.mult))
        for h in range(2):
            V.mark(vector.tensor_tensor_scan(pre[:, h, :], keep[:, h, :], keep[:, h, :], 0.0, ALU.add, ALU.bypass),
                   alone=h == 0)
        V.mark(vector.tensor_tensor(lb, lb, k.across(before_neg[:, qb * P:qb * P + n], 2), ALU.add))
        m = V.mark(vector.tensor_tensor(lb, lb, pre, ALU.subtract), alone=True)
        yield
        S.wait(m)
        for h in range(2):
            m = S.mark(scalar.activation(lb[:, h, :], lb[:, h, :], ACT.Exp, bias=pre[:, h, n - 1:n]), alone=True)
        return work(i)[:, 4 * T:4 * T + 2 * n], 2 * n, m

    units = []
    for c in range(4):
        for qb in range(TB):
            units.append(pair_of_heads(c, qb, qaT, kaT, c // 2, [qa_ready, ka_ready], soften_window,
                                       kv_a, lambda h: P + h // 4 * HD, ya))
            units.append(pair_of_heads(c, qb, qbT, kbT, c, qkb_ready, soften_stick, v_b, lambda h: h * HD, yb))
    banks.use(range(2, 8))
    PE.wait(vb_ready, kva_ready)
    attended = attention(k, units, unit(14), gate_steps(), by_vector=range(0, len(units), 2))
    banks.use(range(8))

    merged, part = tm(unit(8)), unit(10)[:, 0:BANK]
    whole = fm(unit(11))
    PE_done = (PE.semaphore, PE.count)
    ready = [attended, PE_done]
    turned = []
    for y, first in ((ya, 0), (yb, 4)):
        turned.append(k.transposed_split(y, whole[:, first:first + 4, :], ready, first=first, n=4))

    def evac_a(tb, g, ps, ready):
        V.wait(ready, gates_ready)
        cols = slice(g * BANK, (g + 1) * BANK)
        return V.mark(vector.tensor_tensor(merged[:, tb, cols], ps, gates[tb][:, cols], ALU.mult))

    def evac_b(tb, g, ps, ready):
        V.wait(ready, gates_ready)
        cols = slice(g * BANK, (g + 1) * BANK)
        m = V.mark(vector.tensor_tensor(part, ps, gates[tb][:, D + g * BANK:D + (g + 1) * BANK], ALU.mult))
        V.mark(vector.tensor_tensor(merged[:, tb, cols], merged[:, tb, cols], part, ALU.add))
        return m
    k.project_tokens(hT, 2, evac_a, turned[0], kcs=4)
    k.project_tokens(hT, 2, evac_b, turned[1], kcs=4, first=4)
    merged_ready = (V.semaphore, V.count)
    ready = k.transposed_split(merged, whole, [merged_ready, (PE.semaphore, PE.count)])
    out = {}

    def evac(tb, g, ps, ready):
        out[tb] = k.add_to_x(tb, g * BANK, ps, 1.0, ready)
        return out[tb]
    k.project_tokens(hT, 2, evac, ready)
    room.close()
    return [out[0], out[1]]


def top_sixteen(k, jobs):
    V, vector = k.V, k.vector
    rounds = (lambda values, spare, top, index: vector.max(top[:, 0:8], values),
              lambda values, spare, top, index: vector.max_index(index[:, 0:8], top[:, 0:8], values),
              lambda values, spare, top, index: vector.match_replace(spare, top[:, 0:8], values, -3.0e38),
              lambda values, spare, top, index: vector.max(top[:, 8:16], spare),
              lambda values, spare, top, index: vector.max_index(index[:, 8:16], top[:, 8:16], spare))
    before = [None] * len(jobs)
    for n, step in enumerate(rounds):
        for i, job in enumerate(jobs):
            V.wait(before[i])
            before[i] = V.mark(step(*job), alone=True)
        if n in (1, 3):
            yield
    V.wait(before[-1])


def experts(k, x_ready):
    PE, V, S, G, W, banks, tm = k.PE, k.V, k.S, k.G, k.W, k.banks, k.tm
    tensor, vector, scalar, pool, hT, psum = k.tensor, k.vector, k.scalar, k.pool, k.hT, k.psum
    SETS = 2 * PH
    HALF = KEYS // 2
    room = ExitStack()
    picked = k.sb("picked", [P, 3, T], room=room)
    iota = k.sb("iota", [P, P], room=room)[:, :]
    active = k.sb("active", [P, KEYS, T], room=room)
    onehot = k.sb("onehot", [P, 2, 4 * (KEYS + HALF)], room=room)
    unit = lambda n: active[:, 8 * n:8 * n + 8, :].rearrange("p j t -> p (j t)")
    PICKS_UNTIL = 8 * 7
    k.fence()
    iota_ready = k.load(iota, k.A["consts"][:, P:2 * P], x_ready)
    keys = unit(7)
    loaded = k.load(keys, k.A["sub_keys"], x_ready)
    keys = keys.rearrange("p (s k) -> p s k", k=KEYS)
    h_ready = k.norm(k.col("ffn_gain_2"), x_ready, k.fm(unit(0)), tm(unit(1)))

    qT = active[:, 8 * 8:8 * 10, :]
    score = [unit(12 + tb).rearrange("p (s k) -> p s k", k=KEYS) for tb in range(TB)]
    picked_ready, negated_ready = [], []

    def base_of(tb):
        return unit(14 + tb), unit(10 + tb)

    def top_of(tb):
        base, _ = base_of(tb)
        return (base[:, 0:T].rearrange("p (h s n) -> p h s n", h=PH, s=2),
                base[:, T:2 * T].bitcast(U32).rearrange("p (h s n) -> p h s n", h=PH, s=2))

    def score_steps(h, ready):
        PE.wait(ready, loaded)
        b, ps = banks.take(PE)
        for tb in range(TB):
            for s in range(2):
                ins = tensor.matmul(ps[:, (2 * tb + s) * KEYS:(2 * tb + s + 1) * KEYS],
                                    qT[:, 2 * h + s, tb * P:(tb + 1) * P], keys[:, 2 * h + s, :], start=True, stop=True)
        done = PE.mark(ins)
        yield
        S.wait(done)
        for tb in range(TB):
            m = S.mark(scalar.activation(score[tb][:, 2 * h:2 * h + 2, :],
                                         ps[:, tb * T:(tb + 1) * T].rearrange("p (s k) -> p s k", k=KEYS), ACT.Copy),
                       alone=True)
        banks.free(b, m)
        V.wait(m)
        yield from top_sixteen(k, [(score[tb][:, 2 * h + s, :], base_of(tb)[1][:, (2 * h + s) * KEYS:(2 * h + s + 1) * KEYS],
                                    top_of(tb)[0][:, h, s, :], top_of(tb)[1][:, h, s, :])
                                   for tb in range(TB) for s in range(2)])

    def picks(tb):
        base, spare = base_of(tb)
        top, _ = top_of(tb)
        index = base[:, 2 * T:3 * T].rearrange("p (h s n) -> p h s n", h=PH, s=2)
        best = base[:, 3 * T:3 * T + P].rearrange("p (h n) -> p h n", h=PH)
        position = base[:, 3 * T + P:4 * T].bitcast(U32)
        part = [base[:, 4 * T + i * P:4 * T + (i + 1) * P] for i in range(2)]
        raw = base[:, 5 * T:5 * T + P].bitcast(U32)
        gate = base[:, 5 * T + P:6 * T].rearrange("p (h n) -> p h n", h=PH)
        chosen = [base[:, 6 * T + i * P:6 * T + (i + 1) * P] for i in range(2)]
        total = base[:, 7 * T:7 * T + PH]
        V.mark(vector.tensor_copy(base[:, 2 * T:3 * T], base[:, T:2 * T].bitcast(U32)), alone=True)
        for h0 in range(0, PH, 4):
            jobs = []
            for n in range(4):
                h, sums, left = h0 + n, spare[:, 2 * n * T:(2 * n + 1) * T], spare[:, (2 * n + 1) * T:(2 * n + 2) * T]
                V.mark(vector.tensor_tensor(sums.rearrange("p (a b) -> p a b", b=TOP), k.spread(top[:, h, 0, :], TOP),
                                            k.across(top[:, h, 1, :], TOP), ALU.add), alone=n < 3)
                jobs.append((sums, left, best[:, h, :], position[:, h * TOP:(h + 1) * TOP]))
            yield
            yield from top_sixteen(k, jobs)
            yield
        V.wait(iota_ready)
        for side, op, by in ((0, ALU.logical_shift_right, 4), (1, ALU.bitwise_and, TOP - 1)):
            V.mark(vector.tensor_scalar(raw, position, by, None, op))
            V.mark(vector.tensor_copy(part[side], raw))
            for heads in (slice(0, PH // 2), slice(PH // 2, PH)):
                mine = slice(heads.start * TOP, heads.stop * TOP)
                flat = spare.rearrange("p (m n) -> p m n", n=TOP)[:, mine, :]
                hit = spare.rearrange("p (h m n) -> p h m n", h=PH, n=TOP)[:, heads, :, :]
                V.mark(vector.tensor_tensor(flat, k.spread(part[side][:, mine], TOP), k.across(iota[:, 0:TOP], P // 2),
                                            ALU.is_equal))
                yield
                V.mark(vector.tensor_tensor(hit, hit, index[:, heads, side, :].unsqueeze(2).to_broadcast(
                    [P, PH // 2, TOP, TOP]), ALU.mult))
                yield
                V.mark(vector.tensor_reduce(chosen[side][:, mine], flat, AX.X, ALU.add))
                yield
        m = V.mark(vector.tensor_tensor(gate, best, best[:, :, 0:1].to_broadcast([P, PH, TOP]), ALU.subtract))
        S.wait(m)
        m = S.mark(scalar.activation(gate, gate, ACT.Exp))
        yield
        V.wait(m)
        V.mark(vector.tensor_reduce(total, gate, AX.X, ALU.add))
        V.mark(vector.reciprocal(total, total))
        m = V.mark(vector.tensor_tensor(gate, gate, k.spread(total, TOP), ALU.mult))
        yield
        b, ps = banks.take(PE)
        PE.wait(m)
        for i, src in enumerate((base[:, 5 * T + P:6 * T], chosen[0], chosen[1])):
            ins = tensor.transpose(ps[:, i * P:(i + 1) * P], src, k.ident)
        m = PE.mark(ins)
        yield
        V.wait(m)
        picked_ready.append(V.mark(vector.tensor_copy(picked[:, :, tb * P:(tb + 1) * P],
                                                      ps[:, 0:3 * P].rearrange("p (w t) -> p w t", w=3))))
        banks.free(b, picked_ready[-1])
        if tb == TB - 1:
            negated_ready.append(V.mark(vector.tensor_scalar(negated, lots[:, 0, :, lot - 1], -1.0, None, ALU.mult)))
        yield

    lot = 4
    negated = k.small[:, 128:128 + T // lot]
    lots = picked.rearrange("p w (q n) -> p w q n", n=lot)

    def weigh(j0, activated, weighed):
        hots_read, begun, made, products = {}, {}, {}, {}
        while not activated:
            yield
        for lane in (V, S, G):
            lane.wait(negated_ready, (lane.semaphore, lane.count), (PE.semaphore, PE.count))
        G.wait(picked_ready, iota_ready)
        for q in range(T // lot + 3):
            if 3 <= q:
                b, ps, done = products.pop(q - 3)
                V.wait(done, activated[0])
                a = active[:, j0:j0 + HALF, (q - 3) * lot:(q - 2) * lot].rearrange("p j t -> p t j")
                m = V.mark(vector.tensor_tensor(a, ps[:, 0:lot * HALF].rearrange("p (t j) -> p t j", t=lot), a,
                                                ALU.mult), alone=True)
                banks.free(b, m)
            if 2 <= q < T // lot + 2:
                i_hot, j_hot, hots_made = made.pop(q - 2)
                b, ps = banks.take(PE)
                PE.wait(hots_made)
                for n in range(lot):
                    ins = tensor.matmul(ps[:, n * HALF:(n + 1) * HALF], i_hot[:, n, :], j_hot[:, n, :], start=True,
                                        stop=True)
                hots_read[q - 2] = PE.mark(ins)
                products[q - 2] = (b, ps, hots_read[q - 2])
            if 1 <= q < T // lot + 1:
                i_hot, j_hot, mj = begun.pop(q - 1)
                V.wait(hots_read.get(q - 3))
                S.wait(hots_read.get(q - 3))
                for n in range(lot - 1):
                    t = (q - 1) * lot + n
                    mi = V.mark(vector.tensor_scalar(i_hot[:, n, :], iota, picked[:, 1, t:t + 1], picked[:, 0, t:t + 1],
                                                     ALU.is_equal, ALU.mult), alone=True)
                t = q * lot - 1
                last = i_hot[:, lot - 1, :]
                S.mark(scalar.activation(last, iota, ACT.Abs, scale=-1.0, bias=picked[:, 1, t:t + 1]))
                S.mark(scalar.activation(last, last, ACT.Relu, scale=negated[:, q - 1:q], bias=picked[:, 0, t:t + 1]),
                       alone=True)
                S.wait(mj)
                S.mark(scalar.activation(j_hot, j_hot, ACT.Abs))
                mj = S.mark(scalar.activation(j_hot, j_hot, ACT.Relu, scale=-1.0, bias=1.0), alone=True)
                made[q - 1] = (i_hot, j_hot, [mi, mj])
            if q < T // lot:
                i_hot = onehot[:, q % 2, 0:lot * KEYS].rearrange("p (t i) -> p t i", t=lot)
                j_hot = onehot[:, q % 2, lot * KEYS:lot * (KEYS + HALF)].rearrange("p (t j) -> p t j", t=lot)
                G.wait(hots_read.get(q - 2))
                mj = G.mark(pool.tensor_tensor(j_hot, k.across(iota[:, j0:j0 + HALF], lot),
                                               k.spread(picked[:, 2, q * lot:(q + 1) * lot], HALF), ALU.subtract),
                            alone=True)
                begun[q] = (i_hot, j_hot, mj)
            yield
        weighed.append(m)

    def evac_q(g, ps, ready):
        S.wait(ready)
        m = S.mark(scalar.activation(qT[:, 2 * g:2 * g + 2, :], ps.rearrange("p (c t) -> p c t", t=T), ACT.Copy),
                   alone=True)
        W.asides.append(score_steps(g, m))
        return m
    k.project_features(hT, PH, evac_q, h_ready)

    first_activated, last_activated, first_weighed, last_weighed = [], [], [], []
    W.asides += [picks(0), picks(1), weigh(0, first_activated, first_weighed)]
    S.wait((PE.semaphore, PE.count))
    for j in range(0, KEYS, 2):
        if j == PICKS_UNTIL:
            while len(picked_ready) < TB:
                W.step_aside()
            S.wait(picked_ready)
        b, ps = banks.take(PE)
        k.feature_major(ps[:, 0:T], hT)
        done = k.feature_major(ps[:, T:2 * T], hT)
        S.wait(done)
        m = S.mark(scalar.activation(active[:, j:j + 2, :], ps.rearrange("p (j t) -> p j t", j=2), ACT.Gelu),
                   alone=True)
        banks.free(b, m)
        if j == HALF - 2:
            first_activated.append(m)
    last_activated.append(m)
    read_h = done
    W.finish_aside()

    W.asides.append(weigh(HALF, last_activated, last_weighed))
    banks.use(range(4, 8))
    PE.wait(banks.freed[0:4])
    part_ready, part_read = {}, {}

    def part(pair):
        if pair == HALF // 2:
            W.finish_aside()
        source, chunks = active[:, 2 * pair:2 * pair + 2, :], slice(2 * (pair % 3), 2 * (pair % 3) + 2)
        weighed = first_weighed if 2 * pair < HALF else last_weighed
        part_ready[pair] = k.split(hT[0][:, chunks, :], hT[1][:, chunks, :], source,
                                   [read_h] + weighed + [part_read.get(pair - 3)])

    part(0)
    for pair in range(KEYS // 2):
        if pair + 1 < KEYS // 2:
            part(pair + 1)
        PE.wait(part_ready[pair])
        for jj in range(2):
            w = W.take(PE)
            for tb in range(TB):
                still = k.at(hT, slice(None), 2 * (pair % 3) + jj, slice(tb * P, (tb + 1) * P))
                for half in range(2):
                    ins = k.products(psum[:, 2 * tb + half, :], still,
                                     k.at(w, slice(None), slice(half * BANK, (half + 1) * BANK)),
                                     pair == 0 and jj == 0, pair == KEYS // 2 - 1 and jj == 1)
            done = PE.mark(ins)
            part_read[pair] = done
            W.release(done)
    out = [[k.add_to_x(tb, half * BANK, psum[:, 2 * tb + half, :], 1.0, done) for half in range(2)][-1]
           for tb in range(TB)]
    room.close()
    return out


def by_column(v):
    return v.reshape(-1, P).T


def feature_tiles(w):
    k, n = w.shape
    return w.reshape(KC, P, n // P, P).transpose(2, 1, 0, 3).reshape(n // P, P, TILE)


def token_tiles(w, width=BANK):
    k, n = w.shape
    rows = TILE // width
    return w.reshape(k // (rows * P), rows, P, n // width, width).transpose(3, 0, 2, 1, 4).reshape(-1, P, TILE)


def constants():
    i = np.arange(P)
    row, colm = i[:, None], i[None, :]
    parts = {
        "ident": (row == colm), "iota": np.broadcast_to(colm, (P, P)),
        "strict": row < colm, "upto": row <= colm,
    }
    def level(m):
        return (row // (2 * m) == colm // (2 * m)) & (row % (2 * m) >= m) & (colm % (2 * m) < m)
    parts["pairT"] = level(1).T
    parts["level"] = np.concatenate([level(2 ** n) for n in range(LEVELS)], axis=1)
    sel = np.zeros((P, KC, HEADS))
    for c in range(KC):
        for h in range(2):
            sel[h * HD:(h + 1) * HD, c, 2 * c + h] = 1
    parts["headsel"] = sel.reshape(P, -1)
    parts["headspread"] = np.zeros((P, KC * P))
    parts["headspread"][0:HEADS] = sel.transpose(2, 1, 0).reshape(HEADS, -1)
    parts["scan_keep"] = np.broadcast_to((colm != 0), (P, P))
    q = np.concatenate([np.broadcast_to(row, (P, P)), np.broadcast_to(row + P, (P, 2 * P))], axis=1)
    k = np.broadcast_to(np.concatenate([i, i, i + P])[None, :], (P, 3 * P))
    parts["causal_dist"] = np.where(q >= k, -(q - k).astype(np.float64), NEG)
    chunk = 64
    near = (k // chunk <= q // chunk) & (k // chunk >= q // chunk - 2)
    parts["window_dist"] = np.where(near, -np.abs(q - k).astype(np.float64), NEG)
    parts["before"] = k < q
    parts["before_neg"] = np.where(k < q, 0.0, NEG)
    return np.concatenate([parts[name].astype(np.float32) for name, _ in CONSTS], axis=1)


def kernel(**inputs):
    import concourse.bacc as bacc
    from concourse.bass_utils import run_bass_kernel_spmd

    a = {k: np.asarray(v) for k, v in inputs.items()}
    arrays = {"x": a["x"].reshape(TB, P, D)}
    cat = lambda *v: np.concatenate(v, axis=1)
    arrays["cols"] = cat(
        by_column(a["ffn_norm"].reshape(-1)), by_column(a["mix_norm"].reshape(-1)), by_column(a["rwkv_mu"].reshape(-1)),
        *(by_column(a[n].reshape(-1)) for n in ("rwkv_w0", "rwkv_a0", "rwkv_k_k", "rwkv_k_a", "rwkv_r_k", "kv_norm",
                                                "mix_norm_gain_2", "ffn_norm_gain_2", "diff_subln")),
        *(np.tile(a[n].reshape(-1), 2)[:, None] for n in ("k_norm", "diff_q_norm", "swa_q_gain_2", "swa_k_gain_2")))
    arrays["consts"] = constants()
    arrays["ffn_in"] = a["ffn_w_in"].reshape(2, 2, KC, P, 2, FC, P).transpose(0, 1, 5, 4, 3, 2, 6).reshape(
        2, 2, FC, 2, P, TILE)
    arrays["ffn_out"] = a["ffn_w_out"].reshape(2, 2, FC, P, D)
    rows = lambda w: w.reshape(KC, P, -1).transpose(1, 0, 2)
    arrays["lora_in"] = np.concatenate([rows(a["rwkv_w1"][0]), rows(a["rwkv_a1"][0])], axis=2).reshape(P, KC * P)
    arrays["g1"] = rows(a["rwkv_g1"][0]).reshape(P, KC * 160)
    arrays["lora_out"] = cat(a["rwkv_w2"][0], a["rwkv_a2"][0])
    arrays["g2"] = a["rwkv_g2"][0]
    w_rkv = a["rwkv_w_rkv"][0]
    arrays["w_r"], arrays["w_k"], arrays["w_v"] = feature_tiles(w_rkv[0]), feature_tiles(w_rkv[1]), token_tiles(w_rkv[2])
    arrays["w_o"] = token_tiles(a["rwkv_w_o"][0])
    arrays["ln"] = cat(a["rwkv_ln_g"], a["rwkv_ln_b"])
    arrays["w_kv"] = token_tiles(a["w_kv"])
    arrays["diff_w_q"] = token_tiles(a["diff_w_q"][0])
    arrays["diff_w_o"] = token_tiles(a["diff_w_o"][0])
    arrays["lam"] = a["diff_lambda"].reshape(1, 4 * HD)
    w = a["w_in_2"][0]
    arrays["in_q_a"] = token_tiles(w[:, 0:512])
    arrays["in_kv_a"] = token_tiles(w[:, 512:768], 256)
    arrays["in_qk_b"] = feature_tiles(w[:, 768:1792])
    arrays["in_v_b"] = token_tiles(w[:, 1792:2304])
    arrays["in_gates"] = token_tiles(w[:, 2304:])
    arrays["gate_bias"] = a["gate_bias_2"]
    arrays["sinks"] = a["swa_sinks_2"]
    arrays["up_swa"], arrays["up_sb"] = token_tiles(a["w_up_swa_2"][0]), token_tiles(a["w_up_sb_2"][0])
    arrays["w_out"] = token_tiles(a["w_out_2"][0])
    arrays["peer_q"] = feature_tiles(a["peer_w_q_2"][0])
    arrays["sub_keys"] = a["peer_sub_keys_2"][0].reshape(16, P, P).transpose(2, 0, 1).reshape(P, 16 * P)
    u = a["peer_u_2"][0].reshape(KEYS, KEYS, KC, P)
    arrays["peer_u"] = u.transpose(1, 3, 2, 0).reshape(KEYS, P, TILE)
    arrays["peer_v"] = a["peer_v_2"][0].reshape(KEYS, KEYS, D).transpose(1, 0, 2)

    nc = bacc.Bacc("TRN2", target_bir_lowering=False, num_devices=1)
    handles, launch = {}, {}
    for name, value in arrays.items():
        launch[f"{name}_dram"] = np.ascontiguousarray(value)
        handles[name] = nc.dram_tensor(f"{name}_dram", value.shape, F32, kind="ExternalInput").ap()
    out = nc.dram_tensor("out_dram", (TB, P, D), F32, kind="ExternalOutput").ap()
    with ExitStack() as stack:
        block(nc, handles, out, stack)
    result = run_bass_kernel_spmd(nc, [launch], core_ids=[0])
    return result.results[0]["out_dram"].reshape(1, T, D)
```
